# Optimizing a Trainium2 kernel written in Bass

```python
import jax, jax.numpy as jnp
from jax import lax
import numpy as np

D_MODEL = 1024
BATCH = 1
SEQ = 512
DEPTH = 2
DEC_BATCH = 8
DEC_SEQ = 4
PAST_LEN = 256
PAGE_SIZE = 128

N_EVEN = (DEPTH + 1) // 2
N_ODD = DEPTH // 2

RET_HEADS = 4
RET_DK = 128
RET_DV = 128
RET_CHUNK = 128
RET_THETA = 10000.0
SG_GROUPS = 4
SG_CH = 128
SG_CHUNK = 128
RET_W = RET_HEADS * RET_DK
SG_W = SG_GROUPS * SG_CH
EVEN_IN = 4 * RET_W + 2 * SG_W
EVEN_OUT = RET_HEADS * RET_DV + SG_W

NSA_HEADS = 16
NSA_KV = 4
HEAD_DIM = D_MODEL // NSA_HEADS
NSA_REP = NSA_HEADS // NSA_KV
NSA_Q_W = NSA_HEADS * HEAD_DIM
NSA_KV_W = 6 * NSA_KV * HEAD_DIM
ODD_IN = NSA_Q_W + NSA_KV_W + 3 * NSA_HEADS
CMP_LEN = 32
CMP_STRIDE = 16
SEL_BLK = 64
SEL_TOPK = 16
SEL_QBLK = 64
WINDOW = 512
WIN_BLK = 128
ROPE_DIM = HEAD_DIM // 4
ROPE_THETA = 500000.0
ATTN_SCALE = HEAD_DIM ** -0.5

D_FF = ((8 * D_MODEL // 3 + 127) // 128) * 128
CONV_W = 3

EPS = 1e-6
NEG = -1e30
FORCE = 1e9

kernel_name = 'retnet_gmlp_nsa_convffn_hybrid_step'

def rms_norm(x, g):
    xf = x.astype(jnp.float32)
    y = xf * lax.rsqrt(jnp.mean(xf * xf, -1, keepdims=True) + EPS)
    return y.astype(x.dtype) * g

def rms_unit(x):
    xf = x.astype(jnp.float32)
    return (xf * lax.rsqrt(jnp.mean(xf * xf, -1, keepdims=True) + EPS)).astype(x.dtype)

def layer_norm(x, g, b):
    xf = x.astype(jnp.float32)
    xc = xf - jnp.mean(xf, -1, keepdims=True)
    y = xc * lax.rsqrt(jnp.mean(xc * xc, -1, keepdims=True) + EPS)
    return y.astype(x.dtype) * g + b

def rope(x, pos, n_rot, inv_freq):
    ang = pos.astype(jnp.float32)[:, None] * inv_freq[None, :]
    cos = jnp.cos(ang)[:, None, :].astype(x.dtype)
    sin = jnp.sin(ang)[:, None, :].astype(x.dtype)
    h = n_rot // 2
    x1, x2, rest = x[..., :h], x[..., h:n_rot], x[..., n_rot:]
    return jnp.concatenate([x1 * cos - x2 * sin, x2 * cos + x1 * sin, rest], axis=-1)

def ret_freq():
    return 1.0 / (RET_THETA ** jnp.linspace(0.0, 1.0, RET_DK // 2))

def nsa_freq():
    return 1.0 / (ROPE_THETA ** (jnp.arange(0, ROPE_DIM, 2, dtype=jnp.float32) / ROPE_DIM))

def ret_log_decay():
    return jnp.log(1.0 - 2.0 ** (-5.0 - jnp.arange(RET_HEADS, dtype=jnp.float32)))

def retention(q, k, v, s0):
    B, n, H, _ = q.shape
    C = min(n, RET_CHUNK)
    nc = n // C
    log_g = ret_log_decay()
    idx = jnp.arange(C, dtype=jnp.float32)
    diff = idx[:, None] - idx[None, :]
    dmask = jnp.where(diff >= 0, jnp.exp(log_g[:, None, None] * jnp.maximum(diff, 0.0)), 0.0).astype(q.dtype)
    qdec = jnp.exp(log_g[:, None] * (idx + 1.0))[..., None].astype(q.dtype)
    kdec = jnp.exp(log_g[:, None] * (C - 1.0 - idx))[..., None]
    cdec = jnp.exp(log_g * C)[:, None, None]

    def chunks(t):
        return t.reshape(B, nc, C, H, t.shape[-1]).transpose(1, 0, 3, 2, 4)

    def step(s, qkv):
        qc, kc, vc = qkv
        inner = jnp.einsum('bhid,bhjd->bhij', qc, kc) * dmask
        o = (jnp.einsum('bhij,bhjv->bhiv', inner, vc)
             + jnp.einsum('bhid,bhdv->bhiv', qc * qdec, s.astype(qc.dtype)))
        s = s * cdec + jnp.einsum('bhjd,bhjv->bhdv', kc.astype(jnp.float32) * kdec, vc.astype(jnp.float32))
        return s, o

    s, o = lax.scan(step, s0, (chunks(q), chunks(k), chunks(v)))
    return o.transpose(1, 0, 3, 2, 4).reshape(B, n, H, RET_DV), s

def even_mixer(h, pos, s0, w_in, w_out, ln_g, ln_b, sg_w, sg_b):
    B, n, _ = h.shape
    p = h @ w_in
    q, k, v, g, u, sv = jnp.split(p, 6, axis=-1)
    q = rope(q.reshape(B, n, RET_HEADS, RET_DK), pos, RET_DK, ret_freq())
    k = rope(k.reshape(B, n, RET_HEADS, RET_DK), pos, RET_DK, ret_freq()) * (RET_DK ** -0.5)
    o, s1 = retention(q, k, v.reshape(B, n, RET_HEADS, RET_DV), s0)
    ret_out = jax.nn.silu(g) * rms_unit(o).reshape(B, n, RET_HEADS * RET_DV)
    svn = layer_norm(sv.reshape(B, n, SG_GROUPS, SG_CH), ln_g.reshape(SG_GROUPS, SG_CH), ln_b.reshape(SG_GROUPS, SG_CH))
    c = min(n, SG_CHUNK)
    wm = jnp.tril(sg_w[:, :c, :c])
    mixed = (jnp.einsum('gij,bnjgc->bnigc', wm, svn.reshape(B, n // c, c, SG_GROUPS, SG_CH))
             + sg_b[:, :c].T[None, None, :, :, None])
    sg_out = u * mixed.reshape(B, n, SG_W)
    y = jnp.concatenate([ret_out, sg_out], axis=-1) @ w_out
    return y, s1, svn.reshape(B, n, SG_W)

def nsa_project(h, pos, w_in):
    B, n, _ = h.shape
    p = h @ w_in
    q = rope(p[..., :NSA_Q_W].reshape(B, n, NSA_HEADS, HEAD_DIM), pos, ROPE_DIM, nsa_freq())
    q = q.reshape(B, n, NSA_KV, NSA_REP, HEAD_DIM)
    kv = p[..., NSA_Q_W:NSA_Q_W + NSA_KV_W].reshape(B, n, 3, 2, NSA_KV, HEAD_DIM)
    k = rope(kv[:, :, :, 0].reshape(B, n, 3 * NSA_KV, HEAD_DIM), pos, ROPE_DIM, nsa_freq())
    kv = jnp.stack([k.reshape(B, n, 3, NSA_KV, HEAD_DIM), kv[:, :, :, 1]], axis=3)
    gates = jax.nn.sigmoid(p[..., NSA_Q_W + NSA_KV_W:]).reshape(B, n, 3, NSA_KV, NSA_REP)
    return q, kv[:, :, 0], kv[:, :, 1], kv[:, :, 2], gates

def compress(rows, pe_k, pe_v, phi_k, phi_v):
    B, L = rows.shape[:2]
    nc = (L - CMP_LEN) // CMP_STRIDE + 1
    nper = CMP_LEN // CMP_STRIDE
    nsub = nc + nper - 1
    sub = rows[:, :nsub * CMP_STRIDE].reshape((B, nsub, CMP_STRIDE) + rows.shape[2:])
    blocks = jnp.concatenate([sub[:, j:j + nc] for j in range(nper)], axis=2)
    kb = blocks[:, :, :, 0] + pe_k[:, None, :]
    vb = blocks[:, :, :, 1] + pe_v[:, None, :]
    kc = jnp.einsum('bnlgd,lde->bnge', kb, phi_k)
    vc = jnp.einsum('bnlgd,lde->bnge', vb, phi_v)
    return kc, vc

def cmp_attend(q, qpos, kc, vc):
    nc = kc.shape[1]
    blk_end = jnp.arange(nc) * CMP_STRIDE + CMP_LEN - 1
    valid = (blk_end[None, :] <= qpos[:, None])[None, :, None, None, :]
    s = jnp.einsum('bngrd,bmgd->bngrm', q, kc).astype(jnp.float32) * ATTN_SCALE
    p = jax.nn.softmax(jnp.where(valid, s, NEG), axis=-1) * valid
    o = jnp.einsum('bngrm,bmgd->bngrd', p.astype(q.dtype), vc)
    return o, p

def select_blocks(p_cmp, qpos, n_sel):
    nc = p_cmp.shape[-1]
    c_start = jnp.arange(nc) * CMP_STRIDE
    s_start = jnp.arange(n_sel) * SEL_BLK
    cover = ((c_start[:, None] < s_start[None, :] + SEL_BLK)
             & (c_start[:, None] + CMP_LEN > s_start[None, :])).astype(jnp.float32)
    imp = jnp.einsum('bngrm,mj->bngj', p_cmp, cover)
    cur = qpos // SEL_BLK
    j = jnp.arange(n_sel)
    forced = (j[None, :] == 0) | (j[None, :] == cur[:, None]) | (j[None, :] == cur[:, None] - 1)
    causal = s_start[None, :] <= qpos[:, None]
    imp = jnp.where(forced[None, :, None, :], FORCE, jnp.where(causal[None, :, None, :], imp, -1.0))
    _, idx = lax.top_k(imp, min(SEL_TOPK, n_sel))
    return idx

def sel_attend(q, qpos, idx, kblk, vblk):
    idx_t = idx.transpose(0, 2, 1, 3)
    take = jax.vmap(jax.vmap(lambda blk, ii: blk[ii]))
    kg = take(kblk, idx_t)
    vg = take(vblk, idx_t)
    kpos = idx_t[..., None] * SEL_BLK + jnp.arange(SEL_BLK)
    mask = (kpos <= qpos[None, None, :, None, None])[:, :, :, None]
    qg = q.transpose(0, 2, 1, 3, 4)
    s = jnp.einsum('bgqrd,bgqkld->bgqrkl', qg, kg).astype(jnp.float32) * ATTN_SCALE
    s = jnp.where(mask, s, NEG)
    shp = s.shape
    p = jax.nn.softmax(s.reshape(shp[:4] + (-1,)), axis=-1).reshape(shp).astype(q.dtype)
    o = jnp.einsum('bgqrkl,bgqkld->bgqrd', p, vg)
    return o.transpose(0, 2, 1, 3, 4)

def sel_attend_blocked(q, qpos, idx, rows, qblk):
    B, n = q.shape[:2]
    nsel = rows.shape[1] // SEL_BLK
    kblk = rows[:, :, 0].reshape(B, nsel, SEL_BLK, NSA_KV, HEAD_DIM).transpose(0, 3, 1, 2, 4)
    vblk = rows[:, :, 1].reshape(B, nsel, SEL_BLK, NSA_KV, HEAD_DIM).transpose(0, 3, 1, 2, 4)
    nb = n // qblk

    def split(t):
        return t.reshape((B, nb, qblk) + t.shape[2:]).swapaxes(0, 1)

    o = lax.map(lambda a: sel_attend(a[0], a[1], a[2], kblk, vblk), (split(q), qpos.reshape(nb, qblk), split(idx)))
    return o.swapaxes(0, 1).reshape(q.shape)

def window_attend(q, qpos, kv, kpos):
    mask = (kpos[None, :] <= qpos[:, None]) & (kpos[None, :] > qpos[:, None] - WINDOW) & (kpos[None, :] >= 0)
    s = jnp.einsum('bqgrd,bkgd->bqgrk', q, kv[:, :, 0]).astype(jnp.float32) * ATTN_SCALE
    s = jnp.where(mask[None, :, None, None, :], s, NEG)
    p = jax.nn.softmax(s, axis=-1).astype(q.dtype)
    return jnp.einsum('bqgrk,bkgd->bqgrd', p, kv[:, :, 1])

def window_attend_prompt(q, rows):
    B, S = q.shape[:2]
    nb = S // WIN_BLK
    lk = WIN_BLK + WINDOW
    rp = jnp.pad(rows, ((0, 0), (WINDOW, 0), (0, 0), (0, 0), (0, 0)))
    qb = q.reshape((B, nb, WIN_BLK) + q.shape[2:]).swapaxes(0, 1)

    def blk(a):
        b, qq = a
        kv = lax.dynamic_slice_in_dim(rp, b * WIN_BLK, lk, axis=1)
        qpos = b * WIN_BLK + jnp.arange(WIN_BLK)
        kpos = b * WIN_BLK - WINDOW + jnp.arange(lk)
        return window_attend(qq, qpos, kv, kpos)

    o = lax.map(blk, (jnp.arange(nb), qb))
    return o.swapaxes(0, 1).reshape(q.shape)

def nsa_combine(gates, o_c, o_s, o_w, w_out):
    o = gates[:, :, 0, ..., None] * o_c + gates[:, :, 1, ..., None] * o_s + gates[:, :, 2, ..., None] * o_w
    B, n = o.shape[:2]
    return o.reshape(B, n, NSA_Q_W) @ w_out

def nsa_prompt(h, w_in, w_out, pe_k, pe_v, phi_k, phi_v):
    B, S, _ = h.shape
    pos = jnp.arange(S, dtype=jnp.int32)
    q, rows_c, rows_s, rows_w, gates = nsa_project(h, pos, w_in)
    kc, vc = compress(rows_c, pe_k, pe_v, phi_k, phi_v)
    o_c, p_c = cmp_attend(q, pos, kc, vc)
    idx = select_blocks(p_c, pos, S // SEL_BLK)
    o_s = sel_attend_blocked(q, pos, idx, rows_s, SEL_QBLK)
    o_w = window_attend_prompt(q, rows_w)
    y = nsa_combine(gates, o_c, o_s, o_w, w_out)
    return y, rows_c, rows_s, rows_w[:, -min(WINDOW, S):]

def gather_pages(pool, page_table):
    g = pool[page_table]
    return g.reshape((g.shape[0], g.shape[1] * g.shape[2]) + g.shape[3:])

def nsa_sample(h, pos, pool_c, pool_s, buf_w, page_table, w_in, w_out, pe_k, pe_v, phi_k, phi_v):
    B, n, _ = h.shape
    past_len = page_table.shape[1] * PAGE_SIZE
    q, rows_c, rows_s, rows_w, gates = nsa_project(h, pos, w_in)
    full_c = jnp.concatenate([gather_pages(pool_c, page_table).astype(rows_c.dtype), rows_c], axis=1)
    kc, vc = compress(full_c, pe_k, pe_v, phi_k, phi_v)
    o_c, p_c = cmp_attend(q, pos, kc, vc)
    L = past_len + n
    Lp = -(-L // SEL_BLK) * SEL_BLK
    full_s = jnp.concatenate([gather_pages(pool_s, page_table).astype(rows_s.dtype), rows_s,
                              jnp.zeros((B, Lp - L) + rows_s.shape[2:], rows_s.dtype)], axis=1)
    idx = select_blocks(p_c, pos, Lp // SEL_BLK)
    o_s = sel_attend_blocked(q, pos, idx, full_s, 1)
    w_buf = buf_w.shape[1]
    kv_w = jnp.concatenate([buf_w.astype(rows_w.dtype), rows_w], axis=1)
    kpos = jnp.concatenate([past_len - w_buf + jnp.arange(w_buf, dtype=jnp.int32), pos])
    o_w = window_attend(q, pos, kv_w, kpos)
    y = nsa_combine(gates, o_c, o_s, o_w, w_out)
    keep = min(WINDOW, w_buf + n)
    return y, rows_c, rows_s, kv_w[:, -keep:]

def conv_ffn(h, prev, w_in, conv_w, conv_b, w_out):
    n = h.shape[1]
    up = h @ w_in
    full = jnp.concatenate([prev.astype(up.dtype), up], axis=1)
    c = conv_b + full[:, 0:n] * conv_w[0]
    for j in range(1, CONV_W):
        c = c + full[:, j:j + n] * conv_w[j]
    a, b = jnp.split(c, 2, axis=-1)
    y = (jax.nn.gelu(a) * b) @ w_out
    return y, full[:, n:]

def setup_inputs(seed: int = 0) -> dict:
    key = jax.random.key(seed)
    keys = iter(jax.random.split(key, 32))

    def nrm(shape, scale):
        return jax.random.normal(next(keys), shape, jnp.float32) * scale

    n_pages = PAST_LEN // PAGE_SIZE
    n_pool = (DEC_BATCH * n_pages * 5 + 3) // 4
    w_buf = min(WINDOW, PAST_LEN)
    kv_row = (2, NSA_KV, HEAD_DIM)
    x_prompt = nrm((BATCH, SEQ, D_MODEL), 1.0)
    x_sample = nrm((DEC_BATCH, DEC_SEQ, D_MODEL), 1.0)
    state_ret = nrm((N_EVEN, DEC_BATCH, RET_HEADS, RET_DK, RET_DV), 0.3)
    cache_cmp = nrm((N_ODD, n_pool, PAGE_SIZE) + kv_row, 1.0)
    cache_sel = nrm((N_ODD, n_pool, PAGE_SIZE) + kv_row, 1.0)
    state_win = nrm((N_ODD, DEC_BATCH, w_buf) + kv_row, 1.0)
    state_ffn = nrm((DEPTH, DEC_BATCH, CONV_W - 1, 2 * D_FF), 1.0)
    page_table = jax.random.permutation(next(keys), n_pool)[:DEC_BATCH * n_pages].reshape(DEC_BATCH, n_pages).astype(jnp.int32)
    return {
        'x_prompt': x_prompt,
        'x_sample': x_sample,
        'state_ret': state_ret,
        'cache_cmp': cache_cmp,
        'cache_sel': cache_sel,
        'state_win': state_win,
        'state_ffn': state_ffn,
        'page_table': page_table,
        'norm_mix_pre': 1.0 + nrm((DEPTH, D_MODEL), 0.1),
        'norm_mix_post': 1.0 + nrm((DEPTH, D_MODEL), 0.1),
        'norm_ffn_pre': 1.0 + nrm((DEPTH, D_MODEL), 0.1),
        'norm_ffn_post': 1.0 + nrm((DEPTH, D_MODEL), 0.1),
        'e_w_in': nrm((N_EVEN, D_MODEL, EVEN_IN), D_MODEL ** -0.5),
        'e_w_out': nrm((N_EVEN, EVEN_OUT, D_MODEL), EVEN_OUT ** -0.5),
        'e_sg_ln_g': 1.0 + nrm((N_EVEN, SG_W), 0.1),
        'e_sg_ln_b': nrm((N_EVEN, SG_W), 0.1),
        'e_sg_w': nrm((N_EVEN, SG_GROUPS, SG_CHUNK, SG_CHUNK), SG_CHUNK ** -0.5),
        'e_sg_b': 1.0 + nrm((N_EVEN, SG_GROUPS, SG_CHUNK), 0.1),
        'o_w_in': nrm((N_ODD, D_MODEL, ODD_IN), D_MODEL ** -0.5),
        'o_w_out': nrm((N_ODD, NSA_Q_W, D_MODEL), NSA_Q_W ** -0.5),
        'o_pe_k': nrm((N_ODD, CMP_LEN, HEAD_DIM), 0.5),
        'o_pe_v': nrm((N_ODD, CMP_LEN, HEAD_DIM), 0.5),
        'o_phi_k': nrm((N_ODD, CMP_LEN, HEAD_DIM, HEAD_DIM), (CMP_LEN * HEAD_DIM) ** -0.5),
        'o_phi_v': nrm((N_ODD, CMP_LEN, HEAD_DIM, HEAD_DIM), (CMP_LEN * HEAD_DIM) ** -0.5),
        'f_w_in': nrm((DEPTH, D_MODEL, 2 * D_FF), D_MODEL ** -0.5),
        'f_conv_w': nrm((DEPTH, CONV_W, 2 * D_FF), CONV_W ** -0.5),
        'f_conv_b': nrm((DEPTH, 2 * D_FF), 0.1),
        'f_w_out': nrm((DEPTH, D_FF, D_MODEL), D_FF ** -0.5),
    }

def reference(x_prompt, x_sample, state_ret, cache_cmp, cache_sel, state_win, state_ffn, page_table,
              norm_mix_pre, norm_mix_post, norm_ffn_pre, norm_ffn_post,
              e_w_in, e_w_out, e_sg_ln_g, e_sg_ln_b, e_sg_w, e_sg_b,
              o_w_in, o_w_out, o_pe_k, o_pe_v, o_phi_k, o_phi_v,
              f_w_in, f_conv_w, f_conv_b, f_w_out):
    xp, xs = x_prompt, x_sample
    B, S = xp.shape[:2]
    DB, n = xs.shape[:2]
    past_len = page_table.shape[1] * PAGE_SIZE
    pos_p = jnp.arange(S, dtype=jnp.int32)
    pos_s = past_len + jnp.arange(n, dtype=jnp.int32)
    ret_p, ret_s, sgv_s = [], [], []
    cmp_p, cmp_s, sel_p, sel_s, win_p, win_s = [], [], [], [], [], []
    ffn_p, ffn_s = [], []
    for l in range(DEPTH):
        i = l // 2
        hp = rms_norm(xp, norm_mix_pre[l])
        hs = rms_norm(xs, norm_mix_pre[l])
        if l % 2 == 0:
            mp, sp, _ = even_mixer(hp, pos_p, jnp.zeros((B, RET_HEADS, RET_DK, RET_DV), jnp.float32),
                                   e_w_in[i], e_w_out[i], e_sg_ln_g[i], e_sg_ln_b[i], e_sg_w[i], e_sg_b[i])
            ms, ss, vs = even_mixer(hs, pos_s, state_ret[i].astype(jnp.float32),
                                    e_w_in[i], e_w_out[i], e_sg_ln_g[i], e_sg_ln_b[i], e_sg_w[i], e_sg_b[i])
            ret_p.append(sp.astype(xp.dtype))
            ret_s.append(ss.astype(xs.dtype))
            sgv_s.append(vs)
        else:
            mp, rcp, rsp, bwp = nsa_prompt(hp, o_w_in[i], o_w_out[i], o_pe_k[i], o_pe_v[i], o_phi_k[i], o_phi_v[i])
            ms, rcs, rss, bws = nsa_sample(hs, pos_s, cache_cmp[i], cache_sel[i], state_win[i], page_table,
                                           o_w_in[i], o_w_out[i], o_pe_k[i], o_pe_v[i], o_phi_k[i], o_phi_v[i])
            cmp_p.append(rcp)
            cmp_s.append(rcs)
            sel_p.append(rsp)
            sel_s.append(rss)
            win_p.append(bwp)
            win_s.append(bws)
        xp = xp + rms_norm(mp, norm_mix_post[l])
        xs = xs + rms_norm(ms, norm_mix_post[l])
        fp, cp = conv_ffn(rms_norm(xp, norm_ffn_pre[l]), jnp.zeros((B, CONV_W - 1, 2 * D_FF), xp.dtype),
                          f_w_in[l], f_conv_w[l], f_conv_b[l], f_w_out[l])
        fs, cs = conv_ffn(rms_norm(xs, norm_ffn_pre[l]), state_ffn[l],
                          f_w_in[l], f_conv_w[l], f_conv_b[l], f_w_out[l])
        ffn_p.append(cp)
        ffn_s.append(cs)
        xp = xp + rms_norm(fp, norm_ffn_post[l])
        xs = xs + rms_norm(fs, norm_ffn_post[l])
    return (xp, xs, jnp.stack(ret_p), jnp.stack(ret_s), jnp.stack(sgv_s),
            jnp.stack(cmp_p), jnp.stack(cmp_s), jnp.stack(sel_p), jnp.stack(sel_s),
            jnp.stack(win_p), jnp.stack(win_s), jnp.stack(ffn_p), jnp.stack(ffn_s))


_drawn_inputs = setup_inputs


def setup_inputs(seed=0):
    import zlib

    import numpy as np

    out = dict(_drawn_inputs(seed))
    spreads = {}
    factors = {}
    for name, (base, spread) in spreads.items():
        noise = np.random.default_rng([zlib.crc32(name.encode()), seed]).standard_normal(out[name].shape)
        drawn = base * np.exp(spread * noise) if base else spread * noise
        out[name] = __import__('jax').numpy.asarray(drawn.astype(out[name].dtype))
    for name, factor in factors.items():
        out[name] = (out[name] * factor).astype(out[name].dtype)
    return out
```

```python
from contextlib import ExitStack

import numpy as np

import concourse.bass as bass
from concourse import mybir

F32 = mybir.dt.float32
F32R = mybir.dt.float32r
ALU = mybir.AluOpType
ACT = mybir.ActivationFunctionType
AX_X = mybir.AxisListType.X

P = 128
D = 1024
DC = D // P
SEQ, DB, DS = 512, 8, 4
NS = DB * DS
T = NS + SEQ
TH = T // 2
TQ = T // 4
NT = 1 + SEQ // P
RH, DK = 4, 128
FF = 2816
FH = FF // P // 2
G, R, HD = 4, 4, 64
PAST, PAGE = 256, 128
NPG = PAST // PAGE
KS = PAST + DS
KW = PAST + NS
NCP = (SEQ - 32) // 16 + 1
NCS = (PAST + DS - 32) // 16 + 1
CL = 32
NBLK = (2 * DB + 1) * NCS
EPS = 1e-6
SCALE = HD ** -0.5
NEG = -1e30
BIG = 3e38
UNIT = 2048
THETA_E = 1.0 / (10000.0 ** np.linspace(0.0, 1.0, DK // 2))
THETA_O = 1.0 / (500000.0 ** (np.arange(0, 16, 2) / 16.0))
GAMMA = 1.0 - 2.0 ** (-5.0 - np.arange(RH))


def tile_start(t):
    return 0 if t == 0 else NS + P * (t - 1)


def shape_constants():
    pos = np.concatenate([np.tile(PAST + np.arange(DS), DB), np.arange(SEQ)]).astype(np.float64)
    ang = THETA_E[:, None] * pos[None, :]
    c = {}
    c["cos_even"] = np.concatenate([np.cos(ang), np.cos(ang)], 0)
    c["sin_even"] = np.concatenate([-np.sin(ang), np.sin(ang)], 0)
    co, so = np.zeros((P, NT, 8)), np.zeros((P, NT, 8))
    for t in range(NT):
        a = pos[tile_start(t):tile_start(t) + P, None] * THETA_O[None, :]
        co[:, t], so[:, t] = np.cos(a), np.sin(a)
    c["cos_odd"], c["sin_odd"] = co.reshape(P, -1), so.reshape(P, -1)
    i = np.arange(P)
    diff = i[None, :] - i[:, None]
    dm = np.zeros((P, RH, P))
    for h in range(RH):
        dm[:, h] = np.where(diff >= 0, GAMMA[h] ** np.maximum(diff, 0), 0)
    c["decay"] = dm.reshape(P, -1)
    s = np.arange(NS)
    ds = np.zeros((NS, RH, NS))
    same = (s[:, None] // DS) == (s[None, :] // DS)
    for h in range(RH):
        d = (s % DS)[None, :] - (s % DS)[:, None]
        ds[:, h] = np.where(same & (d >= 0), GAMMA[h] ** np.maximum(d, 0), 0)
    c["decay_s"] = ds.reshape(NS, -1)
    c["qdecay"] = np.stack([GAMMA[h] ** (i + 1.0) for h in range(RH)]).reshape(1, -1)
    c["qdecay_s"] = np.stack([GAMMA[h] ** (s % DS + 1.0) for h in range(RH)]).reshape(1, -1)
    c["kdecay"] = np.concatenate([np.stack([GAMMA[h] ** (P - 1.0 - i) for h in range(RH)], 1),
                                  np.stack([GAMMA[h] ** (DS - 1.0 - i % DS) for h in range(RH)], 1)], 1)
    c["tril_t"] = (diff >= 0).astype(np.float64)
    c["same_s"] = same.astype(np.float64)
    c["row_of_s"] = (np.arange(DS)[:, None] == (s % DS)[None, :]).astype(np.float64)
    c["batch_of"] = (s[:, None] // DS == np.arange(DB)[None, :]).astype(np.float64)
    c["ident"] = np.eye(P)
    sel = np.zeros((P, 4, P))
    for q in range(4):
        sel[32 * q, q] = 1
    c["spread"] = sel.reshape(P, -1)
    x = np.arange(SEQ)
    c["causal"] = np.where(x[None, :] - (SEQ - P) <= i[:, None], 0, NEG)
    cm, cv = np.zeros((P, 4, NCP)), np.zeros((P, 4, NCP))
    for t in range(4):
        ok = (np.arange(NCP) * 16 + 31)[None, :] <= (P * t + i)[:, None]
        cm[:, t], cv[:, t] = np.where(ok, 0, NEG), ok
    c["cmp_mask"], c["cmp_valid"] = cm.reshape(P, -1), cv.reshape(P, -1)
    n = i % 4
    new = np.full((P, DB, DB, DS), NEG)
    for b in range(DB):
        new[:, b, b, :] = np.where(np.arange(DS)[None, :] <= n[:, None], 0, NEG)
    c["mask_new"] = new.reshape(P, -1)
    pj = np.zeros((P, 2, NCS))
    for j in range(2):
        pj[:, j] = ((i // 64) == j)[:, None]
    c["pair_of"] = pj.reshape(P, -1)
    return {k: np.ascontiguousarray(v, dtype=np.float32) for k, v in c.items()}


CONSTANTS = shape_constants()


def unit_plan():
    units = []
    for n in (10, 11, 4, 5, 0, 1, 2, 3, 8, 9, 6, 7):
        units.append(("even_in", 0, n, 5 if n in (4, 5, 10, 11) else 2))
    units += [("even_out", 0, n, 2) for n in range(4)]

    def ffn(layer):
        for half in range(2):
            for i in range(FH):
                units.append(("ffn_in", layer, (half, i), 2))
            for m in range(DC):
                units.append(("ffn_out", layer, (half, m), 1))

    ffn(0)
    units.extend(("odd_in", 0, n, 5) for n in (4, 5, 6, 7, 8, 9, 0, 1, 2, 3, 10))
    units.extend(("odd_out", 0, n, 2) for n in range(4))
    ffn(1)
    return units


UNITS = unit_plan()
FIRST_CHUNK = [sum(u[3] for u in UNITS[:n]) for n in range(len(UNITS) + 1)]
E_IN, E_OUT, F0 = 0, 12, 16
FFN_UNITS = 2 * (FH + DC)
O_IN = F0 + FFN_UNITS
O_OUT = O_IN + 11
F1 = O_OUT + 4


class Order:

    def __init__(self, eng, chain):
        self.eng, self.chain, self.count, self.last = eng, chain, {}, None

    def __call__(self, ins, sem=None):
        sem = self.chain if sem is None else sem
        self.count[id(sem)] = self.count.get(id(sem), 0) + 1
        ins.then_inc(sem, 1)
        self.last = (sem, self.count[id(sem)])

    def wait(self):
        self.eng.wait_ge(*self.last)


def build_program(nc, a, o):
    with ExitStack() as ctx:
        sems = {}

        def sem(name):
            if name not in sems:
                sems[name] = ctx.enter_context(nc.semaphore(name))
            return sems[name]

        place = {"at": 16512}

        def sb(name, shape, dt=F32, at=None):
            size = int(np.prod(shape[1:])) * 4
            size = (size + 31) // 32 * 32
            off = place["at"] if at is None else at
            assert off + size <= nc.sbuf_usable_end, (name, off, size)
            t = nc.alloc_sbuf_tensor_at(name, shape, dt, offset=off)
            if at is None:
                place["at"] = off + size
            return t

        xT = sb("xT", [P, DC, T])
        hH, hL = sb("hH", [P, DC, T], F32R), sb("hL", [P, DC, T], F32R)
        raw = sb("raw", [P, 2, UNIT])
        wH, wL = sb("wH", [P, 2, UNIT], F32R), sb("wL", [P, 2, UNIT], F32R)
        ident = sb("ident_sb", [P, P])
        spread = sb("spread_sb", [P, 4, P])
        mean_d, mean_k = sb("mean_d", [P, 32]), sb("mean_k", [P, 32])
        eps, pool_mark = sb("eps", [P, 1]), sb("pool_mark", [1, 1])
        gains = sb("gains", [P, DC, 8])
        kcs = sb("kcs", [P, DB, 2, NCS])
        vcs = sb("vcs", [2 * NCS, DB, P])
        pe_bias = sb("pe_bias", [P, 2])
        rq, rr = sb("rq", [P, TQ]), sb("rr", [P, TQ])
        R0 = place["at"]

        y = sb("y", [P, DC, T])
        aH, aL = sb("aH", [P, FH, T], F32R), sb("aL", [P, FH, T], F32R)
        UW = DB * 6 + 2 + SEQ
        CW = UW - 2
        up = [sb("up0", [P, 2, UW]), sb("up1", [P, 2, UW])]
        conv = sb("conv", [P, 2, CW])
        gated = sb("gated", [P, T])
        top = nc.sbuf_usable_end // 32 * 32
        rows_in = sb("rows_in", [P, FH * P], at=top - FH * P * 4)
        rows_t = sb("rows_t", [P, FH, P], at=top - 2 * FH * P * 4)
        vct = sb("vct", [P, DB, 2, NCS], at=top - 2 * FH * P * 4 - DB * 2 * NCS * 4)
        rows_out = sb("rows_out", [64, FH * P])
        tail = sb("tail", [P, 2, 64])
        sqf = [conv[:, 0, 0:T], conv[:, 1, 0:T]]
        sqm_t = sb("sqm", [P, 2, T], at=R0 + DC * T * 4)
        sqm = [sqm_t[:, 0, :], sqm_t[:, 1, :]]
        end_ffn = place["at"]

        place["at"] = R0
        qT, kT = sb("qT", [P, RH, T]), sb("kT", [P, RH, T])
        vN, svn = sb("vN", [P, NT, 512]), sb("svn", [P, NT, 512])
        silu_g, uT = sb("silu_g", [P, RH, T]), sb("uT", [P, RH, T])
        kN, qd, st = sb("kN", [P, RH, P]), sb("qd", [P, RH, P]), sb("st", [P, RH, P])
        decay, inner = sb("decay_sb", [P, RH, P]), sb("inner", [P, RH, P])
        sgb, wmT, sgw = sb("sgb", [P, 4, P]), sb("wmT", [P, 4, P]), sb("sgw", [P, 4, P])
        wmS = sb("wmS", [NS, 4, NS])
        cosE = sb("cosE", [P, T])
        sin_at = place["at"]
        sinE, swp = sb("sinE", [P, T]), sb("swp", [P, T])
        qdec, qdecs = sb("qdec", [P, RH, P]), sb("qdecs", [P, RH, NS])
        kdec, batch_of = sb("kdec", [P, 8]), sb("batch_of_sb", [NS, DB])
        decs, same_s, row_of_s = sb("decs", [NS, RH, NS]), sb("same_sb", [NS, NS]), sb("row_sb", [4, NS])
        lnt_at = place["at"]
        lnt, lng, lnb = sb("lnt", [P, 512]), sb("lng", [P, 512]), sb("lnb", [P, 512])
        tril = sb("tril", [P, P])
        lns = sb("lns", [P, 4, NT * 4])
        vB = sb("vB", [NS, DB, P])
        s0 = sb("s0", [P, DB, 2, P])
        end_even = place["at"]
        place["at"] = lnt_at
        kNs = sb("kNs", [NS, RH, P])
        place["at"] = sin_at
        qds, inner_s = sb("qds", [P, RH, NS]), sb("inner_s", [NS, RH, NS])
        hsqs = [swp, cosE]

        place["at"] = R0
        xin = sb("xin", [P, NT, D])
        gin = sb("gin", [8, D])
        place["at"] = R0 + (DC + 2) * T * 4
        phiK, phiV = sb("phiK", [P, CL, P]), sb("phiV", [P, CL, P])
        cT = sb("cT", [P, 2, 2 * DB + 1, PAST])
        pages = sb("pages", [P, 4, 512], at=top - 2 * FH * P * 4)
        pe_in = sb("pe_in", [CL, 2, P], at=top - 2 * FH * P * 4 + 8192)
        assert place["at"] <= top - 2 * FH * P * 4 - DB * 2 * NCS * 4

        place["at"] = R0
        qN, kvN, gN = sb("qN", [P, NT, D]), sb("kvN", [P, NT, 3 * 512]), sb("gN", [P, NT, 48])
        cosO, sinO, rt = sb("cosO", [P, NT, 8]), sb("sinO", [P, NT, 8]), sb("rt", [P, 4, NT * 32])
        kcP, vcP, vcPt = sb("kcP", [P, 2, NCP]), sb("vcP", [NCP, 2, P]), sb("vcPt", [P, 2, NCP])
        O1 = place["at"]
        phiK2, phiV2 = sb("phiK2", [P, CL, P]), sb("phiV2", [P, CL, P])
        cPT = sb("cPT", [P, 4, SEQ])
        place["at"] = O1
        qTj, ksT, kwT = sb("qTj", [P, R, SEQ]), sb("ksT", [P, 2, SEQ]), sb("kwT", [P, 2, SEQ])
        sm, pr, pT = sb("sm", [P, 2, SEQ]), sb("pr", [P, 2, SEQ]), sb("pT", [P, 2, SEQ])
        causal = sb("causal_sb", [P, SEQ])
        cmask, cvalid = sb("cmask", [P, 4, NCP]), sb("cvalid", [P, 4, NCP])
        cs, cmx, cpT = sb("cs", [P, R, NCP]), sb("cmx", [P, R]), sb("cpT", [NCP, R, P])
        negmax, rsum, rscale = sb("negmax", [P, 2]), sb("rsum", [P, 2]), sb("rscale", [P, 2])
        crs = sb("crs", [P, 2, R])
        
        qS = sb("qS", [P, DB, 2, 2, 32])
        gS, mask_new, pair_of = sb("gS", [P, DB, 3]), sb("mask_new_sb", [P, DB, NS]), sb("pair_of_sb", [P, 2, NCS])
        mask_s = sb("mask_s", [P, 2, KW])
        rows0 = sb("rows0", [P, 2, 2, NPG, 512], at=R0)
        rows1 = sb("rows1", [P, 2, 2, NPG, 512], at=R0 + (NT * D + 1536) * 4)
        row_slot = [rows0[:, 0], rows0[:, 1], rows1[:, 0], rows1[:, 1]]
        place["at"] = O1
        kTs = sb("kTs", [P, 2, 2, 2, KW])
        sms, prs, pTs = sb("sms", [P, 2, 2, KW]), sb("prs", [P, 2, 2, KW]), sb("pTs", [P, 2, 3, P])
        css, csm, cpb = sb("css", [P, DB, NCS]), sb("csm", [P, DB]), sb("cpb", [P, DB, 2, NCS])
        cpTs = sb("cpTs", [2 * NCS, DB, P])
        nms, rss, rsc = sb("nms", [P, DB, 2]), sb("rss", [P, DB, 3]), sb("rsc", [P, DB, 3])
        yout = sb("yout", [P, NT, D], at=R0 + DC * T * 4 + 64)

        gemm = [ctx.enter_context(nc.psum_tensor(f"gemm{n}", [P, 2, 512], F32)) for n in range(2)]
        misc = ctx.enter_context(nc.psum_tensor("misc", [P, 4, 512], F32))
        b4, b5, b6, b7 = (misc[:, n, :] for n in range(4))
        scratch = nc.dram_tensor("gate_scratch", (NS, 16, 3), F32).ap()

        def halves(ap):
            return ap.rearrange("p (a b) -> p a b", a=2)

        def by4(ap):
            return ap.rearrange("p (a b) -> p a b", a=4)


        raw_ready = [sem("raw_ready0"), sem("raw_ready1")]
        hi_ready, lo_ready = sem("hi_ready"), sem("lo_ready")
        gemm_done = sem("gemm_done")
        evacuated = [sem("evacuated0"), sem("evacuated1")]
        phase = sem("phase")
        h_hi, h_ready, ht_ready = sem("h_hi"), sem("h_ready"), sem("ht_ready")
        sq_ready, sq_used = sem("sq_ready"), sem("sq_used")
        root_ready, rec_ready, rstd_ready = sem("root_ready"), sem("rec_ready"), sem("rstd_ready")
        x_ready, y_scaled = sem("x_ready"), sem("y_scaled")
        pe_c, act_c, dve_c, pool_c = sem("pe_chain"), sem("act_chain"), sem("dve_chain"), sem("pool_chain")
        loads, x_in = sem("first_loads"), sem("x_in")
        consts = sem("consts_set")
        xt_turned, xt_ready, gain_turned, gain_ready = sem("xt_turned"), sem("xt_ready"), sem("gain_turned"), sem("gain_ready")
        phi_in, page_in = sem("phi_in"), [sem(f"page_in{n}") for n in range(4)]
        page_turned, page_ev, pe_in_land = sem("page_turned"), sem("page_ev"), sem("pe_in_land")
        pe_clear, phi_clear, pe_turned, pe_ev, bias_ev = sem("pe_clear"), sem("phi_clear"), sem("pe_turned"), sem("pe_ev"), sem("bias_ev")
        cmp_done, cmp_ev, vct_turned, vct_ev = sem("cmp_done"), sem("cmp_ev"), sem("vct_turned"), sem("vct_ev")
        e_in = sem("e_in")
        gate_turned, gate_ready, gates_s, gates_sev = sem("gate_turned"), sem("gate_ready"), sem("gates_s"), sem("gates_sev")
        ln_var, ln_root, svn_ready = sem("ln_var"), sem("ln_root"), sem("svn_ready")
        swapped, roped = sem("swapped"), sem("roped")
        k_turned, k_ready, in_done, in_ready, qd_ready = sem("k_turned"), sem("k_ready"), sem("in_done"), sem("in_ready"), sem("qd_ready")
        o_done, o_ev, st_done, st_ready = sem("o_done"), sem("o_ev"), sem("st_done"), sem("st_ready")
        s0_in = [sem("s0_in0"), sem("s0_in1")]
        ks_ready, ins_done, ins_ready, qds_ready = sem("ks_ready"), sem("ins_done"), sem("ins_ready"), sem("qds_ready")
        kns_turned, so_done, so_ev = sem("kns_turned"), sem("so_done"), sem("so_ev")
        s0_out, vb_ready, s0_done, s0_ready = sem("s0_out"), sem("vb_ready"), sem("s0_done"), sem("s0_ready")
        e_out = sem("e_out")
        hsq, hsum, hroot, hrec, hspread = sem("hsq"), sem("hsum"), sem("hroot"), sem("hrec"), sem("hspread")
        ret_ready, mixed, mix_ready = sem("ret_ready"), sem("mixed"), sem("mix_ready")
        rows_land, rows_turned, rows_ev = sem("rows_land"), sem("rows_turned"), sem("rows_ev")
        prev_set, tap0, conv_done, gelu_done = sem("prev_set"), sem("tap0"), sem("conv_done"), sem("gelu_done")
        gated_ready, act_hi, act_ready = sem("gated_ready"), sem("act_hi"), sem("act_ready")
        tail_set, tail_turned, tail_ev, rows_stored = sem("tail_set"), sem("tail_turned"), sem("tail_ev"), sem("rows_stored")
        o_in, o_ropes = sem("o_in"), sem("o_ropes")
        cp_turned, cp_ev, cp_done, cp_set, vp_turned = (sem("cp_turned"), sem("cp_ev"), sem("cp_done"), sem("cp_set"),
                                                               sem("vp_turned"))
        qs_turned = sem("qs_turned")
        qk_turned, qk_ev = sem("qk_turned"), sem("qk_ev")
        s_done, masked, exped, scaled, p_turned = sem("s_done"), sem("masked"), sem("exped"), sem("scaled"), sem("p_turned")
        p_ev, v_done = [sem("p_ev0"), sem("p_ev1")], sem("v_done")
        c_scored, c_sub, c_exped, c_ready, c_turned, c_ev = (sem("c_scored"), sem("c_sub"), sem("c_exped"), sem("c_ready"),
                                                             sem("c_turned"), sem("c_ev"))
        o_hi, o_lo = sem("o_hi"), sem("o_lo")
        rows_out_done, gates_out, gs_in, b_in = sem("rows_out_done"), sem("gates_out"), sem("gs_in"), sem("b_in")
        row_in = [sem(f"row_in{n}") for n in range(4)]
        z_scored, z_sub, z_exped, z_ready, z_turned, z_ev = (sem("z_scored"), sem("z_sub"), sem("z_exped"), sem("z_ready"),
                                                             sem("z_turned"), sem("z_ev"))
        ks_turned, ks_ev, ss_done, s_masked, s_exped, s_scaled = (sem("ks_turned"), sem("ks_ev"), sem("ss_done"), sem("s_masked"),
                                                                  sem("s_exped"), sem("s_scaled"))
        ps_turned, ps_ev, os_done, m_set, kn_turned, kn_ev = (sem("ps_turned"), sem("ps_ev"), sem("os_done"), sem("m_set"),
                                                              sem("kn_turned"), sem("kn_ev"))
        out_turned, out_ev, out_stored = sem("out_turned"), sem("out_ev"), sem("out_stored")

        RS = misc[:, 1:3, 0:TH]
        N_BAR = 4
        MIX_FIRST = (4, 5, 6, 7, 0, 1, 2, 3)
        block = ctx.enter_context(nc.Block())

        def meet(eng, order, n, wait=True):
            order(eng.drain(), phase)
            if wait:
                eng.wait_ge(phase, N_BAR * (n + 1))

        FILL_AFTER = [0, E_OUT, F0, O_IN, F1]
        NORM_GAIN = [0, 2, 4, 6, 1, 3, 5, 7]

        def heads_of(t, g):
            return qN[:, t, (g // 2) * 512:(g // 2) * 512 + 512].rearrange("p (r g d) -> p r g d", r=R, g=2)[:, :, g % 2, :]

        def sample_heads(z):
            j, g2, r2 = z // 4, (z // 2) % 2, z % 2
            c0 = 2 * (2 * j + g2)
            src = gemm[1][64 * g2:64 * g2 + 64, :, :].rearrange("p a (b j g r n) -> p (a b) j g r n", b=4, j=2, g=2, n=DS)

            def dst(h):
                return h[64 * r2:64 * r2 + 64, c0:c0 + 2, 0:NS].rearrange("p c (b n) -> p c b n", b=DB)
            return dst, src[:, :, j, g2, r2:r2 + 3:2, :].rearrange("p b c n -> p c b n")

        def attention_unit(n):
            grp, w = n // 8, n % 8
            return grp // 8, (grp % 8) // 2, grp % 2, w // 2, w % 2

        def unit_source(u):
            kind, layer, n, _ = UNITS[u]
            s = u % 2
            if kind in ("even_in", "even_out", "odd_out"):
                w = {"even_in": a["e_w_in"], "even_out": a["e_w_out"], "odd_out": a["o_w_out"]}[kind][0]
                yield raw[:, s, :].rearrange("p (k n) -> p k n", k=DC), w[:, 256 * n:256 * n + 256].rearrange("(k p) n -> p k n", p=P)
            elif kind == "odd_in":
                width = 48 if n == 10 else 256
                yield (raw[:, s, :].rearrange("p (k n) -> p k n", k=DC)[:, :, 0:width],
                       a["o_w_in"][0][:, 256 * n:256 * n + width].rearrange("(k p) n -> p k n", p=P))
            elif kind == "ffn_in":
                half, i = n
                for ab in range(2):
                    col = ab * FF + (half * FH + i) * P
                    yield (raw[:, s, :].rearrange("p (k n) -> p k n", k=DC)[:, :, P * ab:P * ab + P],
                           a["f_w_in"][layer][:, col:col + P].rearrange("(k p) n -> p k n", p=P))
            else:
                half, m = n
                yield (raw[:, s, 0:FH * P].rearrange("p (k n) -> p k n", k=FH),
                       a["f_w_out"][layer][half * FH * P:(half + 1) * FH * P, P * m:P * m + P].rearrange("(k p) n -> p k n", p=P))

        def unit_view(t, u):
            kind, _, n, _ = UNITS[u]
            if kind == "ffn_out":
                return t[:, u % 2, 0:FH * P]
            if kind == "odd_in" and n == 10:
                return t[:, u % 2, :].rearrange("p (k n) -> p k n", k=DC)[:, :, 0:48]
            return t[:, u % 2, :]

        landed, total = [], [0, 0]
        for u in range(len(UNITS)):
            total[u % 2] += 16 * (2 if UNITS[u][0] == "ffn_in" else 1)
            landed.append(total[u % 2])

        @block.sync
        def _(sp):
            sp.dma_start(ident[:, :], a["ident"]).then_inc(x_in, 16)
            sp.dma_start(xin[0:NS, 0, :], a["x_sample"].rearrange("b s d -> (b s) d")).then_inc(x_in, 16)
            for n in range(2):
                sp.dma_start(xin[:, 1 + 2 * n:3 + 2 * n, :], a["x_prompt"][0][256 * n:256 * n + 256, :].rearrange("(t p) d -> p t d", p=P)).then_inc(x_in, 16)
            for u in range(LAST_UNIT):
                if u == E_OUT + 3:
                    sp.wait_ge(phi_clear, 2)
                    for z, phi in enumerate((phiK, phiV)):
                        name = ("o_phi_k", "o_phi_v")[z]
                        for g in range(2):
                            sp.dma_start(phi[64 * g:64 * g + 64, :, 64 * g:64 * g + 64], a[name][0].rearrange("l d e -> d l e")).then_inc(phi_in, 16)
                if u >= 2:
                    sp.wait_ge(lo_ready, u - 1)
                for dst, src in unit_source(u):
                    sp.dma_start(dst, src).then_inc(raw_ready[u % 2], 16)

        @block.tensor
        def _(pe):
            order = Order(pe, pe_c)

            def turn(out, in_, sem_=None, k=P, base=0):
                ins = pe.transpose(out, in_, ident[base:base + k, base:base + k])
                if sem_ is not None:
                    order(ins, sem_)
                return ins

            def take_slot(c):
                if c >= 2:
                    pe.wait_ge(evacuated[c % 2], c // 2)

            def feature_chunk(u, j, nk, xh, xl, fill=None, ks=None):
                c = FIRST_CHUNK[u] + j
                width = P if nk == FH else 256
                take_slot(c)
                for n_k, k in enumerate(ks or range(nk)):
                    if fill is not None:
                        pe.wait_ge(h_ready, DC * fill + n_k + 1)
                    at = k * width + (j * P if width == 256 else 0)
                    wh, wl = wH[:, u % 2, at:at + P], wL[:, u % 2, at:at + P]
                    for part, (w, x) in enumerate(((wh, xh), (wh, xl), (wl, xh))):
                        for n in range(2):
                            ins = pe.matmul(gemm[c % 2][:, n, 0:TH], w, x[:, k, n * TH:(n + 1) * TH],
                                            start=(n_k == 0 and part == 0), stop=(n_k == nk - 1 and part == 2))
                order(ins, gemm_done)

            def token_chunk(u, t, width=256, fill=None):
                c = FIRST_CHUNK[u] + t
                take_slot(c)
                ts = tile_start(t)
                for k in range(DC):
                    if fill is not None:
                        pe.wait_ge(h_ready, DC * fill + k + 1)
                    wh, wl = wH[:, u % 2, k * 256:k * 256 + width], wL[:, u % 2, k * 256:k * 256 + width]
                    xh, xl = hH[:, k, ts:ts + P], hL[:, k, ts:ts + P]
                    for part, (x, w) in enumerate(((xh, wh), (xh, wl), (xl, wh))):
                        ins = pe.matmul(gemm[c % 2][:, 0, 0:width], x, w,
                                        start=(k == 0 and part == 0), stop=(k == DC - 1 and part == 2))
                order(ins, gemm_done)

            def unit(u):
                pe.wait_ge(lo_ready, u + 1)

            def square_sum(n, m, sq):
                pe.wait_ge(sq_ready, DC * n + m + 1)
                if m == 0 and n:
                    pe.wait_ge(root_ready, n)
                for q in range(4):
                    ins = pe.matmul(b4[32 * q:32 * q + 32, 0:TQ], mean_d[:, :], sq[m % 2][:, q * TQ:(q + 1) * TQ],
                                    start=(m == 0), stop=(m == DC - 1))
                order(ins, sq_used)

            def spread_rstd(n):
                pe.wait_ge(rec_ready, n + 1)
                for q in range(4):
                    ins = pe.matmul(misc[:, 1 + q // 2, (q % 2) * TQ:(q % 2 + 1) * TQ], spread[:, q, :], rr[:, :],
                                    start=True, stop=True)
                order(ins, rstd_ready)

            pe.wait_ge(x_in, 64)
            pe.wait_ge(consts, 3)
            for dc in range(DC):
                if dc >= 2:
                    pe.wait_ge(xt_ready, dc - 1)
                for t in range(4):
                    turn(misc[:, dc % 2, t * P:(t + 1) * P], xin[:, t + 1, dc * P:(dc + 1) * P])
                turn(misc[:, 2, dc * NS:(dc + 1) * NS], xin[0:NS, 0, dc * P:(dc + 1) * P], xt_turned, k=NS)
            pe.wait_ge(loads, LOADS)
            for dc in range(DC):
                turn(misc[:, 3, dc * 8:(dc + 1) * 8], gin[:, dc * P:(dc + 1) * P], gain_turned if dc == DC - 1 else None, k=8)

            pe.wait_ge(xt_ready, DC)
            for m in range(DC):
                square_sum(0, m, sqm)
            spread_rstd(0)
            meet(pe, order, 0, wait=False)

            def chunk_cols(c):
                return (NS + P * c, NS + P * (c + 1))

            def retention_scores(c):
                lo, hi = chunk_cols(c)
                pe.wait_ge(roped, 8)
                if c:
                    pe.wait_ge(s0_ready, c)
                for h in range(RH):
                    turn(b4[:, h * P:(h + 1) * P], kT[:, h, lo:hi], k_turned if h == RH - 1 else None)
                for h in range(RH):
                    ins = pe.matmul(b5[:, h * P:(h + 1) * P], kT[:, h, lo:hi], qT[:, h, lo:hi], start=True, stop=True)
                order(ins, in_done)

            def retention_values(c):
                pe.wait_ge(in_ready, c + 1)
                pe.wait_ge(qd_ready, c + 1)
                pe.wait_ge(so_ev, c + 1)
                if c:
                    pe.wait_ge(st_ready, c)
                for h in range(RH):
                    ins = pe.matmul(b6[:, h * P:(h + 1) * P], vN[:, c + 1, h * P:(h + 1) * P], inner[:, h, :],
                                    start=True, stop=(c == 0))
                    if c:
                        ins = pe.matmul(b6[:, h * P:(h + 1) * P], st[:, h, :], qd[:, h, :], start=False, stop=True)
                order(ins, o_done)
                pe.wait_ge(k_ready, c + 1)
                for h in range(RH):
                    ins = pe.matmul(b7[:, h * P:(h + 1) * P], kN[:, h, :], vN[:, c + 1, h * P:(h + 1) * P], start=True, stop=True)
                order(ins, st_done)

            def sample_scores():
                pe.wait_ge(roped, 8)
                for h in range(RH):
                    turn(b6[0:NS, h * P:(h + 1) * P], kT[:, h, 0:NS], kns_turned if h == RH - 1 else None)
                for h in range(RH):
                    ins = pe.matmul(b7[0:NS, h * NS:(h + 1) * NS], kT[:, h, 0:NS], qT[:, h, 0:NS], start=True, stop=True)
                order(ins, ins_done)

            def sample_outputs(h):
                pe.wait_ge(ins_ready, 1)
                pe.wait_ge(qds_ready, 1)
                pe.wait_ge(ks_ready, 1)
                if h:
                    pe.wait_ge(o_ev, h)
                pe.wait_ge(s0_in[h % 2], 16 * (h // 2 + 1))
                ins = pe.matmul(b6[:, 0:NS], vN[0:NS, 0, h * P:(h + 1) * P], inner_s[:, h, :],
                                start=True, stop=True, skip_group_check=True)
                for b in range(DB):
                    ins = pe.matmul(b6[:, DS * b:DS * (b + 1)], s0[:, b, h % 2, :], qds[:, h, DS * b:DS * (b + 1)],
                                    start=False, stop=True, skip_group_check=True)
                order(ins, so_done)

            def sample_states(h):
                pe.wait_ge(vb_ready, h + 1)
                for bb, bank in enumerate((b4, b5)):
                    ins = pe.matmul(bank, kNs[:, h, :], vB[:, 4 * bb:4 * bb + 4, :], start=True, stop=True)
                order(ins, s0_done)

            def mix_tokens():
                pe.wait_ge(svn_ready, 1)
                pe.wait_ge(gates_sev, 1)
                for c in range(NT):
                    if c >= 2:
                        pe.wait_ge(mix_ready, c - 1)
                    for g in range(4):
                        if c == 0:
                            ins = pe.matmul(misc[:, 0, g * NS:(g + 1) * NS], svn[0:NS, 0, g * P:(g + 1) * P], wmS[:, g, :], start=True, stop=True)
                        else:
                            ins = pe.matmul(misc[:, c % 2, g * P:(g + 1) * P], svn[:, c, g * P:(g + 1) * P], wmT[:, g, :], start=True, stop=True)
                    order(ins, mixed)

            def gate_weights():
                pe.wait_ge(e_in, E_LOADS)
                for g in range(4):
                    turn(b7[:, g * P:(g + 1) * P], sgw[:, g, :], gate_turned if g == 3 else None)
                pe.wait_ge(gate_ready, 1)
                for g in range(4):
                    ins = pe.matmul(b5[0:NS, g * NS:(g + 1) * NS], row_of_s[:, :],
                                    wmT[0:4, g, 0:4].unsqueeze(1).to_broadcast([4, DB, 4]), start=True, stop=True)
                order(ins, gates_s)

            pe.wait_ge(h_ready, DC)
            for n in range(12):
                u = E_IN + n
                unit(u)
                if UNITS[u][3] == 5:
                    for t in range(NT):
                        token_chunk(u, t)
                else:
                    for j in range(2):
                        feature_chunk(u, j, DC, hH, hL)
                        if n >= 8 and j == 0:
                            if n == 8:
                                pe.wait_ge(mix_ready, NT)
                                sample_scores()
                            retention_scores(n - 8)
                            sample_outputs(n - 8)
                        elif n >= 8:
                            retention_values(n - 8)
                            sample_states(n - 8)
                if n == 3:
                    gate_weights()
                elif n == 4:
                    mix_tokens()
            last = FIRST_CHUNK[E_OUT] - 1
            pe.wait_ge(evacuated[last % 2], last // 2 + 1)
            for h in range(RH):
                pe.wait_ge(hsq, h + 1)
                for n in range(2):
                    ins = pe.matmul(gemm[last % 2][32 * h:32 * h + 32, n, 0:TH], mean_k[:, :], hsqs[h % 2][:, n * TH:(n + 1) * TH],
                                    start=True, stop=True)
                order(ins, hsum)
            pe.wait_ge(o_ev, 4)
            pe.wait_ge(st_ready, 4)
            pe.wait_ge(hrec, 1)
            for h in range(RH):
                if h:
                    pe.wait_ge(ret_ready, h)
                for n in range(2):
                    ins = pe.matmul(misc[:, 2 + n, 0:TH], spread[:, h, :], kT[:, 1, n * TH:(n + 1) * TH], start=True, stop=True)
                order(ins, hspread)
            meet(pe, order, 1, wait=False)

            def turn_pages(first):
                if first == 0:
                    pe.wait_ge(pe_in_land, 64)
                    for z in range(2):
                        turn(b7[:, 32 * z:32 * z + CL], pe_in[:, z, :], pe_turned, k=CL)
                for n in (first, first + 1):
                    pe.wait_ge(page_in[n % 4], 16 * (n // 4 + 1))
                    if n >= 2:
                        pe.wait_ge(page_ev, n - 1)
                    for zj in range(4):
                        turn(misc[:, 1 + n % 2, zj * P:(zj + 1) * P], pages[:, n % 4, zj * P:(zj + 1) * P], page_turned if zj == 3 else None)

            def compress(z, l0, l1):
                if z == l0 == 0:
                    pe.wait_ge(page_ev, DB * NPG)
                    pe.wait_ge(pe_ev, 1)
                    pe.wait_ge(phi_in, PHI_LOADS)
                out = gemm[1][:, 0, 0:NBLK] if z else b7[:, 0:NBLK]
                for l in range(l0, l1):
                    ins = pe.matmul(out, (phiK, phiV)[z][:, l, :], cT[:, z, :, l:l + 16 * (NCS - 1) + 1:16],
                                    start=(l == 0), stop=(l == CL - 1))
                if l1 == CL:
                    order(ins, cmp_done)

            def project_out(first, fill, n):
                for i in range(4):
                    unit(first + i)
                    for j in range(2):
                        if fill and 2 * i + j:
                            turn_pages(4 * i + 2 * j - 2)
                        feature_chunk(first + i, j, DC, hH, hL, fill if i == j == 0 else None, MIX_FIRST)
                        if 2 * i + j:
                            square_sum(n, 2 * i + j - 1, sqm)
                if fill:
                    turn_pages(DB * NPG - 2)
                square_sum(n, DC - 1, sqm)
                if fill:
                    compress(0, 0, 4)
                spread_rstd(n)

            def rows_in_turned(layer, i0=0, i1=FH):
                pe.wait_ge(rows_land, ROWS_LAND * (layer + 1))
                for i in range(i0, i1):
                    n = i // 4 + 3 * layer
                    if i % 4 == 0 and n:
                        pe.wait_ge(rows_ev, n)
                    turn(b7[:, (i % 4) * P:(i % 4 + 1) * P], rows_in[:, i * P:(i + 1) * P],
                         rows_turned if i % 4 == 3 or i == FH - 1 else None)

            def tail_turn(e):
                pe.wait_ge(tail_set, e + 1)
                if e:
                    pe.wait_ge(tail_ev, e)
                turn(b7[0:64, 0:P], tail[:, e % 2, :], tail_turned)

            def ffn(layer, fill, n):
                if layer == 0:
                    pe.wait_ge(cmp_ev, 1)
                    rows_in_turned(layer, 0, 4)
                    last = FIRST_CHUNK[F0] - 1
                    pe.wait_ge(evacuated[1], last // 2 + 1)
                    compress(1, 0, CL)
                    rows_in_turned(layer, 4)
                else:
                    rows_in_turned(layer)
                first = F0 if layer == 0 else F1
                for half in range(2):
                    for i in range(FH):
                        u, e = first + half * (FH + DC) + i, (2 * layer + half) * FH + i
                        unit(u)
                        feature_chunk(u, 0, DC, hH, hL, fill if i == half == 0 else None)
                        if i == 0 and half == 0:
                            pe.wait_ge(rows_ev, 3 * (layer + 1))
                            if layer == 0:
                                pe.wait_ge(cmp_ev, 2)
                                for b in range(DB):
                                    turn(misc[0:2 * NCS, 1 + b // 4, (b % 4) * P:(b % 4 + 1) * P],
                                         vct[:, b, :, :].rearrange("p j m -> p (j m)"), vct_turned if b == DB - 1 else None)
                        if i:
                            tail_turn(e - 1)
                        feature_chunk(u, 1, DC, hH, hL)
                    tail_turn(e)
                    for m in range(DC):
                        u = first + half * (FH + DC) + FH + m
                        unit(u)
                        pe.wait_ge(act_ready, (2 * layer + half + 1) * FH)
                        feature_chunk(u, 0, FH, aH, aL)
                        if half and m:
                            square_sum(n, m - 1, sqf)
                square_sum(n, DC - 1, sqf)
                spread_rstd(n)

            project_out(E_OUT, 1, 1)
            compress(0, 4, 8)
            for m in range(DC):
                square_sum(2, m, sqm)
                compress(0, 8 + 3 * m, 11 + 3 * m)
            spread_rstd(2)
            ffn(0, 2, 3)
            for m in range(DC):
                square_sum(4, m, sqf)
            spread_rstd(4)
            meet(pe, order, 2)
            for n in range(11):
                u = O_IN + n
                unit(u)
                for t in range(NT):
                    token_chunk(u, t, 48 if n == 10 else 256, 3 if n == t == 0 else None)
            pe.wait_ge(o_in, ODD_LOADS)
            pe.wait_ge(o_ropes, 7)
            last = FIRST_CHUNK[O_IN + 11] - 1
            pe.wait_ge(evacuated[last % 2], last // 2 + 1)
            for z in range(4):
                if z >= 2:
                    pe.wait_ge(cp_ev, z - 1)
                for t in range(4):
                    turn(misc[:, z % 2, t * P:(t + 1) * P], kvN[:, t + 1, z * P:(z + 1) * P], cp_turned if t == 3 else None)
            for z in range(8):
                turn(b6[:, z * NS:(z + 1) * NS], qN[0:NS, 0, z * P:(z + 1) * P], qs_turned if z == 7 else None, k=NS)
            pe.wait_ge(cp_ev, 4)
            for z in range(2):
                for l in range(CL):
                    ins = pe.matmul(b7[:, z * 2 * NCP:(z + 1) * 2 * NCP], (phiK2, phiV2)[z][:, l, :],
                                    cPT[:, 2 * z:2 * z + 2, l:l + 16 * (NCP - 1) + 1:16], start=(l == 0), stop=(l == CL - 1))
                order(ins, cp_done)
            pe.wait_ge(cp_set, 2)
            for j in range(2):
                turn(b4[0:NCP, j * P:(j + 1) * P], vcPt[:, j, :], vp_turned if j else None)
            meet(pe, order, 3)

            def scores(n):
                j, qt, g2, r, br = attention_unit(n)
                half = slice(64 * g2, 64 * g2 + 64)
                keys = (qt + 1) * P
                if n >= 2:
                    pe.wait_ge(masked, n - 1)
                if n % 8 == 0:
                    if n:
                        pe.wait_ge(c_sub, n // 8)
                    for rr_ in range(R):
                        ins = pe.matmul(b6[:, rr_ * NCP:(rr_ + 1) * NCP], qTj[half, rr_, qt * P:(qt + 1) * P], kcP[half, j, :], start=True, stop=True)
                    order(ins, c_scored)
                order(pe.matmul(gemm[0][:, n % 2, 0:keys], qTj[half, r, qt * P:(qt + 1) * P], (ksT, kwT)[br][half, j, 0:keys],
                                start=True, stop=True), s_done)

            def turn_probs(n):
                _, qt, _, _, _ = attention_unit(n)
                pe.wait_ge(scaled, n + 1)
                if n >= 2:
                    pe.wait_ge(p_ev[n % 2], n // 2)
                for kt in range(qt + 1):
                    turn(gemm[1][:, n % 2, kt * P:(kt + 1) * P], pr[:, n % 2, kt * P:(kt + 1) * P], p_turned if kt == qt else None)
                if n % 8 == 0:
                    grp = n // 8
                    pe.wait_ge(c_ready, grp + 1)
                    if grp:
                        pe.wait_ge(c_ev, grp)
                    for r in range(R):
                        turn(b7[0:NCP, r * P:(r + 1) * P], cs[:, r, :], c_turned if r == R - 1 else None)

            def mix_values(n):
                j, qt, g2, r, br = attention_unit(n)
                g, grp = 2 * j + g2, n // 8
                pe.wait_ge(p_ev[n % 2], n // 2 + 1)
                if n % 8 == 0 and grp >= 2:
                    pe.wait_ge(o_lo, grp - 1)
                if n % 8 == 1:
                    pe.wait_ge(c_ev, grp + 1)
                out = misc[64 * (r % 2):64 * (r % 2) + 64, grp % 2, (r // 2) * P:(r // 2 + 1) * P]
                for kt in range(qt + 1):
                    ins = pe.matmul(out, kvN[:, 1 + kt, (2 * br + 3) * 256 + g * HD:(2 * br + 3) * 256 + (g + 1) * HD],
                                    pT[:, n % 2, kt * P:(kt + 1) * P], start=(br == 0 and kt == 0), stop=False)
                if br:
                    ins = pe.matmul(out, vcP[:, j, g2 * HD:(g2 + 1) * HD], cpT[:, r, :], start=False, stop=True)
                order(ins, v_done)

            for j in range(2):
                if j:
                    pe.wait_ge(c_ev, 8)
                for z in range(6):
                    n = 6 * j + z
                    if n >= 2:
                        pe.wait_ge(qk_ev, n - 1)
                    for t in range(4):
                        if z < R:
                            src = qN[:, t + 1, (j * R + z) * P:(j * R + z + 1) * P]
                        else:
                            src = kvN[:, t + 1, (2 * (z - 3)) * 256 + j * P:(2 * (z - 3)) * 256 + (j + 1) * P]
                        turn(misc[:, 2 + n % 2, t * P:(t + 1) * P], src, qk_turned if t == 3 else None)
                pe.wait_ge(qk_ev, 6 * (j + 1))
                for n in range(64 * j, 64 * j + 67):
                    if n < 64 * j + 64:
                        scores(n)
                    if 64 * j + 2 <= n < 64 * j + 66:
                        turn_probs(n - 2)
                    if n >= 64 * j + 3:
                        mix_values(n - 3)
            meet(pe, order, 4)

            def rows_turn(b):
                pe.wait_ge(row_in[b % 4], 48 * (b // 4 + 1))
                for br in range(2):
                    n = 2 * b + br
                    if b:
                        pe.wait_ge(ks_ev, n - 1)
                    for j in range(2):
                        for pg in range(NPG):
                            ins = turn(misc[:, br, (2 * j + pg) * P:(2 * j + pg + 1) * P], row_slot[b % 4][:, br, pg, j * P:(j + 1) * P])
                    order(ins, ks_turned)

            def sample_scores(b):
                for br in range(2):
                    n = 2 * b + br
                    pe.wait_ge(ks_ev, n + 1)
                    if b:
                        pe.wait_ge(s_masked, n - 1)
                    for j in range(2):
                        ins = pe.matmul(gemm[0][64 * j:64 * j + 64, br, 0:KW], qS[:, b, j, :, :],
                                        kTs[:, b % 2, br, j, :], start=True, stop=True)
                    order(ins, ss_done)

            for z in range(4):
                turn(misc[:, 2, z * NS:(z + 1) * NS], kvN[0:NS, 0, (2 * (z // 2) + 2) * 256 + (z % 2) * P:(2 * (z // 2) + 2) * 256 + (z % 2 + 1) * P],
                     kn_turned if z == 3 else None, k=NS)
            for b in range(DB):
                for j in range(2):
                    ins = pe.matmul(gemm[0][64 * j:64 * j + 64, 0, b * NCS:(b + 1) * NCS], qS[:, b, j, :, :], kcs[:, b, j, :], start=True, stop=True)
            order(ins, z_scored)
            rows_turn(0)
            pe.wait_ge(kn_ev, 2)
            pe.wait_ge(z_sub, 1)
            sample_scores(0)
            pe.wait_ge(z_ready, 1)
            for b in range(DB):
                turn(gemm[1][0:2 * NCS, b // 4, (b % 4) * P:(b % 4 + 1) * P], cpb[:, b, :, :].rearrange("p j m -> p (j m)"),
                     z_turned if b == DB - 1 else None)
            for b in range(DB):
                if b + 1 < DB:
                    rows_turn(b + 1)
                for br in range(2):
                    n = 2 * b + br
                    pe.wait_ge(s_scaled, n + 1)
                    if b:
                        pe.wait_ge(ps_ev, 2 * b)
                    for kt in range(3):
                        w = P if kt < 2 else NS
                        turn(misc[0:w, 2 + br, kt * P:(kt + 1) * P], prs[:, b % 2, br, kt * P:kt * P + w], ps_turned if kt == 2 else None)
                if b + 1 < DB:
                    sample_scores(b + 1)
                if b == 0:
                    pe.wait_ge(z_ev, 1)
                pe.wait_ge(ps_ev, 2 * (b + 1))
                for j in range(2):
                    at = (b % 4) * P + 64 * j
                    out = gemm[1][:, b // 4, at:at + 64]
                    for br in range(2):
                        for kt in range(3):
                            k = P if kt < 2 else NS
                            if kt < 2:
                                v = row_slot[b % 4][:, br, kt, 256 + j * P:256 + (j + 1) * P]
                            else:
                                v = kvN[0:NS, 0, (2 * br + 3) * 256 + j * P:(2 * br + 3) * 256 + (j + 1) * P]
                            pe.matmul(out, v, pTs[0:k, br, kt, 64 * j:64 * j + 64], start=(br == 0 and kt == 0), stop=False)
                    ins = pe.matmul(out, vcs[:, b, :], cpTs[:, b, 64 * j:64 * j + 64], start=False, stop=True)
                order(ins, os_done)
            meet(pe, order, 5, wait=False)
            pe.wait_ge(o_lo, 16 + 8)
            project_out(O_OUT, None, 5)
            for m in range(DC):
                square_sum(6, m, sqm)
            spread_rstd(6)
            ffn(1, 4, 7)
            finish_turn = range(DC)
            for m in finish_turn:
                pe.wait_ge(x_ready, DC * (FINAL_POST + 1))
                for half in range(2):
                    n = 2 * m + half
                    if n >= 2:
                        pe.wait_ge(out_ev, n - 1)
                    tiles = (0, 1) if half == 0 else (2, 3, 4)
                    for z, t in enumerate(tiles):
                        w = NS if t == 0 else P
                        turn(misc[0:w, n % 2, z * P:(z + 1) * P],
                             xT[:, m, tile_start(t):tile_start(t) + w], out_turned if z == len(tiles) - 1 else None)

        @block.scalar
        def _(act):
            order = Order(act, act_c)

            def activate(out, in_, func, sem_=None, **kw):
                order(act.activation(out, in_, func, **kw), sem_)

            def split_hi(u):
                if u >= LAST_UNIT:
                    return
                act.wait_ge(raw_ready[u % 2], landed[u])
                if u >= 2:
                    act.wait_ge(gemm_done, FIRST_CHUNK[u - 1])
                activate(unit_view(wH, u), unit_view(raw, u), ACT.Copy, hi_ready)

            def square(n, m, src, sq):
                if DC * n + m >= 2:
                    act.wait_ge(sq_used, DC * n + m - 1)
                activate(sq[m % 2], src, ACT.Square, sq_ready)

            def root(n):
                act.wait_ge(sq_used, DC * (n + 1))
                if n:
                    act.wait_ge(rec_ready, n)
                activate(rq[:, :], b4[:, 0:TQ], ACT.Sqrt, root_ready, bias=eps[:, 0:1])

            def fill_hi(fill, k, src, first=0):
                if k == first and fill:
                    act.wait_ge(gemm_done, FIRST_CHUNK[FILL_AFTER[fill]])
                activate(hH[:, k, :], src, ACT.Copy, h_hi)

            def norm_fill(pf, fill):
                for k in range(DC):
                    act.wait_ge(ht_ready, DC * pf + k + 1)
                    fill_hi(fill, k, y[:, k, :])

            def chunk_ready(c):
                act.wait_ge(gemm_done, c + 1)
                return gemm[c % 2]

            for dc in range(DC):
                act.wait_ge(xt_turned, dc + 1)
                activate(xT[:, dc, NS:T], misc[:, dc % 2, :], ACT.Copy, xt_ready)
            act.wait_ge(gain_ready, 2)
            for m in range(DC):
                square(0, m, xT[:, m, :], sqm)
            root(0)

            split_hi(0)
            norm_fill(0, 0)
            meet(act, order, 0)

            for n in range(12):
                u = E_IN + n
                split_hi(u + 1)
                what = UNITS[u][2]
                for j in range(UNITS[u][3]):
                    c = FIRST_CHUNK[u] + j
                    if what < 4:
                        rc = 2 * what + j
                        ps = chunk_ready(c)
                        if rc:
                            act.wait_ge(roped, rc)
                        activate(halves(swp[0:64, :]), ps[64:128, :, 0:TH], ACT.Copy)
                        activate(halves(swp[64:128, :]), ps[0:64, :, 0:TH], ACT.Copy, swapped)
                    elif what < 6:
                        activate(vN[:, j, 256 * (what % 2):256 * (what % 2) + 256], chunk_ready(c)[:, 0, 0:256], ACT.Copy, evacuated[c % 2])
                    elif what in (6, 7):
                        activate(halves(silu_g[:, 2 * (what - 6) + j, :]), chunk_ready(c)[:, :, 0:TH], ACT.Silu, evacuated[c % 2])
                if n == 1:
                    act.wait_ge(ln_var, 1)
                    activate(lns[:, 2, :], lns[:, 1, :], ACT.Sqrt, ln_root, bias=eps[:, 0:1], scale=1.0 / P)
            act.wait_ge(o_ev, 4)
            act.wait_ge(so_ev, 4)
            for h in range(RH):
                if h >= 2:
                    act.wait_ge(hsum, h - 1)
                activate(hsqs[h % 2][:, :], qT[:, h, :], ACT.Square, hsq)
            for k in range(4, DC):
                fill_hi(1, k, uT[:, k - 4, :], 4)
            act.wait_ge(hsum, RH)
            activate(halves(kT[:, 0, :]), gemm[(FIRST_CHUNK[E_OUT] - 1) % 2][:, :, 0:TH], ACT.Sqrt, hroot, bias=eps[:, 0:1])
            for k in range(4):
                act.wait_ge(ret_ready, k + 1)
                fill_hi(1, k, qT[:, k, :], 4)
            meet(act, order, 1)

            def take_pages(first):
                if first == 0:
                    act.wait_ge(pe_clear, 1)
                    act.wait_ge(pe_turned, 2)
                    activate(cT[:, :, 2 * DB, 0:CL], b7[:, 0:64].rearrange("p (z l) -> p z l", z=2), ACT.Copy, pe_ev)
                for n in (first, first + 1):
                    b, pg = n // NPG, n % NPG
                    act.wait_ge(page_turned, n + 1)
                    activate(cT[:, :, 0:2 * DB, :].rearrange("p z (j b) t -> p z j b t", j=2)[:, :, :, b, pg * PAGE:(pg + 1) * PAGE],
                             misc[:, 1 + n % 2, :].rearrange("p (z j t) -> p z j t", z=2, j=2), ACT.Copy, page_ev)

            def take_blocks(z):
                ps = gemm[1][:, 0, :] if z else b7
                act.wait_ge(cmp_done, z + 1)
                activate(pe_bias[:, z:z + 1], ps[:, 2 * DB * NCS:2 * DB * NCS + 1], ACT.Copy, bias_ev)
                act.wait_ge(bias_ev, z + 1)
                activate((kcs, vct)[z][:, :, :, :].rearrange("p b j m -> p j b m"),
                         ps[:, 0:2 * DB * NCS].rearrange("p (j b m) -> p j b m", j=2, b=DB), ACT.Identity, cmp_ev,
                         bias=pe_bias[:, z:z + 1])

            def project_out(first, n):
                for i in range(4):
                    split_hi(first + i + 1)
                    for j in range(2):
                        if first == E_OUT and 2 * i + j:
                            take_pages(4 * i + 2 * j - 2)
                        c, m = FIRST_CHUNK[first + i] + j, 2 * i + j
                        activate(halves(y[:, m, :]), chunk_ready(c)[:, :, 0:TH], ACT.Copy, evacuated[c % 2])
                        act.wait_ge(evacuated[c % 2], c // 2 + 1)
                        square(n, m, y[:, m, :], sqm)
                if first == E_OUT:
                    take_pages(DB * NPG - 2)
                root(n)

            def next_squares(n, post, sq):
                for m in range(DC):
                    act.wait_ge(x_ready, DC * post + m + 1)
                    square(n, m, xT[:, m, :], sq)
                root(n)

            def ffn(layer, n):
                first = F0 if layer == 0 else F1
                for b in range(3):
                    act.wait_ge(rows_turned, 3 * layer + b + 1)
                    w = min(4, FH - 4 * b)
                    activate(rows_t[:, 4 * b:4 * b + w, :], b7[:, 0:w * P].rearrange("p (i r) -> p i r", i=w), ACT.Copy, rows_ev)
                    if layer == b == 0:
                        take_blocks(1)
                for half in range(2):
                    for i in range(FH):
                        u, e = first + half * (FH + DC) + i, (2 * layer + half) * FH + i
                        U = up[e % 2]
                        for j in range(2):
                            c = FIRST_CHUNK[u] + j
                            ps = chunk_ready(c)
                            if j == 0 and e >= 2:
                                act.wait_ge(conv_done, 2 * e - 2)
                                act.wait_ge(tail_set, e - 1)
                            activate(U[:, j, 0:6 * DB].rearrange("p (b r) -> p b r", b=DB)[:, :, 2:6],
                                     ps[:, 0, 0:NS].rearrange("p (b r) -> p b r", b=DB), ACT.Copy)
                            activate(U[:, j, 50:50 + TH - NS], ps[:, 0, NS:TH], ACT.Copy)
                            activate(U[:, j, 50 + TH - NS:UW], ps[:, 1, 0:TH], ACT.Copy, evacuated[c % 2])
                            act.wait_ge(prev_set, e + 1)
                            if e:
                                act.wait_ge(gated_ready, e)
                            w = rows_t[:, i, 32 * (2 * j + half):32 * (2 * j + half) + 32]
                            act.wait_ge(evacuated[c % 2], c // 2 + 1)
                            activate(conv[:, j, :], U[:, j, 0:CW], ACT.Identity, tap0, bias=w[:, 19:20], scale=w[:, 16:17])
                            if j == 0:
                                split_hi(u + 1)
                                if e == 0:
                                    act.wait_ge(vct_turned, 1)
                                    activate(vcs[:, :, :], misc[0:2 * NCS, 1:3, :].rearrange("p a (b e) -> p (a b) e", b=4), ACT.Copy, vct_ev)
                                if i:
                                    tail_out(e - 1, i - 1, half, layer)
                        act.wait_ge(conv_done, 2 * e + 1)
                        activate(conv[:, 0, :], conv[:, 0, :], ACT.Gelu_apprx_tanh, gelu_done)
                        act.wait_ge(gated_ready, e + 1)
                        if i == 0:
                            act.wait_ge(gemm_done, FIRST_CHUNK[first + half * (FH + DC)])
                        activate(aH[:, i, :], gated[:, :], ACT.Copy, act_hi)
                    tail_out(e, FH - 1, half, layer)
                    for m in range(DC):
                        u = first + half * (FH + DC) + FH + m
                        split_hi(u + 1)
                        c = FIRST_CHUNK[u]
                        if half == 0:
                            activate(halves(y[:, m, :]), chunk_ready(c)[:, :, 0:TH], ACT.Copy, evacuated[c % 2])
                        else:
                            act.wait_ge(evacuated[c % 2], c // 2 + 1)
                            square(n, m, y[:, m, :], sqf)
                root(n)

            def tail_out(e, i, half, layer):
                act.wait_ge(tail_turned, e + 1)
                if i == 0 and (half or layer):
                    act.wait_ge(rows_stored, 64 * (2 * layer + half))
                activate(rows_out[:, i * P:(i + 1) * P], b7[0:64, 0:P], ACT.Copy, tail_ev)

            project_out(E_OUT, 1)
            next_squares(2, 0, sqm)
            take_blocks(0)
            norm_fill(1, 2)
            ffn(0, 3)
            next_squares(4, 1, sqf)
            norm_fill(2, 3)
            meet(act, order, 2)
            for n in range(11):
                u = O_IN + n
                split_hi(u + 1)
                what = UNITS[u][2]
                for t in range(NT):
                    c = FIRST_CHUNK[u] + t
                    ps = chunk_ready(c)[:, 0, :]
                    if what < 4:
                        activate(heads_of(t, what), ps[:, 0:256].rearrange("p (r d) -> p r d", r=R), ACT.Copy, evacuated[c % 2])
                    elif what < 10:
                        activate(kvN[:, t, (what - 4) * 256:(what - 3) * 256], ps[:, 0:256], ACT.Copy, evacuated[c % 2])
                    else:
                        activate(gN[:, t, :], ps[:, 0:48], ACT.Sigmoid, evacuated[c % 2])
            for z in range(4):
                act.wait_ge(cp_turned, z + 1)
                activate(cPT[:, z, :], misc[:, z % 2, :], ACT.Copy, cp_ev)
            act.wait_ge(cp_done, 2)
            for z in range(2):
                activate((kcP, vcPt)[z][:, :, :], b7[:, z * 2 * NCP:(z + 1) * 2 * NCP].rearrange("p (j m) -> p j m", j=2),
                         ACT.Identity, cp_set, bias=pe_bias[:, z:z + 1])
            act.wait_ge(vp_turned, 1)
            activate(vcP[:, :, :], b4[0:NCP, 0:2 * P].rearrange("p (j e) -> p j e", j=2), ACT.Copy)
            meet(act, order, 3)

            def exps(n):
                _, qt, _, _, _ = attention_unit(n)
                keys = (qt + 1) * P
                act.wait_ge(masked, n + 1)
                if n >= 2:
                    act.wait_ge(p_turned, n - 1)
                activate(pr[:, n % 2, 0:keys], sm[:, n % 2, 0:keys], ACT.Exp, exped, bias=negmax[:, n % 2:n % 2 + 1], scale=-1.0,
                         accum_out=rsum[:, n % 2:n % 2 + 1])
                if n % 8 == 0:
                    act.wait_ge(c_sub, n // 8 + 1)
                    activate(cs[:, :, :], cs[:, :, :], ACT.Exp, c_exped, scale=SCALE)

            def take_probs(n):
                _, qt, _, _, _ = attention_unit(n)
                keys = (qt + 1) * P
                if n % 2 == 0:
                    act.wait_ge(p_turned, n + 1)
                    if n >= 2:
                        act.wait_ge(v_done, n - 1)
                    activate(pT[:, 0, 0:keys], gemm[1][:, 0, 0:keys], ACT.Copy, p_ev[0])
                if n % 8 == 0:
                    grp = n // 8
                    act.wait_ge(c_turned, grp + 1)
                    if grp:
                        act.wait_ge(v_done, 8 * grp)
                    activate(cpT[:, :, :], b7[0:NCP, :].rearrange("p (r q) -> p r q", r=R), ACT.Copy, c_ev)

            def heads_hi(grp):
                j, qt, g2, _, _ = attention_unit(8 * grp)
                act.wait_ge(v_done, 8 * (grp + 1))
                c0 = 2 * (2 * j + g2)
                activate(hH[:, c0:c0 + 2, NS + qt * P:NS + (qt + 1) * P], misc[:, grp % 2, 0:2 * P].rearrange("p (c q) -> p c q", c=2), ACT.Copy, o_hi)

            for j in range(2):
                for z in range(6):
                    n = 6 * j + z
                    act.wait_ge(qk_turned, n + 1)
                    if j and z == 0:
                        act.wait_ge(s_done, 64)
                    activate(qTj[:, z, :] if z < R else (ksT, kwT)[z - R][:, j, :], misc[:, 2 + n % 2, :], ACT.Copy, qk_ev)
                for n in range(64 * j, 64 * j + 67):
                    if n >= 64 * j + 3:
                        take_probs(n - 3)
                    if n < 64 * j + 64:
                        exps(n)
                    if n >= 64 * j + 3:
                        if (n - 3) % 8 == 1 and n - 3 > 64 * j + 8:
                            heads_hi((n - 3) // 8 - 1)
                heads_hi(8 * j + 7)
            meet(act, order, 4)

            def take_keys(b):
                for br in range(2):
                    n = 2 * b + br
                    act.wait_ge(ks_turned, n + 1)
                    if b >= 2:
                        act.wait_ge(ss_done, n - 3)
                    activate(kTs[:, b % 2, br, :, 0:PAST], misc[:, br, :].rearrange("p (j t) -> p j t", j=2), ACT.Copy, ks_ev)

            def sample_exps(b):
                for br in range(2):
                    n = 2 * b + br
                    act.wait_ge(s_masked, n + 1)
                    if b >= 2:
                        act.wait_ge(ps_turned, n - 3)
                    activate(prs[:, b % 2, br, :], sms[:, b % 2, br, :], ACT.Exp, s_exped, bias=nms[:, b, br:br + 1], scale=-1.0, accum_out=rss[:, b, br:br + 1])

            act.wait_ge(kn_turned, 1)
            for slot in range(2):
                activate(kTs[:, slot, :, :, PAST:KW], misc[:, 2, 0:4 * NS].rearrange("p (e j t) -> p e j t", e=2, j=2), ACT.Copy, kn_ev)
            take_keys(0)
            act.wait_ge(z_sub, 1)
            activate(css[:, :, :], css[:, :, :], ACT.Exp, z_exped, scale=SCALE)
            sample_exps(0)
            act.wait_ge(z_turned, 1)
            activate(cpTs[:, :, :], gemm[1][0:2 * NCS, :, :].rearrange("p a (b e) -> p (a b) e", b=4), ACT.Copy, z_ev)
            for b in range(DB):
                if b + 1 < DB:
                    take_keys(b + 1)
                act.wait_ge(ps_turned, 2 * (b + 1))
                if b:
                    act.wait_ge(os_done, b)
                activate(pTs[:, :, 0:2, :], misc[:, 2:4, 0:2 * P].rearrange("p e (k q) -> p e k q", k=2), ACT.Copy, ps_ev)
                activate(pTs[0:NS, :, 2, :], misc[0:NS, 2:4, 2 * P:3 * P], ACT.Copy, ps_ev)
                if b + 1 < DB:
                    sample_exps(b + 1)
            act.wait_ge(os_done, DB)
            for z in range(8):
                dst, src = sample_heads(z)
                activate(dst(hH), src, ACT.Copy, o_hi)
            meet(act, order, 5)
            project_out(O_OUT, 5)
            next_squares(6, 2, sqm)
            norm_fill(3, 4)
            ffn(1, 7)
            for n in range(2 * DC):
                m, half = n // 2, n % 2
                act.wait_ge(out_turned, n + 1)
                if half == 0:
                    activate(yout[0:NS, 0, m * P:(m + 1) * P], misc[0:NS, 0, 0:P], ACT.Copy)
                    activate(yout[:, 1, m * P:(m + 1) * P], misc[:, 0, P:2 * P], ACT.Copy, out_ev)
                else:
                    activate(yout[:, 2:5, m * P:(m + 1) * P], misc[:, 1, 0:3 * P].rearrange("p (t f) -> p t f", t=3), ACT.Copy, out_ev)

        @block.vector
        def _(dve):
            order = Order(dve, dve_c)

            def split_lo(u):
                if u >= LAST_UNIT:
                    return
                dve.wait_ge(hi_ready, u + 1)
                order(dve.tensor_tensor(unit_view(wL, u), unit_view(raw, u), unit_view(wH, u).bitcast(F32), ALU.subtract), lo_ready)

            def rec(n):
                dve.wait_ge(root_ready, n + 1)
                if n:
                    dve.wait_ge(rstd_ready, n)
                order(dve.reciprocal(rr[:, :], rq[:, :]), rec_ready)
                dve.wait_ge(rstd_ready, n + 1)

            def fill_lo(fill, k, src, first=0):
                dve.wait_ge(h_hi, DC * fill + (k - first) % DC + 1)
                order(dve.tensor_tensor(hL[:, k, :], src, hH[:, k, :].bitcast(F32), ALU.subtract), h_ready)

            def norm_fill(n, fill):
                rec(n)
                for k in range(DC + 1):
                    if k < DC:
                        order(dve.scalar_tensor_tensor(halves(y[:, k, :]), halves(xT[:, k, :]), gains[:, k, NORM_GAIN[n]:NORM_GAIN[n] + 1],
                                                       RS, ALU.mult, ALU.mult), ht_ready)
                    if k:
                        fill_lo(fill, k - 1, y[:, k - 1, :])

            def residual(n):
                rec(n)
                for k in range(DC + 1):
                    if k < DC:
                        order(dve.scalar_tensor_tensor(halves(y[:, k, :]), halves(y[:, k, :]), gains[:, k, NORM_GAIN[n]:NORM_GAIN[n] + 1],
                                                       RS, ALU.mult, ALU.mult), y_scaled)
                    if k:
                        dve.wait_ge(y_scaled, DC * (n // 2) + k)
                        order(dve.tensor_tensor(xT[:, k - 1, :], xT[:, k - 1, :], y[:, k - 1, :], ALU.add), x_ready)
                order.wait()

            dve.wait_ge(xt_turned, DC)
            order(dve.tensor_copy(xT[:, :, 0:NS], misc[:, 2, 0:DC * NS].rearrange("p (c t) -> p c t", c=DC)), gain_ready)
            dve.wait_ge(gain_turned, 1)
            order(dve.tensor_copy(gains[:, :, :], misc[:, 3, 0:DC * 8].rearrange("p (c t) -> p c t", c=DC)), gain_ready)
            split_lo(0)
            norm_fill(0, 0)
            meet(dve, order, 0)

            def gate_weights():
                dve.wait_ge(gate_turned, 1)
                order(dve.tensor_tensor(wmT[:, :, :], by4(b7), tril[:, :].unsqueeze(1).to_broadcast([P, 4, P]), ALU.mult), gate_ready)
                dve.wait_ge(gates_s, 1)
                order(dve.tensor_tensor(wmS[:, :, :], b5[0:NS, 0:4 * NS].rearrange("p (g i) -> p g i", g=4),
                                        same_s[:, :].unsqueeze(1).to_broadcast([NS, 4, NS]), ALU.mult), gates_sev)

            def layer_norm():
                dve.wait_ge(e_in, E_LOADS)
                allx = svn[:, :, :].rearrange("p t (g c) -> p (t g) c", g=4)

                def per_group(row):
                    return lns[:, row, :].unsqueeze(2).to_broadcast([P, 4 * NT, P])

                order.wait()
                order(dve.tensor_reduce(lns[:, 3, :], allx, AX_X, ALU.add))
                order.wait()
                order(dve.tensor_scalar(lns[:, 0, :], lns[:, 3, :], -1.0 / P, None, ALU.mult))
                order.wait()
                order(dve.tensor_tensor(allx, allx, per_group(0), ALU.add))
                for t in range(NT):
                    order.wait()
                    order(dve.tensor_tensor(lnt[:, :], svn[:, t, :], svn[:, t, :], ALU.mult))
                    order.wait()
                    order(dve.tensor_reduce(lns[:, 1, 4 * t:4 * t + 4], by4(lnt[:, :]), AX_X, ALU.add),
                          ln_var if t == NT - 1 else None)

            def layer_norm_scaled():
                allx = svn[:, :, :].rearrange("p t (g c) -> p (t g) c", g=4)

                def per_group(row):
                    return lns[:, row, :].unsqueeze(2).to_broadcast([P, 4 * NT, P])

                dve.wait_ge(ln_root, 1)
                order(dve.reciprocal(lns[:, 3, :], lns[:, 2, :]))
                order.wait()
                order(dve.tensor_tensor(allx, allx, per_group(3), ALU.mult))
                for op, vec in ((ALU.mult, lng), (ALU.add, lnb)):
                    order.wait()
                    order(dve.tensor_tensor(svn[:, :, :], svn[:, :, :], vec[:, :].unsqueeze(1).to_broadcast([P, NT, 512]), op),
                          svn_ready if vec is lnb else None)

            def rope(c, what, j):
                rc = 2 * what + j
                dst, h = (qT, rc) if what < 2 else (kT, rc - 4)
                scale = 1.0 if what < 2 else DK ** -0.5
                dve.wait_ge(swapped, rc + 1)
                order(dve.scalar_tensor_tensor(halves(dst[:, h, :]), gemm[c % 2][:, :, 0:TH], scale, halves(cosE[:, :]),
                                               ALU.mult, ALU.mult), evacuated[c % 2])
                order(dve.scalar_tensor_tensor(swp[:, :], swp[:, :], scale, sinE[:, :], ALU.mult, ALU.mult))
                order.wait()
                order(dve.tensor_tensor(dst[:, h, :], dst[:, h, :], swp[:, :], ALU.add), roped)

            def retention_scores(c):
                lo, hi = NS + P * c, NS + P * (c + 1)
                dve.wait_ge(k_turned, c + 1)
                if c:
                    dve.wait_ge(st_done, c)
                order(dve.tensor_tensor(kN[:, :, :], by4(b4), kdec[:, 0:4].unsqueeze(2).to_broadcast([P, 4, P]), ALU.mult), k_ready)
                order(dve.tensor_tensor(qd[:, :, :], qT[:, :, lo:hi], qdec[:, :, :], ALU.mult), qd_ready)
                dve.wait_ge(in_done, c + 1)
                order(dve.tensor_tensor(inner[:, :, :], by4(b5), decay[:, :, :], ALU.mult), in_ready)

            def retention_values(c):
                lo, hi = NS + P * c, NS + P * (c + 1)
                dve.wait_ge(o_done, c + 1)
                order(dve.tensor_copy(qT[:, :, lo:hi], by4(b6)), o_ev)
                dve.wait_ge(st_done, c + 1)
                if c == 0:
                    order(dve.tensor_copy(st[:, :, :], by4(b7)), st_ready)
                else:
                    for h in range(RH):
                        order(dve.scalar_tensor_tensor(st[:, h, :], st[:, h, :], float(GAMMA[h] ** P), b7[:, h * P:(h + 1) * P],
                                                       ALU.mult, ALU.add), st_ready if h == RH - 1 else None)

            def sample_scores():
                dve.wait_ge(kns_turned, 1)
                order(dve.tensor_tensor(kNs[:, :, :], by4(b6[0:NS, :]), kdec[0:NS, 4:8].unsqueeze(2).to_broadcast([NS, 4, P]), ALU.mult), ks_ready)
                order(dve.tensor_tensor(qds[:, :, :], qT[:, :, 0:NS], qdecs[:, :, :], ALU.mult), qds_ready)
                dve.wait_ge(ins_done, 1)
                order(dve.tensor_tensor(inner_s[:, :, :], b7[0:NS, 0:4 * NS].rearrange("p (h i) -> p h i", h=4), decs[:, :, :], ALU.mult), ins_ready)

            def sample_outputs(h):
                dve.wait_ge(so_done, h + 1)
                order(dve.tensor_copy(qT[:, h, 0:NS], b6[:, 0:NS]), so_ev)
                if h:
                    dve.wait_ge(s0_done, h)
                order(dve.tensor_tensor(vB[:, :, :], vN[0:NS, 0, h * P:(h + 1) * P].unsqueeze(1).to_broadcast([NS, DB, P]),
                                        batch_of[:, :].unsqueeze(2).to_broadcast([NS, DB, P]), ALU.mult), vb_ready)

            def sample_states(h):
                dve.wait_ge(s0_done, h + 1)
                for bb, bank in enumerate((b4, b5)):
                    part = s0[:, 4 * bb:4 * bb + 4, h % 2, :]
                    order(dve.scalar_tensor_tensor(part, part, float(GAMMA[h] ** DS), by4(bank), ALU.mult, ALU.add),
                          s0_ready if bb else None)

            def mix_tokens():
                for c in range(NT):
                    dve.wait_ge(mixed, c + 1)
                    w = NS if c == 0 else P
                    ps = misc[:, c % 2, 0:4 * w].rearrange("p (g i) -> p g i", g=4)
                    if c:
                        order(dve.tensor_tensor(uT[:, :, tile_start(c):tile_start(c) + P], ps, sgb[:, :, :], ALU.add), mix_ready)
                    else:
                        for g in range(4):
                            order(dve.tensor_tensor(uT[:, g, 0:NS].rearrange("p (b i) -> p b i", b=DB), ps[:, g, :].rearrange("p (b i) -> p b i", b=DB),
                                                    sgb[:, g, 0:DS].unsqueeze(1).to_broadcast([P, DB, DS]), ALU.add), mix_ready if g == 3 else None)

            for n in range(12):
                u = E_IN + n
                split_lo(u + 1)
                what = UNITS[u][2]
                for j in range(UNITS[u][3]):
                    c = FIRST_CHUNK[u] + j
                    if what < 4:
                        rope(c, what, j)
                    elif what >= 10:
                        dve.wait_ge(gemm_done, c + 1)
                        order(dve.tensor_copy(svn[:, j, 256 * (what % 2):256 * (what % 2) + 256], gemm[c % 2][:, 0, 0:256]), evacuated[c % 2])
                    elif what in (8, 9):
                        m = 2 * (what - 8) + j
                        dve.wait_ge(gemm_done, c + 1)
                        order(dve.tensor_tensor(halves(uT[:, m, :]), halves(uT[:, m, :]), gemm[c % 2][:, :, 0:TH], ALU.mult), evacuated[c % 2])
                    if n >= 8 and j == 0:
                        if n == 8:
                            sample_scores()
                        retention_scores(n - 8)
                        sample_outputs(n - 8)
                    elif n >= 8:
                        retention_values(n - 8)
                        sample_states(n - 8)
                if n == 1:
                    layer_norm()
                elif n == 2:
                    layer_norm_scaled()
                elif n == 3:
                    gate_weights()
                elif n == 4:
                    mix_tokens()
            last = FIRST_CHUNK[E_OUT] - 1
            dve.wait_ge(evacuated[last % 2], last // 2 + 1)
            for h in range(RH):
                dve.wait_ge(hsq, h + 1)
                order(dve.tensor_tensor(qT[:, h, :], qT[:, h, :], silu_g[:, h, :], ALU.mult))
            for k in range(4, DC):
                fill_lo(1, k, uT[:, k - 4, :], 4)
            dve.wait_ge(hroot, 1)
            order(dve.reciprocal(kT[:, 1, :], kT[:, 0, :]), hrec)
            for h in range(RH + 1):
                if h < RH:
                    dve.wait_ge(hspread, h + 1)
                    order(dve.tensor_tensor(halves(qT[:, h, :]), halves(qT[:, h, :]), misc[:, 2:4, 0:TH], ALU.mult), ret_ready)
                if h:
                    fill_lo(1, h - 1, qT[:, h - 1, :], 4)
            meet(dve, order, 1)

            def project_out(first):
                for i in range(4):
                    split_lo(first + i + 1)

            def ffn(layer):
                first = F0 if layer == 0 else F1
                for half in range(2):
                    for i in range(FH):
                        u, e = first + half * (FH + DC) + i, (2 * layer + half) * FH + i
                        U = up[e % 2]
                        for j in range(2):
                            w = rows_t[:, i, 32 * (2 * j + half):32 * (2 * j + half) + 32]
                            dve.wait_ge(tap0, 2 * e + j + 1)
                            order(dve.scalar_tensor_tensor(conv[:, j, :], U[:, j, 1:1 + CW], w[:, 17:18], conv[:, j, :], ALU.mult, ALU.add))
                            order.wait()
                            order(dve.scalar_tensor_tensor(conv[:, j, :], U[:, j, 2:2 + CW], w[:, 18:19], conv[:, j, :], ALU.mult, ALU.add), conv_done)
                            if j == 0:
                                split_lo(u + 1)
                        dve.wait_ge(conv_done, 2 * e + 2)
                        dve.wait_ge(gelu_done, e + 1)
                        if e:
                            dve.wait_ge(act_ready, e)
                        order(dve.tensor_tensor(gated[:, 0:NS].rearrange("p (b r) -> p b r", b=DB),
                                                conv[:, 0, 0:6 * DB].rearrange("p (b r) -> p b r", b=DB)[:, :, 0:4],
                                                conv[:, 1, 0:6 * DB].rearrange("p (b r) -> p b r", b=DB)[:, :, 0:4], ALU.mult))
                        order(dve.tensor_tensor(gated[:, NS:T], conv[:, 0, 48:CW], conv[:, 1, 48:CW], ALU.mult), gated_ready)
                        dve.wait_ge(act_hi, e + 1)
                        order(dve.tensor_tensor(aL[:, i, :], gated[:, :], aH[:, i, :].bitcast(F32), ALU.subtract), act_ready)
                    for m in range(DC):
                        u = first + half * (FH + DC) + FH + m
                        split_lo(u + 1)
                        if half:
                            c = FIRST_CHUNK[u]
                            dve.wait_ge(gemm_done, c + 1)
                            order(dve.tensor_tensor(halves(y[:, m, :]), halves(y[:, m, :]), gemm[c % 2][:, :, 0:TH], ALU.add), evacuated[c % 2])

            project_out(E_OUT)
            residual(1)
            norm_fill(2, 2)
            ffn(0)
            residual(3)
            norm_fill(4, 3)
            order.wait()
            meet(dve, order, 2)
            for n in range(11):
                u = O_IN + n
                split_lo(u + 1)
                what = UNITS[u][2]
                if what in (4, 6, 8, 0, 1, 2, 3):
                    last = FIRST_CHUNK[u + 1] - 1
                    dve.wait_ge(evacuated[last % 2], last // 2 + 1)
                    dve.wait_ge(o_in, ODD_LOADS)
                    if what < 4:
                        x = qN[:, :, (what // 2) * 512:(what // 2) * 512 + 512].rearrange("p t (r g d) -> p t r g d", r=R, g=2)[:, :, :, what % 2, :]
                    else:
                        x = kvN[:, :, (what - 4) * 256:(what - 3) * 256].rearrange("p t (g d) -> p t g d", g=G)
                    x1, x2 = x[:, :, :, 0:8], x[:, :, :, 8:16]
                    ta, tb, tc, td = (rt[:, z, :].rearrange("p (t h d) -> p t h d", t=NT, h=4) for z in range(4))
                    cos = cosO[:, :, :].unsqueeze(2).to_broadcast([P, NT, 4, 8])
                    sin = sinO[:, :, :].unsqueeze(2).to_broadcast([P, NT, 4, 8])
                    for dst, p1, p2 in ((ta, x1, cos), (tb, x2, sin), (tc, x2, cos), (td, x1, sin)):
                        order(dve.tensor_tensor(dst, p1, p2, ALU.mult))
                    order.wait()
                    order(dve.tensor_tensor(x1, ta, tb, ALU.subtract))
                    order(dve.tensor_tensor(x2, tc, td, ALU.add), o_ropes)
                    order.wait()
            dve.wait_ge(cp_done, 2)
            order(dve.memset(qS[:, :, :, :, :], 0.0))
            dve.wait_ge(qs_turned, 1)
            order.wait()
            for j in range(2):
                for g2 in range(2):
                    half = slice(64 * g2, 64 * g2 + 64)
                    order(dve.tensor_copy(qS[half, :, j, g2, 0:16].rearrange("p b (r n) -> p r b n", r=R),
                                          b6[half, j * P:(j + 1) * P].rearrange("p (r b n) -> p r b n", r=R, b=DB)))
            meet(dve, order, 3)

            def mask(n):
                _, qt, _, _, _ = attention_unit(n)
                keys = (qt + 1) * P
                dve.wait_ge(s_done, n + 1)
                if n >= 2:
                    dve.wait_ge(exped, n - 1)
                order(dve.tensor_tensor_reduce(sm[:, n % 2, 0:keys], gemm[0][:, n % 2, 0:keys], causal[:, SEQ - keys:SEQ], -SCALE, BIG,
                                               ALU.add, ALU.min, negmax[:, n % 2:n % 2 + 1]), masked)
                if n % 8 == 0:
                    grp = n // 8
                    dve.wait_ge(c_scored, grp + 1)
                    if grp:
                        dve.wait_ge(c_turned, grp)
                    order(dve.tensor_tensor(cs[:, :, :], b6[:, 0:R * NCP].rearrange("p (r m) -> p r m", r=R),
                                            cmask[:, qt, :].unsqueeze(1).to_broadcast([P, R, NCP]), ALU.add))
                    order.wait()
                    order(dve.tensor_reduce(cmx[:, :], cs[:, :, :], AX_X, ALU.max))
                    order.wait()
                    order(dve.tensor_tensor(cs[:, :, :], cs[:, :, :], cmx[:, :].unsqueeze(2).to_broadcast([P, R, NCP]), ALU.subtract), c_sub)

            def scale(n):
                j, qt, g2, r, br = attention_unit(n)
                g = 2 * j + g2
                keys = (qt + 1) * P
                dve.wait_ge(exped, n + 1)
                order(dve.reciprocal(rscale[:, n % 2:n % 2 + 1], rsum[:, n % 2:n % 2 + 1]))
                order.wait()
                gate = gN[:, qt + 1, (br + 1) * 16 + g * R + r:(br + 1) * 16 + g * R + r + 1]
                order(dve.tensor_scalar(pr[:, n % 2, 0:keys], pr[:, n % 2, 0:keys], rscale[:, n % 2:n % 2 + 1], gate, ALU.mult, ALU.mult), scaled)
                if n % 8 == 0:
                    dve.wait_ge(c_exped, n // 8 + 1)
                    order(dve.tensor_reduce(crs[:, 0, :], cs[:, :, :], AX_X, ALU.add))
                    order.wait()
                    order(dve.tensor_tensor(cs[:, :, :], cs[:, :, :], cvalid[:, qt, :].unsqueeze(1).to_broadcast([P, R, NCP]), ALU.mult))
                    order(dve.reciprocal(crs[:, 1, :], crs[:, 0, :]))
                    order.wait()
                    order(dve.tensor_tensor(crs[:, 0, :], crs[:, 1, :], gN[:, qt + 1, g * R:(g + 1) * R], ALU.mult))
                    order.wait()
                    order(dve.tensor_tensor(cs[:, :, :], cs[:, :, :], crs[:, 0, :].unsqueeze(2).to_broadcast([P, R, NCP]), ALU.mult), c_ready)

            def take_probs(n):
                _, qt, _, _, _ = attention_unit(n)
                keys = (qt + 1) * P
                if n % 2:
                    dve.wait_ge(p_turned, n + 1)
                    if n >= 2:
                        dve.wait_ge(v_done, n - 1)
                    order(dve.tensor_copy(pT[:, 1, 0:keys], gemm[1][:, 1, 0:keys]), p_ev[1])

            def heads_lo(grp):
                j, qt, g2, _, _ = attention_unit(8 * grp)
                dve.wait_ge(o_hi, grp + 1)
                c0 = 2 * (2 * j + g2)
                cols = slice(NS + qt * P, NS + (qt + 1) * P)
                order(dve.tensor_tensor(hL[:, c0:c0 + 2, cols], misc[:, grp % 2, 0:2 * P].rearrange("p (c q) -> p c q", c=2),
                                        hH[:, c0:c0 + 2, cols].bitcast(F32), ALU.subtract), o_lo)

            dve.wait_ge(b_in, BIN_LOADS)
            for j in range(2):
                for n in range(64 * j, 64 * j + 67):
                    if n >= 64 * j + 3:
                        take_probs(n - 3)
                    if n < 64 * j + 64:
                        mask(n)
                    if 64 * j + 1 <= n < 64 * j + 65:
                        scale(n - 1)
                    if n >= 64 * j + 3:
                        if (n - 3) % 8 == 1 and n - 3 > 64 * j + 8:
                            heads_lo((n - 3) // 8 - 1)
                heads_lo(8 * j + 7)
            meet(dve, order, 4)

            dve.wait_ge(z_scored, 1)
            cpsum = gemm[0][:, 0, 0:DB * NCS].rearrange("p (b m) -> p b m", b=DB)
            order(dve.tensor_reduce(csm[:, :], cpsum, AX_X, ALU.max))
            order.wait()
            order(dve.tensor_tensor(css[:, :, :], cpsum, csm[:, :].unsqueeze(2).to_broadcast([P, DB, NCS]), ALU.subtract), z_sub)
            dve.wait_ge(z_exped, 1)
            order(dve.tensor_reduce(rss[:, :, 2], css[:, :, :], AX_X, ALU.add))
            order.wait()
            order(dve.reciprocal(rsc[:, :, 2], rss[:, :, 2]))
            order.wait()
            dve.wait_ge(gs_in, GS_LOADS)
            order(dve.tensor_tensor(rsc[:, :, 2], rsc[:, :, 2], gS[:, :, 0], ALU.mult))
            order.wait()
            order(dve.tensor_tensor(css[:, :, :], css[:, :, :], rsc[:, :, 2].unsqueeze(2).to_broadcast([P, DB, NCS]), ALU.mult))
            order.wait()
            for j in range(2):
                order(dve.tensor_tensor(cpb[:, :, j, :], css[:, :, :], pair_of[:, j, :].unsqueeze(1).to_broadcast([P, DB, NCS]), ALU.mult),
                      z_ready if j else None)
            for b in range(DB):
                for br in range(2):
                    n = 2 * b + br
                    dve.wait_ge(ss_done, n + 1)
                    dve.wait_ge(m_set, b + 1)
                    if b >= 2:
                        dve.wait_ge(s_exped, n - 3)
                    order(dve.tensor_tensor_reduce(sms[:, b % 2, br, :], gemm[0][:, br, 0:KW], mask_s[:, b % 2, :], -SCALE, BIG, ALU.add, ALU.min,
                                                   nms[:, b, br:br + 1]), s_masked)
                for br in range(2):
                    n = 2 * b + br
                    dve.wait_ge(s_exped, n + 1)
                    order(dve.reciprocal(rsc[:, b, br:br + 1], rss[:, b, br:br + 1]))
                    order.wait()
                    order(dve.tensor_scalar(prs[:, b % 2, br, :], prs[:, b % 2, br, :], rsc[:, b, br:br + 1], gS[:, b, br + 1:br + 2], ALU.mult, ALU.mult), s_scaled)
            for z in range(8):
                dve.wait_ge(o_hi, 16 + 8)
                dst, src = sample_heads(z)
                order(dve.tensor_tensor(dst(hL), src, dst(hH).bitcast(F32), ALU.subtract), o_lo)
            meet(dve, order, 5)
            project_out(O_OUT)
            residual(5)
            norm_fill(6, 4)
            ffn(1)
            residual(7)

        @block.gpsimd
        def _(pool):
            order = Order(pool, pool_c)
            order(pool.memset(mean_d[:, :], 1.0 / D), consts)
            order(pool.memset(mean_k[:, :], 1.0 / DK), consts)
            order(pool.memset(eps[:, :], EPS), consts)
            for dst, src in ((spread[:, :, :], a["spread"].rearrange("p (q m) -> p q m", q=4)),
                             (gin[0:2, :], a["norm_mix_pre"]), (gin[2:4, :], a["norm_mix_post"]),
                             (gin[4:6, :], a["norm_ffn_pre"]), (gin[6:8, :], a["norm_ffn_post"])):
                pool.dma_start(dst, src).then_inc(loads, 16)
            order(pool.memset(pool_mark[:, :], 0.0), phase)
            for dst, src in ((decay[:, :, :], by4(a["decay"])), (decs[:, :, :], by4(a["decay_s"])),
                             (qdec[:, :, :], by4(a["qdecay"].to_broadcast([P, 4 * P]))), (qdecs[:, :, :], by4(a["qdecay_s"].to_broadcast([P, 4 * NS]))),
                             (kdec[:, :], a["kdecay"]), (batch_of[:, :], a["batch_of"]), (same_s[:, :], a["same_s"]), (row_of_s[:, :], a["row_of_s"]),
                             (tril[:, :], a["tril_t"]), (cosE[:, :], a["cos_even"]), (sinE[:, :], a["sin_even"]),
                             (sgw[:, :, :], a["e_sg_w"][0].rearrange("g i j -> i g j")),
                             (sgb[:, :, :], by4(a["e_sg_b"].rearrange("n g i -> n (g i)").to_broadcast([P, 4 * P]))),
                             (lng[:, :], a["e_sg_ln_g"].to_broadcast([P, 512])), (lnb[:, :], a["e_sg_ln_b"].to_broadcast([P, 512]))):
                pool.dma_start(dst, src).then_inc(e_in, 16)

            def load_s0(h):
                pool.dma_start(s0[:, :, h % 2, :], a["state_ret"][0, :, h].rearrange("b d v -> d b v")).then_inc(s0_in[h % 2], 16)

            load_s0(0)
            load_s0(1)
            pool.wait_ge(svn_ready, 1)
            pool.dma_start(o["sg_v_sample"][0].rearrange("b s w -> (b s) w"), svn[0:NS, 0, :]).then_inc(e_out, 16)
            for h in range(RH):
                pool.wait_ge(s0_ready, h + 1)
                pool.dma_start(o["ret_state_sample"][0, :, h].rearrange("b d v -> d b v"), s0[:, :, h % 2, :]).then_inc(s0_out, 16)
                if h == RH - 1:
                    pool.wait_ge(st_ready, 4)
                    pool.dma_start(o["ret_state_prompt"][0, 0].rearrange("h d v -> d h v"), st[:, :, :]).then_inc(e_out, 16)
                pool.wait_ge(s0_out, 16 * (h + 1))
                if h + 2 < RH:
                    load_s0(h + 2)
            pool.wait_ge(e_out, 32)
            meet(pool, order, 1)

            def load_page(n):
                if n >= 4:
                    pool.wait_ge(page_turned, n - 3)
                page = pool.value_load(a["page_table"][n // NPG:n // NPG + 1, n % NPG:n % NPG + 1], min_val=0, max_val=N_POOL - 1)
                pool.dma_start(pages[:, n % 4, :], a["cache_cmp"][0, page].rearrange("t z g d -> t (z g d)")).then_inc(page_in[n % 4], 16)

            for n in range(4):
                load_page(n)
            for z in range(2):
                for g in range(2):
                    pool.dma_start(pe_in[:, z, 64 * g:64 * g + 64], a[("o_pe_k", "o_pe_v")[z]][0]).then_inc(pe_in_land, 16)
            order(pool.memset(cT[:, :, 2 * DB, :], 0.0), pe_clear)
            for phi in (phiK, phiV):
                order(pool.memset(phi[:, :, :], 0.0), phi_clear)
            for n in range(4, DB * NPG):
                load_page(n)
            pool.wait_ge(page_turned, DB * NPG)

            def load_ffn_rows(layer):
                for q in range(4):
                    cols = slice(q * FH * P, (q + 1) * FH * P)
                    pool.dma_start(rows_in[32 * q:32 * q + 16, :], a["state_ffn"][layer].rearrange("b r f -> (b r) f")[:, cols]).then_inc(rows_land, 16)
                    pool.dma_start(rows_in[32 * q + 16:32 * q + 19, :], a["f_conv_w"][layer][:, cols]).then_inc(rows_land, 16)
                    pool.dma_start(rows_in[32 * q + 19:32 * q + 20, :], a["f_conv_b"][layer:layer + 1, cols]).then_inc(rows_land, 16)

            def ffn(layer):
                order(pool.memset(rows_in[:, :], 0.0))
                if layer == 0:
                    order.wait()
                    load_ffn_rows(layer)
                    pool.wait_ge(cmp_ev, 2)
                for s in range(2):
                    order(pool.memset(up[s][:, :, 48:50], 0.0))
                order(pool.memset(tail[:, :, :], 0.0))
                order.wait()
                if layer:
                    load_ffn_rows(layer)
                pool.wait_ge(rows_ev, 3 * (layer + 1))
                first = F0 if layer == 0 else F1
                for half in range(2):
                    for i in range(FH):
                        e = (2 * layer + half) * FH + i
                        U = up[e % 2]
                        if e >= 2:
                            pool.wait_ge(conv_done, 2 * e - 2)
                        for j in range(2):
                            q = 2 * j + half
                            order(pool.tensor_copy(U[:, j, 0:6 * DB].rearrange("p (b r) -> p b r", b=DB)[:, :, 0:2],
                                                   rows_t[:, i, 32 * q:32 * q + 16].rearrange("p (b r) -> p b r", b=DB)), prev_set if j else None)
                        if e >= 2:
                            pool.wait_ge(tail_turned, e - 1)
                        for j in range(2):
                            c = FIRST_CHUNK[first + half * (FH + DC) + i] + j
                            pool.wait_ge(evacuated[c % 2], c // 2 + 1)
                            order(pool.tensor_copy(tail[:, e % 2, 32 * j:32 * j + 2], U[:, j, UW - 2:UW]))
                            order(pool.tensor_copy(tail[:, e % 2, 32 * j + 2:32 * j + 18].rearrange("p (b r) -> p b r", b=DB),
                                                   U[:, j, 0:6 * DB].rearrange("p (b r) -> p b r", b=DB)[:, :, 4:6]), tail_set if j else None)
                    pool.wait_ge(tail_ev, e + 1)
                    for j in range(2):
                        cols = slice(j * FF + half * FH * P, j * FF + (half + 1) * FH * P)
                        pool.dma_start(o["ffn_prompt"][layer, 0][:, cols], rows_out[32 * j:32 * j + 2, :]).then_inc(rows_stored, 16)
                        pool.dma_start(o["ffn_sample"][layer].rearrange("b r f -> (b r) f")[:, cols], rows_out[32 * j + 2:32 * j + 18, :]).then_inc(rows_stored, 16)

            ffn(0)
            pool.wait_ge(rows_stored, 128)
            meet(pool, order, 2)
            for dst, src in ((cosO[:, :, :], a["cos_odd"].rearrange("p (t d) -> p t d", t=NT)),
                             (sinO[:, :, :], a["sin_odd"].rearrange("p (t d) -> p t d", t=NT))):
                pool.dma_start(dst, src).then_inc(o_in, 16)
            for phi in (phiK2, phiV2):
                order(pool.memset(phi[:, :, :], 0.0))
            order.wait()
            for phi, name in ((phiK2, "o_phi_k"), (phiV2, "o_phi_v")):
                for g in range(2):
                    pool.dma_start(phi[64 * g:64 * g + 64, :, 64 * g:64 * g + 64], a[name][0].rearrange("l d e -> d l e")).then_inc(o_in, 16)
            win_out = o["win_sample"][0].rearrange("b s z g d -> b s (z g d)")
            pool.dma_start(win_out[:, 0:PAST, :], a["state_win"][0].rearrange("b s z g d -> b s (z g d)")).then_inc(rows_out_done, 16)
            pool.wait_ge(o_ropes, 7)
            for br, name in enumerate(("cmp_rows", "sel_rows", "win")):
                dst = o[f"{name}_prompt"][0, 0].rearrange("(t p) z g d -> p t (z g d)", p=P)
                pool.dma_start(dst, kvN[:, 1:NT, 512 * br:512 * br + 512]).then_inc(rows_out_done, 16)
                if br < 2:
                    dst = o[f"{name}_sample"][0].rearrange("b s z g d -> (b s) (z g d)")
                    pool.dma_start(dst, kvN[0:NS, 0, 512 * br:512 * br + 512]).then_inc(rows_out_done, 16)
                else:
                    for b in range(DB):
                        pool.dma_start(win_out[b, PAST:KS, :], kvN[DS * b:DS * (b + 1), 0, 512 * br:512 * br + 512]).then_inc(rows_out_done, 16)
            last = FIRST_CHUNK[O_IN + 11] - 1
            for c in (last - 4,):
                pool.wait_ge(evacuated[c % 2], c // 2 + 1)
            pool.wait_ge(evacuated[last % 2], last // 2 + 1)
            for e in range(3):
                pool.dma_start(scratch[:, :, e], gN[0:NS, 0, 16 * e:16 * e + 16], allow_slow_non_contiguous=True).then_inc(gates_out, 16)
            meet(pool, order, 3)
            for dst, src in ((causal[:, :], a["causal"]), (cmask[:, :, :], by4(a["cmp_mask"])), (cvalid[:, :, :], by4(a["cmp_valid"]))):
                pool.dma_start(dst, src).then_inc(b_in, 16)
            pool.wait_ge(gates_out, 48)
            order(pool.memset(gS[:, :, :], 0.0))
            order(pool.memset(mask_s[:, :, :], 0.0))
            order.wait()
            for g in range(G):
                for r in range(R):
                    at = 32 * g + DS * r
                    pool.dma_start(gS[at:at + DS, :, :], scratch.rearrange("(b n) h e -> n h b e", b=DB)[:, g * R + r, :, :]).then_inc(gs_in, 16)
            for dst, src in ((mask_new[:, :, :], a["mask_new"].rearrange("p (b m) -> p b m", b=DB)),
                             (pair_of[:, :, :], a["pair_of"].rearrange("p (j m) -> p j m", j=2))):
                pool.dma_start(dst, src).then_inc(gs_in, 16)
            pool.wait_ge(gs_in, GS_LOADS)

            def load_rows(b):
                for pg in range(NPG):
                    page = pool.value_load(a["page_table"][b:b + 1, pg:pg + 1], min_val=0, max_val=N_POOL - 1)
                    pool.dma_start(row_slot[b % 4][:, 0, pg, :], a["cache_sel"][0, page].rearrange("t z g d -> t (z g d)")).then_inc(row_in[b % 4], 16)
                pool.dma_start(row_slot[b % 4][:, 1, :, :], a["state_win"][0, b].rearrange("(q t) z g d -> t q (z g d)", q=NPG)).then_inc(row_in[b % 4], 16)

            pool.wait_ge(qk_ev, 12)
            for b in range(2):
                load_rows(b)
            pool.wait_ge(rows_out_done, ROWS_OUT)
            pool.wait_ge(b_in, BIN_LOADS)
            meet(pool, order, 4)
            for b in range(DB):
                if b >= 2:
                    pool.wait_ge(s_masked, 2 * (b - 1))
                order(pool.tensor_copy(mask_s[:, b % 2, PAST:KW], mask_new[:, b, :]), m_set)
                if b + 2 < DB:
                    if b >= 2:
                        pool.wait_ge(os_done, b - 1)
                    load_rows(b + 2)
            meet(pool, order, 5)
            ffn(1)
            pool.wait_ge(out_ev, 2 * DC)
            pool.dma_start(o["y_sample"].rearrange("b s d -> (b s) d"), yout[0:NS, 0, :]).then_inc(out_stored, 16)
            pool.dma_start(o["y_prompt"][0].rearrange("(t p) d -> p t d", p=P), yout[:, 1:NT, :]).then_inc(out_stored, 16)
            pool.wait_ge(out_stored, 32)
            pool.wait_ge(rows_stored, 64 * N_FFN_HALVES)


LOADS = 16 * 5
PHI_LOADS = 16 * 4
E_LOADS = 16 * 15
ROWS_LAND = 16 * 12
N_POOL = (DB * NPG * 5 + 3) // 4
ODD_LOADS = 16 * 6
BIN_LOADS = 16 * 3
ROWS_OUT = 16 * (1 + 3 + 2 + DB)
GS_LOADS = 16 * (G * R + 2)
LAST_UNIT = len(UNITS)
FINAL_POST = 3
N_FFN_HALVES = 4

OUTPUTS = (
    ("y_prompt", (1, SEQ, D)), ("y_sample", (DB, DS, D)),
    ("ret_state_prompt", (1, 1, RH, DK, DK)), ("ret_state_sample", (1, DB, RH, DK, DK)),
    ("sg_v_sample", (1, DB, DS, 512)),
    ("cmp_rows_prompt", (1, 1, SEQ, 2, G, HD)), ("cmp_rows_sample", (1, DB, DS, 2, G, HD)),
    ("sel_rows_prompt", (1, 1, SEQ, 2, G, HD)), ("sel_rows_sample", (1, DB, DS, 2, G, HD)),
    ("win_prompt", (1, 1, SEQ, 2, G, HD)), ("win_sample", (1, DB, KS, 2, G, HD)),
    ("ffn_prompt", (2, 1, 2, 2 * FF)), ("ffn_sample", (2, DB, 2, 2 * FF)),
)


def kernel(**inputs):
    import concourse.bacc as bacc
    from concourse.bass_utils import run_bass_kernel_spmd

    nc = bacc.Bacc("TRN2", target_bir_lowering=False, num_devices=1)
    arrays, a, o = {}, {}, {}
    for name, value in {**inputs, **CONSTANTS}.items():
        value = np.ascontiguousarray(value)
        arrays[f"in_{name}"] = value
        a[name] = nc.dram_tensor(f"in_{name}", value.shape, mybir.dt.from_np(value.dtype), kind="ExternalInput").ap()
    for name, shape in OUTPUTS:
        o[name] = nc.dram_tensor(f"out_{name}", shape, F32, kind="ExternalOutput").ap()
    build_program(nc, a, o)
    r = run_bass_kernel_spmd(nc, [arrays], core_ids=[0])
    return tuple(r.results[0][f"out_{name}"] for name, _ in OUTPUTS)
```

```python
from contextlib import ExitStack

import numpy as np

import concourse.bass as bass
from concourse import mybir

F32 = mybir.dt.float32
F32R = mybir.dt.float32r
ALU = mybir.AluOpType
ACT = mybir.ActivationFunctionType
AX_X = mybir.AxisListType.X

P = 128
D = 1024
DC = D // P
SEQ, DB, DS = 512, 8, 4
NS = DB * DS
T = NS + SEQ
TH = T // 2
TQ = T // 4
NT = 1 + SEQ // P
RH, DK = 4, 128
FF = 2816
FH = FF // P // 2
G, R, HD = 4, 4, 64
PAST, PAGE = 256, 128
NPG = PAST // PAGE
KS = PAST + DS
KW = PAST + NS
NCP = (SEQ - 32) // 16 + 1
NCS = (PAST + DS - 32) // 16 + 1
CL = 32
NBLK = (2 * DB + 1) * NCS
EPS = 1e-6
SCALE = HD ** -0.5
NEG = -1e30
BIG = 3e38
UNIT = 2048
THETA_E = 1.0 / (10000.0 ** np.linspace(0.0, 1.0, DK // 2))
THETA_O = 1.0 / (500000.0 ** (np.arange(0, 16, 2) / 16.0))
GAMMA = 1.0 - 2.0 ** (-5.0 - np.arange(RH))


def tile_start(t):
    return 0 if t == 0 else NS + P * (t - 1)


def shape_constants():
    pos = np.concatenate([np.tile(PAST + np.arange(DS), DB), np.arange(SEQ)]).astype(np.float64)
    ang = THETA_E[:, None] * pos[None, :]
    c = {}
    c["cos_even"] = np.concatenate([np.cos(ang), np.cos(ang)], 0)
    c["sin_even"] = np.concatenate([-np.sin(ang), np.sin(ang)], 0)
    co, so = np.zeros((P, NT, 8)), np.zeros((P, NT, 8))
    for t in range(NT):
        a = pos[tile_start(t):tile_start(t) + P, None] * THETA_O[None, :]
        co[:, t], so[:, t] = np.cos(a), np.sin(a)
    c["cos_odd"], c["sin_odd"] = co.reshape(P, -1), so.reshape(P, -1)
    i = np.arange(P)
    diff = i[None, :] - i[:, None]
    dm = np.zeros((P, RH, P))
    for h in range(RH):
        dm[:, h] = np.where(diff >= 0, GAMMA[h] ** np.maximum(diff, 0), 0)
    c["decay"] = dm.reshape(P, -1)
    s = np.arange(NS)
    ds = np.zeros((NS, RH, NS))
    same = (s[:, None] // DS) == (s[None, :] // DS)
    for h in range(RH):
        d = (s % DS)[None, :] - (s % DS)[:, None]
        ds[:, h] = np.where(same & (d >= 0), GAMMA[h] ** np.maximum(d, 0), 0)
    c["decay_s"] = ds.reshape(NS, -1)
    c["qdecay"] = np.stack([GAMMA[h] ** (i + 1.0) for h in range(RH)]).reshape(1, -1)
    c["qdecay_s"] = np.stack([GAMMA[h] ** (s % DS + 1.0) for h in range(RH)]).reshape(1, -1)
    c["kdecay"] = np.concatenate([np.stack([GAMMA[h] ** (P - 1.0 - i) for h in range(RH)], 1),
                                  np.stack([GAMMA[h] ** (DS - 1.0 - i % DS) for h in range(RH)], 1)], 1)
    c["tril_t"] = (diff >= 0).astype(np.float64)
    c["same_s"] = same.astype(np.float64)
    c["row_of_s"] = (np.arange(DS)[:, None] == (s % DS)[None, :]).astype(np.float64)
    c["batch_of"] = (s[:, None] // DS == np.arange(DB)[None, :]).astype(np.float64)
    c["ident"] = np.eye(P)
    sel = np.zeros((P, 4, P))
    for q in range(4):
        sel[32 * q, q] = 1
    c["spread"] = sel.reshape(P, -1)
    x = np.arange(SEQ)
    c["causal"] = np.where(x[None, :] - (SEQ - P) <= i[:, None], 0, NEG)
    cm, cv = np.zeros((P, 4, NCP)), np.zeros((P, 4, NCP))
    for t in range(4):
        ok = (np.arange(NCP) * 16 + 31)[None, :] <= (P * t + i)[:, None]
        cm[:, t], cv[:, t] = np.where(ok, 0, NEG), ok
    c["cmp_mask"], c["cmp_valid"] = cm.reshape(P, -1), cv.reshape(P, -1)
    n = i % 4
    new = np.full((P, DB, DB, DS), NEG)
    for b in range(DB):
        new[:, b, b, :] = np.where(np.arange(DS)[None, :] <= n[:, None], 0, NEG)
    c["mask_new"] = new.reshape(P, -1)
    pj = np.zeros((P, 2, NCS))
    for j in range(2):
        pj[:, j] = ((i // 64) == j)[:, None]
    c["pair_of"] = pj.reshape(P, -1)
    return {k: np.ascontiguousarray(v, dtype=np.float32) for k, v in c.items()}


CONSTANTS = shape_constants()


def unit_plan():
    units = []
    for n in (10, 11, 4, 5, 0, 1, 2, 3, 8, 9, 6, 7):
        units.append(("even_in", 0, n, 5 if n in (4, 5, 10, 11) else 2))
    units += [("even_out", 0, n, 2) for n in range(4)]

    def ffn(layer):
        for half in range(2):
            for i in range(FH):
                units.append(("ffn_in", layer, (half, i), 2))
            for m in range(DC):
                units.append(("ffn_out", layer, (half, m), 1))

    ffn(0)
    units.extend(("odd_in", 0, n, 1 if n == 10 else 5) for n in (4, 5, 6, 7, 8, 9, 0, 1, 2, 3, 10))
    units.extend(("odd_out", 0, n, 2) for n in range(4))
    ffn(1)
    return units


UNITS = unit_plan()
FIRST_CHUNK = [sum(u[3] for u in UNITS[:n]) for n in range(len(UNITS) + 1)]
E_IN, E_OUT, F0 = 0, 12, 16
FFN_UNITS = 2 * (FH + DC)
O_IN = F0 + FFN_UNITS
O_OUT = O_IN + 11
F1 = O_OUT + 4


class Order:

    def __init__(self, eng, chain):
        self.eng, self.chain, self.count, self.last = eng, chain, {}, None

    def __call__(self, ins, sem=None):
        sem = self.chain if sem is None else sem
        self.count[id(sem)] = self.count.get(id(sem), 0) + 1
        ins.then_inc(sem, 1)
        self.last = (sem, self.count[id(sem)])

    def wait(self):
        self.eng.wait_ge(*self.last)


def build_program(nc, a, o):
    with ExitStack() as ctx:
        sems = {}

        def sem(name):
            if name not in sems:
                sems[name] = ctx.enter_context(nc.semaphore(name))
            return sems[name]

        place = {"at": 16512}

        def sb(name, shape, dt=F32, at=None):
            size = int(np.prod(shape[1:])) * 4
            size = (size + 31) // 32 * 32
            off = place["at"] if at is None else at
            assert off + size <= nc.sbuf_usable_end, (name, off, size)
            t = nc.alloc_sbuf_tensor_at(name, shape, dt, offset=off)
            if at is None:
                place["at"] = off + size
            return t

        xT = sb("xT", [P, DC, T])
        hH, hL = sb("hH", [P, DC, T], F32R), sb("hL", [P, DC, T], F32R)
        raw = sb("raw", [P, 2, UNIT])
        wH, wL = sb("wH", [P, 2, UNIT], F32R), sb("wL", [P, 2, UNIT], F32R)
        ident = sb("ident_sb", [P, P])
        spread = sb("spread_sb", [P, 4, P])
        mean_d, mean_k = sb("mean_d", [P, 32]), sb("mean_k", [P, 32])
        eps, pool_mark = sb("eps", [P, 1]), sb("pool_mark", [1, 1])
        gains = sb("gains", [P, DC, 8])
        kcs = sb("kcs", [P, DB, 2, NCS])
        vcs = sb("vcs", [2 * NCS, DB, P])
        pe_bias = sb("pe_bias", [P, 2])
        rq, rr = sb("rq", [P, TQ]), sb("rr", [P, TQ])
        R0 = place["at"]

        y = sb("y", [P, DC, T])
        aH, aL = sb("aH", [P, FH, T], F32R), sb("aL", [P, FH, T], F32R)
        UW = DB * 6 + 2 + SEQ
        CW = UW - 2
        up = [sb("up0", [P, 2, UW]), sb("up1", [P, 2, UW])]
        conv = sb("conv", [P, 2, CW])
        gated = sb("gated", [P, T])
        top = nc.sbuf_usable_end // 32 * 32
        rows_in = sb("rows_in", [P, FH * P], at=top - FH * P * 4)
        rows_t = sb("rows_t", [P, FH, P], at=top - 2 * FH * P * 4)
        vct = sb("vct", [P, DB, 2, NCS], at=top - 2 * FH * P * 4 - DB * 2 * NCS * 4)
        rows_out = sb("rows_out", [64, FH * P])
        tail = sb("tail", [P, 2, 64])
        sqf = [conv[:, 0, 0:T], conv[:, 1, 0:T]]
        sqm_t = sb("sqm", [P, 2, T], at=R0 + DC * T * 4)
        sqm = [sqm_t[:, 0, :], sqm_t[:, 1, :]]

        place["at"] = R0
        qT, kT = sb("qT", [P, RH, T]), sb("kT", [P, RH, T])
        vN, svn = sb("vN", [P, NT, 512]), sb("svn", [P, NT, 512])
        silu_g, uT = sb("silu_g", [P, RH, T]), sb("uT", [P, RH, T])
        kN, qd, st = sb("kN", [P, RH, P]), sb("qd", [P, RH, P]), sb("st", [P, RH, P])
        decay, inner = sb("decay_sb", [P, RH, P]), sb("inner", [P, RH, P])
        sgb, wmT, sgw = sb("sgb", [P, 4, P]), sb("wmT", [P, 4, P]), sb("sgw", [P, 4, P])
        wmS = sb("wmS", [NS, 4, NS])
        cosE = sb("cosE", [P, T])
        sin_at = place["at"]
        sinE, swp = sb("sinE", [P, T]), sb("swp", [P, T])
        qdec, qdecs = sb("qdec", [P, RH, P]), sb("qdecs", [P, RH, NS])
        kdec, batch_of = sb("kdec", [P, 8]), sb("batch_of_sb", [NS, DB])
        decs, same_s, row_of_s = sb("decs", [NS, RH, NS]), sb("same_sb", [NS, NS]), sb("row_sb", [4, NS])
        lnt_at = place["at"]
        lnt, lng, lnb = sb("lnt", [P, 512]), sb("lng", [P, 512]), sb("lnb", [P, 512])
        tril = sb("tril", [P, P])
        lns = sb("lns", [P, 4, NT * 4])
        vB = sb("vB", [NS, DB, P])
        s0 = sb("s0", [P, DB, 2, P])
        place["at"] = lnt_at
        kNs = sb("kNs", [NS, RH, P])
        place["at"] = sin_at
        qds, inner_s = sb("qds", [P, RH, NS]), sb("inner_s", [NS, RH, NS])
        hsqs = [swp, cosE]

        place["at"] = R0
        xin = sb("xin", [P, NT, D])
        gin = sb("gin", [8, D])
        sqx_t = sb("sqx", [P, 2, T])
        sqx = [sqx_t[:, 0, :], sqx_t[:, 1, :]]
        place["at"] = R0 + (DC + 2) * T * 4
        phiK, phiV = sb("phiK", [P, CL, P]), sb("phiV", [P, CL, P])
        cT = sb("cT", [P, 2, 2 * DB + 1, PAST])
        pages = sb("pages", [P, 4, 512], at=top - 2 * FH * P * 4)
        pe_in = sb("pe_in", [CL, 2, P], at=top - 2 * FH * P * 4 + 8192)
        assert place["at"] <= top - 2 * FH * P * 4 - DB * 2 * NCS * 4

        place["at"] = R0
        qN, kvN, gN = sb("qN", [P, NT, D]), sb("kvN", [P, NT, 3 * 512]), sb("gN", [P, NT, 48])
        cosO, sinO, rt = sb("cosO", [P, NT, 8]), sb("sinO", [P, NT, 8]), sb("rt", [P, 4, NT * 32])
        kcP, vcP, vcPt = sb("kcP", [P, 2, NCP]), sb("vcP", [NCP, 2, P]), sb("vcPt", [P, 2, NCP])
        O1 = place["at"]
        phiK2, phiV2 = sb("phiK2", [P, CL, P]), sb("phiV2", [P, CL, P])
        cPT = sb("cPT", [P, 4, SEQ])
        gT = sb("gT", [48, T], at=O1)
        place["at"] = O1
        qTj, ksT, kwT = sb("qTj", [P, R, SEQ]), sb("ksT", [P, 2, SEQ]), sb("kwT", [P, 2, SEQ])
        sm, pr, pT = sb("sm", [P, 2, SEQ]), sb("pr", [P, 2, SEQ]), sb("pT", [P, 2, SEQ])
        causal = sb("causal_sb", [P, SEQ])
        cmask, cvalid = sb("cmask", [P, 4, NCP]), sb("cvalid", [P, 4, NCP])
        cs, cmx, cpT = sb("cs", [P, R, NCP]), sb("cmx", [P, R]), sb("cpT", [NCP, R, P])
        negmax, rsum, rscale = sb("negmax", [P, 2]), sb("rsum", [P, 2]), sb("rscale", [P, 2])
        crs = sb("crs", [P, 2, R])
        
        qS = sb("qS", [P, DB, 2, 2, 32])
        gS, mask_new, pair_of = sb("gS", [P, DB, 3]), sb("mask_new_sb", [P, DB, NS]), sb("pair_of_sb", [P, 2, NCS])
        mask_s = sb("mask_s", [P, 2, KW])
        rows0 = sb("rows0", [P, 2, 2, NPG, 512], at=R0)
        rows1 = sb("rows1", [P, 2, 2, NPG, 512], at=R0 + (NT * D + 1536) * 4)
        row_slot = [rows0[:, 0], rows0[:, 1], rows1[:, 0], rows1[:, 1]]
        place["at"] = O1
        kTs = sb("kTs", [P, 2, 2, 2, KW])
        sms, prs, pTs = sb("sms", [P, 2, 2, KW]), sb("prs", [P, 2, 2, KW]), sb("pTs", [P, 2, 3, P])
        css, csm, cpb = sb("css", [P, DB, NCS]), sb("csm", [P, DB]), sb("cpb", [P, DB, 2, NCS])
        cpTs = sb("cpTs", [2 * NCS, DB, P])
        nms, rss, rsc = sb("nms", [P, DB, 2]), sb("rss", [P, DB, 3]), sb("rsc", [P, DB, 3])
        yout = sb("yout", [P, NT, D], at=R0 + DC * T * 4 + 64)

        gemm = [ctx.enter_context(nc.psum_tensor(f"gemm{n}", [P, 2, 512], F32)) for n in range(2)]
        misc = ctx.enter_context(nc.psum_tensor("misc", [P, 4, 512], F32))
        b4, b5, b6, b7 = (misc[:, n, :] for n in range(4))
        scratch = nc.dram_tensor("gate_scratch", (NS, 16, 3), F32).ap()

        def halves(ap):
            return ap.rearrange("p (a b) -> p a b", a=2)

        def by4(ap):
            return ap.rearrange("p (a b) -> p a b", a=4)


        raw_ready = [sem("raw_ready0"), sem("raw_ready1")]
        hi_ready, lo_ready = sem("hi_ready"), sem("lo_ready")
        gemm_done = sem("gemm_done")
        evacuated = [sem("evacuated0"), sem("evacuated1")]
        phase = sem("phase")
        h_hi, h_ready, ht_ready = sem("h_hi"), sem("h_ready"), sem("ht_ready")
        sq_ready, sq_used = sem("sq_ready"), sem("sq_used")
        root_ready, rec_ready, rstd_ready = sem("root_ready"), sem("rec_ready"), sem("rstd_ready")
        x_ready, y_scaled = sem("x_ready"), sem("y_scaled")
        pe_c, act_c, dve_c, pool_c = sem("pe_chain"), sem("act_chain"), sem("dve_chain"), sem("pool_chain")
        loads, x_in = sem("first_loads"), sem("x_in")
        consts = sem("consts_set")
        xt_turned, xt_ready, gain_ready = sem("xt_turned"), sem("xt_ready"), sem("gain_ready")
        phi_in, page_in = sem("phi_in"), [sem(f"page_in{n}") for n in range(4)]
        page_turned, page_ev, pe_in_land = sem("page_turned"), sem("page_ev"), sem("pe_in_land")
        pe_clear, phi_clear, pe_turned, pe_ev, bias_ev = sem("pe_clear"), sem("phi_clear"), sem("pe_turned"), sem("pe_ev"), sem("bias_ev")
        cmp_done, cmp_ev, vct_turned = sem("cmp_done"), sem("cmp_ev"), sem("vct_turned")
        e_in = sem("e_in")
        gate_turned, gate_ready, gates_s, gates_sev = sem("gate_turned"), sem("gate_ready"), sem("gates_s"), sem("gates_sev")
        ln_var, ln_root, svn_ready = sem("ln_var"), sem("ln_root"), sem("svn_ready")
        swapped, roped = sem("swapped"), sem("roped")
        k_turned, k_ready, in_done, in_ready, qd_ready = sem("k_turned"), sem("k_ready"), sem("in_done"), sem("in_ready"), sem("qd_ready")
        o_done, o_ev, st_done, st_ready = sem("o_done"), sem("o_ev"), sem("st_done"), sem("st_ready")
        s0_in = [sem("s0_in0"), sem("s0_in1")]
        ks_ready, ins_done, ins_ready, qds_ready = sem("ks_ready"), sem("ins_done"), sem("ins_ready"), sem("qds_ready")
        kns_turned, so_done, so_ev = sem("kns_turned"), sem("so_done"), sem("so_ev")
        s0_out, vb_ready, s0_done, s0_ready = sem("s0_out"), sem("vb_ready"), sem("s0_done"), sem("s0_ready")
        e_out = sem("e_out")
        hsq, hsum, hroot, hrec, hspread = sem("hsq"), sem("hsum"), sem("hroot"), sem("hrec"), sem("hspread")
        ret_ready, mixed, mix_ready = sem("ret_ready"), sem("mixed"), sem("mix_ready")
        rows_land, rows_turned, rows_ev = sem("rows_land"), sem("rows_turned"), sem("rows_ev")
        prev_set, tap0, conv_done, gelu_done = sem("prev_set"), sem("tap0"), sem("conv_done"), sem("gelu_done")
        gated_ready, act_hi, act_ready = sem("gated_ready"), sem("act_hi"), sem("act_ready")
        tail_set, tail_turned, tail_ev, rows_stored = sem("tail_set"), sem("tail_turned"), sem("tail_ev"), sem("rows_stored")
        o_in, o_ropes = sem("o_in"), sem("o_ropes")
        cp_turned, cp_ev, cp_done, cp_set, vp_turned = (sem("cp_turned"), sem("cp_ev"), sem("cp_done"), sem("cp_set"),
                                                               sem("vp_turned"))
        qs_turned, g_turned, g_ready = sem("qs_turned"), sem("g_turned"), sem("g_ready")
        qk_turned, qk_ev = sem("qk_turned"), sem("qk_ev")
        s_done, masked, exped, scaled, p_turned = sem("s_done"), sem("masked"), sem("exped"), sem("scaled"), sem("p_turned")
        p_ev, v_done = [sem("p_ev0"), sem("p_ev1")], sem("v_done")
        c_scored, c_sub, c_exped, c_ready, c_turned, c_ev = (sem("c_scored"), sem("c_sub"), sem("c_exped"), sem("c_ready"),
                                                             sem("c_turned"), sem("c_ev"))
        o_hi, o_lo = sem("o_hi"), sem("o_lo")
        rows_out_done, gates_out, gs_in, b_in = sem("rows_out_done"), sem("gates_out"), sem("gs_in"), sem("b_in")
        row_in = [sem(f"row_in{n}") for n in range(4)]
        z_scored, z_sub, z_exped, z_ready, z_turned, z_ev = (sem("z_scored"), sem("z_sub"), sem("z_exped"), sem("z_ready"),
                                                             sem("z_turned"), sem("z_ev"))
        ks_turned, ks_ev, ss_done, s_masked, s_exped, s_scaled = (sem("ks_turned"), sem("ks_ev"), sem("ss_done"), sem("s_masked"),
                                                                  sem("s_exped"), sem("s_scaled"))
        ps_turned, ps_ev, os_done, m_set, kn_turned, kn_ev = (sem("ps_turned"), sem("ps_ev"), sem("os_done"), sem("m_set"),
                                                              sem("kn_turned"), sem("kn_ev"))
        out_turned, out_ev, out_stored = sem("out_turned"), sem("out_ev"), sem("out_stored")

        RS = misc[:, 1:3, 0:TH]
        N_BAR = 4
        MIX_FIRST = (4, 5, 6, 7, 0, 1, 2, 3)
        block = ctx.enter_context(nc.Block())

        def meet(eng, order, n):
            order(eng.drain(), phase)
            if eng is nc.gpsimd:
                eng.wait_ge(phase, N_BAR * (n + 1))

        FILL_AFTER = [0, E_OUT, F0, O_IN, F1]
        NORM_GAIN = [0, 2, 4, 6, 1, 3, 5, 7]

        def heads_of(t, g):
            return qN[:, t, (g // 2) * 512:(g // 2) * 512 + 512].rearrange("p (r g d) -> p r g d", r=R, g=2)[:, :, g % 2, :]

        def sample_heads(z):
            j, g2, r2 = z // 4, (z // 2) % 2, z % 2
            c0 = 2 * (2 * j + g2)
            src = gemm[1][64 * g2:64 * g2 + 64, :, :].rearrange("p a (b j g r n) -> p (a b) j g r n", b=4, j=2, g=2, n=DS)

            def dst(h):
                return h[64 * r2:64 * r2 + 64, c0:c0 + 2, 0:NS].rearrange("p c (b n) -> p c b n", b=DB)
            return dst, src[:, :, j, g2, r2:r2 + 3:2, :].rearrange("p b c n -> p c b n")

        def attention_unit(n):
            grp, w = n // 8, n % 8
            return grp // 8, (grp % 8) // 2, grp % 2, w // 2, w % 2

        def on_vector(n):
            return n % 2 == 1 and attention_unit(n)[1] < 2

        FIRST_TURNS = [(0, z) for z in range(R + 2)] + [(1, R), (1, R + 1)]

        def unit_source(u):
            kind, layer, n, _ = UNITS[u]
            s = u % 2
            if kind in ("even_in", "even_out", "odd_out"):
                w = {"even_in": a["e_w_in"], "even_out": a["e_w_out"], "odd_out": a["o_w_out"]}[kind][0]
                yield raw[:, s, :].rearrange("p (k n) -> p k n", k=DC), w[:, 256 * n:256 * n + 256].rearrange("(k p) n -> p k n", p=P)
            elif kind == "odd_in":
                width = 48 if n == 10 else 256
                yield (raw[:, s, :].rearrange("p (k n) -> p k n", k=DC)[:, :, 0:width],
                       a["o_w_in"][0][:, 256 * n:256 * n + width].rearrange("(k p) n -> p k n", p=P))

        def unit_view(t, u):
            kind, _, n, _ = UNITS[u]
            if kind == "ffn_out":
                return t[:, u % 2, 0:FH * P]
            if kind == "odd_in" and n == 10:
                return t[:, u % 2, :].rearrange("p (k n) -> p k n", k=DC)[:, :, 0:48]
            return t[:, u % 2, :]

        landed, total = [], [0, 0]
        for u in range(len(UNITS)):
            total[u % 2] += 16 * (2 if UNITS[u][0] == "ffn_in" else 1)
            landed.append(total[u % 2])

        @block.sync
        def _(sp):
            sp.dma_start(ident[:, :], a["ident"]).then_inc(x_in, 16)
            sp.dma_start(xin[0:NS, 0, :], a["x_sample"].rearrange("b s d -> (b s) d")).then_inc(x_in, 16)
            for n in range(2):
                sp.dma_start(xin[:, 1 + 2 * n:3 + 2 * n, :], a["x_prompt"][0][256 * n:256 * n + 256, :].rearrange("(t p) d -> p t d", p=P)).then_inc(x_in, 16)
            def load_unit(u):
                if u >= 2:
                    sp.wait_ge(lo_ready, u - 1)
                for dst, src in unit_source(u):
                    sp.dma_start(dst, src).then_inc(raw_ready[u % 2], 16)

            def load_ffn(layer):
                for half in range(2):
                    u0 = (F0 if layer == 0 else F1) + half * (FH + DC)
                    w_in = a["f_w_in"][layer].rearrange("(k p) (c n) -> p k c n", p=P, n=P)
                    w_out = a["f_w_out"][layer][half * FH * P:(half + 1) * FH * P, :].rearrange("(k p) (m n) -> p k m n", p=P, n=P)

                    def load_in(slot, i):
                        for ab in range(2):
                            sp.dma_start(raw[:, slot, :].rearrange("p (k n) -> p k n", k=DC)[:, :, P * ab:P * ab + P],
                                         w_in[:, :, i + (ab * 2 * FH + half * FH), :]).then_inc(raw_ready[slot], 16)

                    with sp.Fori(0, FH // 2) as t:
                        for z in range(2):
                            sp.wait_ge(lo_ready, t * 2 + (u0 + z - 1))
                            load_in((u0 + z) % 2, t * 2 + z)
                    u1 = u0 + FH
                    sp.wait_ge(lo_ready, u1 - 2)
                    load_in((u1 - 1) % 2, FH - 1)
                    with sp.Fori(0, DC // 2) as t:
                        for z in range(2):
                            slot = (u1 + z) % 2
                            sp.wait_ge(lo_ready, t * 2 + (u1 + z - 1))
                            sp.dma_start(raw[:, slot, 0:FH * P].rearrange("p (k n) -> p k n", k=FH),
                                         w_out[:, :, t * 2 + z, :]).then_inc(raw_ready[slot], 16)

            for u in range(F0):
                if u == E_OUT + 3:
                    sp.wait_ge(phi_clear, 2)
                    for z, phi in enumerate((phiK, phiV)):
                        name = ("o_phi_k", "o_phi_v")[z]
                        for g in range(2):
                            sp.dma_start(phi[64 * g:64 * g + 64, :, 64 * g:64 * g + 64], a[name][0].rearrange("l d e -> d l e")).then_inc(phi_in, 16)
                load_unit(u)
            load_ffn(0)
            for u in range(O_IN, F1):
                load_unit(u)
            load_ffn(1)

        @block.tensor
        def _(pe):
            order = Order(pe, pe_c)

            def turn(out, in_, sem_=None, k=P, base=0):
                ins = pe.transpose(out, in_, ident[base:base + k, base:base + k])
                if sem_ is not None:
                    order(ins, sem_)
                return ins

            def take_slot(c):
                if c >= 2:
                    pe.wait_ge(evacuated[c % 2], c // 2)

            def feature_chunk(u, j, nk, xh, xl, fill=None, ks=None, m=P, act_from=None, part_of=(0, None)):
                c = FIRST_CHUNK[u] + j
                width = P if nk == FH else 256
                if part_of[0] == 0:
                    take_slot(c)
                for n_k, k in list(enumerate(ks or range(nk)))[part_of[0]:part_of[1]]:
                    if fill is not None:
                        pe.wait_ge(h_ready, DC * fill + n_k + 1)
                    if act_from is not None:
                        pe.wait_ge(act_ready, act_from + k + 1)
                    at = k * width + (j * P if width == 256 else 0)
                    wh, wl = wH[:, u % 2, at:at + m], wL[:, u % 2, at:at + m]
                    for part, (w, x) in enumerate(((wh, xh), (wh, xl), (wl, xh))):
                        for n in range(2):
                            ins = pe.matmul(gemm[c % 2][0:m, n, 0:TH], w, x[:, k, n * TH:(n + 1) * TH],
                                            start=(n_k == 0 and part == 0), stop=(n_k == nk - 1 and part == 2))
                if part_of[1] is None:
                    order(ins, gemm_done)

            def token_chunk(u, t, width=256, fill=None):
                c = FIRST_CHUNK[u] + t
                take_slot(c)
                ts = tile_start(t)
                for k in range(DC):
                    if fill is not None:
                        pe.wait_ge(h_ready, DC * fill + k + 1)
                    wh, wl = wH[:, u % 2, k * 256:k * 256 + width], wL[:, u % 2, k * 256:k * 256 + width]
                    xh, xl = hH[:, k, ts:ts + P], hL[:, k, ts:ts + P]
                    for part, (x, w) in enumerate(((xh, wh), (xh, wl), (xl, wh))):
                        ins = pe.matmul(gemm[c % 2][:, 0, 0:width], x, w,
                                        start=(k == 0 and part == 0), stop=(k == DC - 1 and part == 2))
                order(ins, gemm_done)

            def unit(u):
                pe.wait_ge(lo_ready, u + 1)

            def square_sum(n, m, sq):
                pe.wait_ge(sq_ready, DC * n + m + 1)
                if m == 0 and n:
                    pe.wait_ge(root_ready, n)
                for q in range(4):
                    ins = pe.matmul(b4[32 * q:32 * q + 32, 0:TQ], mean_d[:, :], sq[m % 2][:, q * TQ:(q + 1) * TQ],
                                    start=(m == 0), stop=(m == DC - 1))
                order(ins, sq_used)

            def spread_rstd(n):
                pe.wait_ge(rec_ready, n + 1)
                for q in range(4):
                    ins = pe.matmul(misc[:, 1 + q // 2, (q % 2) * TQ:(q % 2 + 1) * TQ], spread[:, q, :], rr[:, :],
                                    start=True, stop=True)
                order(ins, rstd_ready)

            pe.wait_ge(x_in, 64)
            pe.wait_ge(consts, 3)
            for dc in range(DC):
                turn(misc[:, 2, dc * NS:(dc + 1) * NS], xin[0:NS, 0, dc * P:(dc + 1) * P], xt_turned if dc == DC - 1 else None, k=NS)
            for dc in range(DC):
                if dc >= 2:
                    pe.wait_ge(xt_ready, dc - 1)
                for t in range(4):
                    turn(misc[:, 1 + 2 * (dc % 2), t * P:(t + 1) * P], xin[:, t + 1, dc * P:(dc + 1) * P], xt_turned if t == 3 else None)
                if dc:
                    square_sum(0, dc - 1, sqx)
            pe.wait_ge(loads, LOADS)
            for dc in range(DC):
                turn(gemm[1][:, 0, dc * 8:(dc + 1) * 8], gin[:, dc * P:(dc + 1) * P], xt_turned if dc == DC - 1 else None, k=8)
            square_sum(0, DC - 1, sqx)
            spread_rstd(0)
            meet(pe, order, 0)

            def chunk_cols(c):
                return (NS + P * c, NS + P * (c + 1))

            def retention_scores(c):
                lo, hi = chunk_cols(c)
                pe.wait_ge(roped, 8)
                if c:
                    pe.wait_ge(s0_ready, c)
                for h in range(RH):
                    turn(b4[:, h * P:(h + 1) * P], kT[:, h, lo:hi], k_turned if h == RH - 1 else None)
                for h in range(RH):
                    ins = pe.matmul(b5[:, h * P:(h + 1) * P], kT[:, h, lo:hi], qT[:, h, lo:hi], start=True, stop=True)
                order(ins, in_done)

            def retention_values(c):
                pe.wait_ge(in_ready, c + 1)
                pe.wait_ge(qd_ready, c + 1)
                pe.wait_ge(so_ev, c + 1)
                if c:
                    pe.wait_ge(st_ready, c)
                for h in range(RH):
                    ins = pe.matmul(b6[:, h * P:(h + 1) * P], vN[:, c + 1, h * P:(h + 1) * P], inner[:, h, :],
                                    start=True, stop=(c == 0))
                    if c:
                        ins = pe.matmul(b6[:, h * P:(h + 1) * P], st[:, h, :], qd[:, h, :], start=False, stop=True)
                order(ins, o_done)
                pe.wait_ge(k_ready, c + 1)
                for h in range(RH):
                    ins = pe.matmul(b7[:, h * P:(h + 1) * P], kN[:, h, :], vN[:, c + 1, h * P:(h + 1) * P], start=True, stop=True)
                order(ins, st_done)

            def sample_scores():
                pe.wait_ge(roped, 8)
                for h in range(RH):
                    turn(b6[0:NS, h * P:(h + 1) * P], kT[:, h, 0:NS], kns_turned if h == RH - 1 else None)
                for h in range(RH):
                    ins = pe.matmul(b7[0:NS, h * NS:(h + 1) * NS], kT[:, h, 0:NS], qT[:, h, 0:NS], start=True, stop=True)
                order(ins, ins_done)

            def sample_outputs(h):
                pe.wait_ge(ins_ready, 1)
                pe.wait_ge(qds_ready, 1)
                pe.wait_ge(ks_ready, 1)
                if h:
                    pe.wait_ge(o_ev, h)
                pe.wait_ge(s0_in[h % 2], 16 * (h // 2 + 1))
                ins = pe.matmul(b6[:, 0:NS], vN[0:NS, 0, h * P:(h + 1) * P], inner_s[:, h, :],
                                start=True, stop=True, skip_group_check=True)
                for b in range(DB):
                    ins = pe.matmul(b6[:, DS * b:DS * (b + 1)], s0[:, b, h % 2, :], qds[:, h, DS * b:DS * (b + 1)],
                                    start=False, stop=True, skip_group_check=True)
                order(ins, so_done)

            def sample_states(h):
                pe.wait_ge(vb_ready, h + 1)
                for bb, bank in enumerate((b4, b5)):
                    ins = pe.matmul(bank, kNs[:, h, :], vB[:, 4 * bb:4 * bb + 4, :], start=True, stop=True)
                order(ins, s0_done)

            def mix_tokens():
                pe.wait_ge(svn_ready, 1)
                pe.wait_ge(gates_sev, 1)
                for c in range(NT):
                    if c >= 2:
                        pe.wait_ge(mix_ready, c - 1)
                    for g in range(4):
                        if c == 0:
                            ins = pe.matmul(misc[:, 0, g * NS:(g + 1) * NS], svn[0:NS, 0, g * P:(g + 1) * P], wmS[:, g, :], start=True, stop=True)
                        else:
                            ins = pe.matmul(misc[:, c % 2, g * P:(g + 1) * P], svn[:, c, g * P:(g + 1) * P], wmT[:, g, :], start=True, stop=True)
                    order(ins, mixed)

            def gate_weights():
                pe.wait_ge(e_in, E_LOADS)
                for g in range(4):
                    turn(b7[:, g * P:(g + 1) * P], sgw[:, g, :], gate_turned if g == 3 else None)
                pe.wait_ge(gate_ready, 1)
                for g in range(4):
                    ins = pe.matmul(b5[0:NS, g * NS:(g + 1) * NS], row_of_s[:, :],
                                    wmT[0:4, g, 0:4].unsqueeze(1).to_broadcast([4, DB, 4]), start=True, stop=True)
                order(ins, gates_s)

            for n in range(12):
                u = E_IN + n
                unit(u)
                if UNITS[u][3] == 5:
                    for t in range(NT):
                        token_chunk(u, t, fill=0 if n == t == 0 else None)
                else:
                    for j in range(2):
                        feature_chunk(u, j, DC, hH, hL)
                        if n >= 8 and j == 0:
                            if n == 8:
                                pe.wait_ge(mix_ready, NT)
                                sample_scores()
                            retention_scores(n - 8)
                            sample_outputs(n - 8)
                        elif n >= 8:
                            retention_values(n - 8)
                            sample_states(n - 8)
                if n == 3:
                    gate_weights()
                elif n == 4:
                    mix_tokens()
            last = FIRST_CHUNK[E_OUT] - 1
            pe.wait_ge(evacuated[last % 2], last // 2 + 1)
            for h in range(RH):
                pe.wait_ge(hsq, h + 1)
                for n in range(2):
                    ins = pe.matmul(gemm[last % 2][32 * h:32 * h + 32, n, 0:TH], mean_k[:, :], hsqs[h % 2][:, n * TH:(n + 1) * TH],
                                    start=True, stop=True)
                order(ins, hsum)
            unit(E_OUT)
            feature_chunk(E_OUT, 0, DC, hH, hL, 1, MIX_FIRST, part_of=(0, 4))
            pe.wait_ge(o_ev, 4)
            pe.wait_ge(st_ready, 4)
            pe.wait_ge(s0_ready, RH)
            pe.wait_ge(hrec, 1)
            for h in range(RH):
                if h >= 2:
                    pe.wait_ge(ret_ready, h - 1)
                for n in range(2):
                    ins = pe.matmul(misc[:, 2 * (h % 2) + n, 0:TH], spread[:, h, :], kT[:, 1, n * TH:(n + 1) * TH], start=True, stop=True)
                order(ins, hspread)
            meet(pe, order, 1)

            def turn_pages(first):
                if first == DB * NPG - 2:
                    pe.wait_ge(pe_in_land, 64)
                    for z in range(2):
                        turn(b7[:, 32 * z:32 * z + CL], pe_in[:, z, :], pe_turned, k=CL)
                for n in (first, first + 1):
                    pe.wait_ge(page_in[n % 4], 16 * (n // 4 + 1))
                    if n >= 2:
                        pe.wait_ge(page_ev, n - 1)
                    for zj in range(4):
                        turn(misc[:, 1 + n % 2, zj * P:(zj + 1) * P], pages[:, n % 4, zj * P:(zj + 1) * P], page_turned if zj == 3 else None)

            def compress(z, l0, l1):
                if z == l0 == 0:
                    pe.wait_ge(page_ev, DB * NPG)
                    pe.wait_ge(pe_ev, 1)
                    pe.wait_ge(phi_in, PHI_LOADS)
                out = gemm[1][:, 0, 0:NBLK] if z else b7[:, 0:NBLK]
                for l in range(l0, l1):
                    ins = pe.matmul(out, (phiK, phiV)[z][:, l, :], cT[:, z, :, l:l + 16 * (NCS - 1) + 1:16],
                                    start=(l == 0), stop=(l == CL - 1))
                if l1 == CL:
                    order(ins, cmp_done)

            def project_out(first, fill, n):
                for i in range(4):
                    unit(first + i)
                    for j in range(2):
                        if fill and 2 * i + j:
                            turn_pages(4 * i + 2 * j - 2)
                        feature_chunk(first + i, j, DC, hH, hL, fill if i == j == 0 else None, MIX_FIRST,
                                      part_of=(4 if fill and i == j == 0 else 0, None))
                        if 2 * i + j:
                            square_sum(n, 2 * i + j - 1, sqm)
                if fill:
                    turn_pages(DB * NPG - 2)
                square_sum(n, DC - 1, sqm)
                if fill:
                    compress(0, 0, 4)
                spread_rstd(n)

            def rows_in_turned(layer):
                pe.wait_ge(rows_land, ROWS_LAND * (layer + 1))
                for i in range(FH):
                    turn(misc[:, 3 - i // 4, (i % 4) * P:(i % 4 + 1) * P], rows_in[:, i * P:(i + 1) * P],
                         rows_turned if i % 4 == 3 or i == FH - 1 else None)

            def tail_turn(e):
                pe.wait_ge(tail_set, e + 1)
                if e:
                    pe.wait_ge(tail_ev, e + 1)
                turn(b7[0:64, 0:P], tail[:, e % 2, :], tail_turned)

            def ffn_product(weight_slot, chunk, j, nk, xh, xl):
                width, (count, odd) = P if nk == FH else 256, chunk
                pe.wait_ge(evacuated[odd], count)
                for k in range(nk):
                    at = k * width + (j * P if width == 256 else 0)
                    wh, wl = wH[:, weight_slot, at:at + P], wL[:, weight_slot, at:at + P]
                    for part, (w, x) in enumerate(((wh, xh), (wh, xl), (wl, xh))):
                        for n in range(2):
                            ins = pe.matmul(gemm[odd][:, n, 0:TH], w, x[:, k, n * TH:(n + 1) * TH],
                                            start=(k == 0 and part == 0), stop=(k == nk - 1 and part == 2))
                ins.then_inc(gemm_done, 1)

            def ffn(layer, fill, n):
                if layer == 0:
                    last = FIRST_CHUNK[F0] - 1
                    pe.wait_ge(evacuated[1], last // 2 + 1)
                    compress(1, 0, CL)
                first = F0 if layer == 0 else F1
                for half in range(2):
                    u0, e0 = first + half * (FH + DC), (2 * layer + half) * FH
                    c0 = FIRST_CHUNK[u0]
                    unit(u0)
                    feature_chunk(u0, 0, DC, hH, hL, fill if half == 0 else None)
                    if half == 0:
                        if layer == 0:
                            pe.wait_ge(cmp_ev, 1)
                        rows_in_turned(layer)
                        pe.wait_ge(rows_ev, 3 * (layer + 1))
                        if layer == 0:
                            pe.wait_ge(cmp_ev, 2)
                            for b in range(DB):
                                turn(misc[0:2 * NCS, 1 + b // 4, (b % 4) * P:(b % 4 + 1) * P],
                                     vct[:, b, :, :].rearrange("p j m -> p (j m)"), vct_turned if b == DB - 1 else None)
                    feature_chunk(u0, 1, DC, hH, hL)
                    with pe.Fori(0, FH // 2) as t:
                        for z in range(2):
                            i = 1 + z
                            pe.wait_ge(lo_ready, t * 2 + (u0 + i + 1))
                            for j in range(2):
                                odd = (c0 + j) % 2
                                if j:
                                    pe.wait_ge(tail_set, t * 2 + (e0 + i))
                                    pe.wait_ge(tail_ev, t * 2 + (e0 + i))
                                ffn_product((u0 + i) % 2, (t * 2 + ((c0 + 2 * i + j) // 2), odd), j, DC, hH, hL)
                            turn(b7[0:64, 0:P], tail[:, (e0 + i - 1) % 2, :]).then_inc(tail_turned, 1)
                    e = e0 + FH - 1
                    u1, c1 = u0 + FH, c0 + 2 * FH
                    for m in range(2):
                        unit(u1 + m)
                        feature_chunk(u1 + m, 0, FH, aH, aL, act_from=None if m else e0)
                        if m == 0:
                            tail_turn(e)
                        elif half:
                            square_sum(n, 0, sqf)
                    with pe.Fori(0, DC // 2 - 1) as t:
                        for z in range(2):
                            m = 2 + z
                            pe.wait_ge(lo_ready, t * 2 + (u1 + m + 1))
                            ffn_product((u1 + m) % 2, (t + (c1 + m) // 2, (c1 + m) % 2), 0, FH, aH, aL)
                            if half:
                                pe.wait_ge(sq_ready, t * 2 + (DC * n + m))
                                for q in range(4):
                                    ins = pe.matmul(b4[32 * q:32 * q + 32, 0:TQ], mean_d[:, :],
                                                    sqf[(m - 1) % 2][:, q * TQ:(q + 1) * TQ], start=False, stop=False)
                                ins.then_inc(sq_used, 1)
                square_sum(n, DC - 1, sqf)
                spread_rstd(n)

            project_out(E_OUT, 1, 1)
            compress(0, 4, 8)
            for m in range(DC):
                square_sum(2, m, sqm)
                compress(0, 8 + 3 * m, 11 + 3 * m)
            spread_rstd(2)
            ffn(0, 2, 3)
            for m in range(DC):
                square_sum(4, m, sqf)
            spread_rstd(4)
            meet(pe, order, 2)
            def turn_rows():
                pe.wait_ge(o_ropes, 1)
                last = FIRST_CHUNK[O_IN + 2] - 1
                for c in (last - 1, last):
                    pe.wait_ge(evacuated[c % 2], c // 2 + 1)
                for z in range(4):
                    if z >= 2:
                        pe.wait_ge(cp_ev, z - 1)
                    for t in range(4):
                        turn(misc[:, z % 2, t * P:(t + 1) * P], kvN[:, t + 1, z * P:(z + 1) * P], cp_turned if t == 3 else None)

            def compress_prompt(z):
                pe.wait_ge(o_in, ODD_LOADS)
                pe.wait_ge(cp_ev, 4)
                for l in range(CL):
                    ins = pe.matmul(b7[:, z * 2 * NCP:(z + 1) * 2 * NCP], (phiK2, phiV2)[z][:, l, :],
                                    cPT[:, 2 * z:2 * z + 2, l:l + 16 * (NCP - 1) + 1:16], start=(l == 0), stop=(l == CL - 1))
                order(ins, cp_done)

            for n in range(11):
                u = O_IN + n
                unit(u)
                if n == 10:
                    feature_chunk(u, 0, DC, hH, hL, m=48)
                    c = FIRST_CHUNK[u]
                    pe.wait_ge(evacuated[c % 2], c // 2 + 1)
                    for t in range(NT):
                        turn(b5[:, 48 * t:48 * t + 48], gT[:, tile_start(t):tile_start(t) + P], g_turned if t == NT - 1 else None, k=48)
                else:
                    for t in range(NT):
                        token_chunk(u, t, fill=3 if n == t == 0 else None)
                if n == 3:
                    turn_rows()
                elif n in (5, 7):
                    compress_prompt((n - 5) // 2)
                elif n == 8:
                    pe.wait_ge(cp_set, 2)
                    for j in range(2):
                        turn(b4[0:NCP, j * P:(j + 1) * P], vcPt[:, j, :], vp_turned if j else None)
            pe.wait_ge(o_ropes, 7)
            for z in range(8):
                turn(b4[:, z * NS:(z + 1) * NS], qN[0:NS, 0, z * P:(z + 1) * P], qs_turned if z == 7 else None, k=NS)
            meet(pe, order, 3)

            def scores(n):
                j, qt, g2, r, br = attention_unit(n)
                half = slice(64 * g2, 64 * g2 + 64)
                keys = (qt + 1) * P
                if n >= 2:
                    pe.wait_ge(masked, n - 1)
                if n % 8 == 0:
                    if n:
                        pe.wait_ge(c_sub, n // 8)
                    for rr_ in range(R):
                        ins = pe.matmul(b6[:, rr_ * NCP:(rr_ + 1) * NCP], qTj[half, rr_, qt * P:(qt + 1) * P], kcP[half, j, :], start=True, stop=True)
                    order(ins, c_scored)
                order(pe.matmul(gemm[0][:, n % 2, 0:keys], qTj[half, r, qt * P:(qt + 1) * P], (ksT, kwT)[br][half, j, 0:keys],
                                start=True, stop=True), s_done)

            def turn_probs(n):
                _, qt, _, _, _ = attention_unit(n)
                pe.wait_ge(scaled, n + 1)
                if n >= 2:
                    pe.wait_ge(p_ev[n % 2], n // 2)
                for kt in range(qt + 1):
                    turn(gemm[1][:, n % 2, kt * P:(kt + 1) * P], pr[:, n % 2, kt * P:(kt + 1) * P], p_turned if kt == qt else None)
                if n % 8 == 0:
                    grp = n // 8
                    pe.wait_ge(c_ready, grp + 1)
                    if grp:
                        pe.wait_ge(c_ev, grp)
                    for r in range(R):
                        turn(b7[0:NCP, r * P:(r + 1) * P], cs[:, r, :], c_turned if r == R - 1 else None)

            def mix_values(n):
                j, qt, g2, r, br = attention_unit(n)
                g, grp = 2 * j + g2, n // 8
                pe.wait_ge(p_ev[n % 2], n // 2 + 1)
                if n % 8 == 0 and grp >= 2:
                    pe.wait_ge(o_lo, grp - 1)
                if n % 8 == 1:
                    pe.wait_ge(c_ev, grp + 1)
                out = misc[64 * (r % 2):64 * (r % 2) + 64, grp % 2, (r // 2) * P:(r // 2 + 1) * P]
                for kt in range(qt + 1):
                    ins = pe.matmul(out, kvN[:, 1 + kt, (2 * br + 3) * 256 + g * HD:(2 * br + 3) * 256 + (g + 1) * HD],
                                    pT[:, n % 2, kt * P:(kt + 1) * P], start=(br == 0 and kt == 0), stop=False)
                if br:
                    ins = pe.matmul(out, vcP[:, j, g2 * HD:(g2 + 1) * HD], cpT[:, r, :], start=False, stop=True)
                order(ins, v_done)

            def turn_in(n, j, z):
                if n >= 2:
                    pe.wait_ge(qk_ev, n - 1)
                for t in range(4):
                    if z < R:
                        src = qN[:, t + 1, (j * R + z) * P:(j * R + z + 1) * P]
                    else:
                        src = kvN[:, t + 1, (2 * (z - 3)) * 256 + j * P:(2 * (z - 3)) * 256 + (j + 1) * P]
                    turn(misc[:, 2 + n % 2, t * P:(t + 1) * P], src, qk_turned if t == 3 else None)

            for n, (j, z) in enumerate(FIRST_TURNS):
                turn_in(n, j, z)
            for n in range(128 + 3):
                if n == 64:
                    pe.wait_ge(c_sub, 8)
                    pe.wait_ge(c_ev, 8)
                    for z in range(R):
                        turn_in(8 + z, 1, z)
                if n < 128:
                    if n % 64 == 0:
                        pe.wait_ge(qk_ev, 8 + 4 * (n // 64))
                    scores(n)
                if 2 <= n < 130:
                    turn_probs(n - 2)
                if n >= 3:
                    mix_values(n - 3)
            meet(pe, order, 4)

            def rows_turn(b):
                pe.wait_ge(row_in[b % 4], 48 * (b // 4 + 1))
                for br in range(2):
                    n = 2 * b + br
                    if b:
                        pe.wait_ge(ks_ev, n - 1)
                    for j in range(2):
                        for pg in range(NPG):
                            ins = turn(misc[:, br, (2 * j + pg) * P:(2 * j + pg + 1) * P], row_slot[b % 4][:, br, pg, j * P:(j + 1) * P])
                    order(ins, ks_turned)

            def sample_scores(b):
                for br in range(2):
                    n = 2 * b + br
                    pe.wait_ge(ks_ev, n + 1)
                    if b:
                        pe.wait_ge(s_masked, n - 1)
                    for j in range(2):
                        ins = pe.matmul(gemm[0][64 * j:64 * j + 64, br, 0:KW], qS[:, b, j, :, :],
                                        kTs[:, b % 2, br, j, :], start=True, stop=True)
                    order(ins, ss_done)

            for z in range(4):
                turn(misc[:, 2, z * NS:(z + 1) * NS], kvN[0:NS, 0, (2 * (z // 2) + 2) * 256 + (z % 2) * P:(2 * (z // 2) + 2) * 256 + (z % 2 + 1) * P],
                     kn_turned if z == 3 else None, k=NS)
            for b in range(DB):
                for j in range(2):
                    ins = pe.matmul(gemm[0][64 * j:64 * j + 64, 0, b * NCS:(b + 1) * NCS], qS[:, b, j, :, :], kcs[:, b, j, :], start=True, stop=True)
            order(ins, z_scored)
            pe.wait_ge(o_lo, 16)
            rows_turn(0)
            pe.wait_ge(kn_ev, 2)
            pe.wait_ge(z_sub, 1)
            sample_scores(0)
            pe.wait_ge(z_ready, 1)
            for b in range(DB):
                turn(gemm[1][0:2 * NCS, b // 4, (b % 4) * P:(b % 4 + 1) * P], cpb[:, b, :, :].rearrange("p j m -> p (j m)"),
                     z_turned if b == DB - 1 else None)
            for b in range(DB):
                if b + 1 < DB:
                    rows_turn(b + 1)
                for br in range(2):
                    n = 2 * b + br
                    pe.wait_ge(s_scaled, n + 1)
                    if b:
                        pe.wait_ge(ps_ev, 2 * b)
                    for kt in range(3):
                        w = P if kt < 2 else NS
                        turn(misc[0:w, 2 + br, kt * P:(kt + 1) * P], prs[:, b % 2, br, kt * P:kt * P + w], ps_turned if kt == 2 else None)
                if b + 1 < DB:
                    sample_scores(b + 1)
                if b == 0:
                    pe.wait_ge(z_ev, 1)
                pe.wait_ge(ps_ev, 2 * (b + 1))
                for j in range(2):
                    at = (b % 4) * P + 64 * j
                    out = gemm[1][:, b // 4, at:at + 64]
                    for br in range(2):
                        for kt in range(3):
                            k = P if kt < 2 else NS
                            if kt < 2:
                                v = row_slot[b % 4][:, br, kt, 256 + j * P:256 + (j + 1) * P]
                            else:
                                v = kvN[0:NS, 0, (2 * br + 3) * 256 + j * P:(2 * br + 3) * 256 + (j + 1) * P]
                            pe.matmul(out, v, pTs[0:k, br, kt, 64 * j:64 * j + 64], start=(br == 0 and kt == 0), stop=False)
                    ins = pe.matmul(out, vcs[:, b, :], cpTs[:, b, 64 * j:64 * j + 64], start=False, stop=True)
                order(ins, os_done)
            meet(pe, order, 5)
            pe.wait_ge(o_lo, 16 + 8)
            project_out(O_OUT, None, 5)
            for m in range(DC):
                square_sum(6, m, sqm)
            spread_rstd(6)
            ffn(1, 4, 7)
            for m in range(DC):
                pe.wait_ge(x_ready, DC * FINAL_POST + m + 1)
                for half in range(2):
                    n = 2 * m + half
                    if n >= 2:
                        pe.wait_ge(out_ev, n - 1)
                    tiles = (0, 1) if half == 0 else (2, 3, 4)
                    for z, t in enumerate(tiles):
                        w = NS if t == 0 else P
                        turn(misc[0:w, 3 * (n % 2), z * P:(z + 1) * P],
                             xT[:, m, tile_start(t):tile_start(t) + w], out_turned if z == len(tiles) - 1 else None)

        @block.scalar
        def _(act):
            order = Order(act, act_c)

            def activate(out, in_, func, sem_=None, **kw):
                order(act.activation(out, in_, func, **kw), sem_)

            def split_hi(u):
                if u >= LAST_UNIT:
                    return
                act.wait_ge(raw_ready[u % 2], landed[u])
                if u >= 2:
                    act.wait_ge(gemm_done, FIRST_CHUNK[u - 1])
                activate(unit_view(wH, u), unit_view(raw, u), ACT.Copy, hi_ready)

            def square(n, m, src, sq):
                if DC * n + m >= 2:
                    act.wait_ge(sq_used, DC * n + m - 1)
                activate(sq[m % 2], src, ACT.Square, sq_ready)

            def root(n):
                act.wait_ge(sq_used, DC * (n + 1))
                if n:
                    act.wait_ge(rec_ready, n)
                activate(rq[:, :], b4[:, 0:TQ], ACT.Sqrt, root_ready, bias=eps[:, 0:1])

            def fill_hi(fill, k, src, first=0):
                if k == first and fill:
                    act.wait_ge(gemm_done, FIRST_CHUNK[FILL_AFTER[fill]])
                activate(hH[:, k, :], src, ACT.Copy, h_hi)

            def norm_fill(pf, fill):
                for k in range(DC):
                    act.wait_ge(ht_ready, DC * pf + k + 1)
                    fill_hi(fill, k, y[:, k, :])

            def chunk_ready(c):
                act.wait_ge(gemm_done, c + 1)
                return gemm[c % 2]

            for dc in range(DC):
                act.wait_ge(xt_turned, dc + 2)
                activate(xT[:, dc, NS:T], misc[:, 1 + 2 * (dc % 2), :], ACT.Copy, xt_ready)
                if dc == 0:
                    act.wait_ge(gain_ready, 1)
                act.wait_ge(xt_ready, dc + 1)
                square(0, dc, xT[:, dc, :], sqx)
            act.wait_ge(gain_ready, 2)
            root(0)

            split_hi(0)
            norm_fill(0, 0)
            meet(act, order, 0)

            for n in range(12):
                u = E_IN + n
                split_hi(u + 1)
                what = UNITS[u][2]
                for j in range(UNITS[u][3]):
                    c = FIRST_CHUNK[u] + j
                    if what < 4:
                        rc = 2 * what + j
                        ps = chunk_ready(c)
                        if rc:
                            act.wait_ge(roped, rc)
                        activate(halves(swp[0:64, :]), ps[64:128, :, 0:TH], ACT.Copy)
                        activate(halves(swp[64:128, :]), ps[0:64, :, 0:TH], ACT.Copy, swapped)
                    elif what < 6:
                        activate(vN[:, j, 256 * (what % 2):256 * (what % 2) + 256], chunk_ready(c)[:, 0, 0:256], ACT.Copy, evacuated[c % 2])
                    elif what in (6, 7):
                        activate(halves(silu_g[:, 2 * (what - 6) + j, :]), chunk_ready(c)[:, :, 0:TH], ACT.Silu, evacuated[c % 2])
                if n == 1:
                    act.wait_ge(ln_var, 1)
                    activate(lns[:, 2, :], lns[:, 1, :], ACT.Sqrt, ln_root, bias=eps[:, 0:1], scale=1.0 / P)
            act.wait_ge(o_ev, 4)
            act.wait_ge(so_ev, 4)
            for h in range(RH):
                if h >= 2:
                    act.wait_ge(hsum, h - 1)
                activate(hsqs[h % 2][:, :], qT[:, h, :], ACT.Square, hsq)
            for k in range(4, DC):
                fill_hi(1, k, uT[:, k - 4, :], 4)
            act.wait_ge(hsum, RH)
            activate(halves(kT[:, 0, :]), gemm[(FIRST_CHUNK[E_OUT] - 1) % 2][:, :, 0:TH], ACT.Sqrt, hroot, bias=eps[:, 0:1])
            for k in range(4):
                act.wait_ge(ret_ready, k + 1)
                fill_hi(1, k, qT[:, k, :], 4)
            meet(act, order, 1)

            def take_pages(first):
                if first == DB * NPG - 2:
                    act.wait_ge(pe_clear, 1)
                    act.wait_ge(pe_turned, 2)
                    activate(cT[:, :, 2 * DB, 0:CL], b7[:, 0:64].rearrange("p (z l) -> p z l", z=2), ACT.Copy, pe_ev)
                for n in (first, first + 1):
                    b, pg = n // NPG, n % NPG
                    act.wait_ge(page_turned, n + 1)
                    activate(cT[:, :, 0:2 * DB, :].rearrange("p z (j b) t -> p z j b t", j=2)[:, :, :, b, pg * PAGE:(pg + 1) * PAGE],
                             misc[:, 1 + n % 2, :].rearrange("p (z j t) -> p z j t", z=2, j=2), ACT.Copy, page_ev)

            def take_blocks(z):
                ps = gemm[1][:, 0, :] if z else b7
                act.wait_ge(cmp_done, z + 1)
                activate(pe_bias[:, z:z + 1], ps[:, 2 * DB * NCS:2 * DB * NCS + 1], ACT.Copy, bias_ev)
                act.wait_ge(bias_ev, z + 1)
                activate((kcs, vct)[z][:, :, :, :].rearrange("p b j m -> p j b m"),
                         ps[:, 0:2 * DB * NCS].rearrange("p (j b m) -> p j b m", j=2, b=DB), ACT.Identity, cmp_ev,
                         bias=pe_bias[:, z:z + 1])

            def project_out(first, n):
                for i in range(4):
                    split_hi(first + i + 1)
                    for j in range(2):
                        if first == E_OUT and 2 * i + j:
                            take_pages(4 * i + 2 * j - 2)
                        c, m = FIRST_CHUNK[first + i] + j, 2 * i + j
                        activate(halves(y[:, m, :]), chunk_ready(c)[:, :, 0:TH], ACT.Copy, evacuated[c % 2])
                        act.wait_ge(evacuated[c % 2], c // 2 + 1)
                        square(n, m, y[:, m, :], sqm)
                if first == E_OUT:
                    take_pages(DB * NPG - 2)
                root(n)

            def next_squares(n, post, sq):
                for m in range(DC):
                    act.wait_ge(x_ready, DC * post + m + 1)
                    square(n, m, xT[:, m, :], sq)
                root(n)

            def ffn(layer, n):
                first = F0 if layer == 0 else F1
                if layer == 0:
                    take_blocks(1)
                for b in range(3):
                    act.wait_ge(rows_turned, 3 * layer + b + 1)
                    w = min(4, FH - 4 * b)
                    activate(rows_t[:, 4 * b:4 * b + w, :], misc[:, 3 - b, 0:w * P].rearrange("p (i r) -> p i r", i=w), ACT.Copy, rows_ev)
                for half in range(2):
                    for i in range(FH):
                        u, e = first + half * (FH + DC) + i, (2 * layer + half) * FH + i
                        U = up[e % 2]
                        for j in range(2):
                            c = FIRST_CHUNK[u] + j
                            ps = chunk_ready(c)
                            if j == 0 and e >= 2:
                                act.wait_ge(conv_done, 2 * e - 2)
                                act.wait_ge(tail_set, e - 1)
                            activate(U[:, j, 0:6 * DB].rearrange("p (b r) -> p b r", b=DB)[:, :, 2:6],
                                     ps[:, 0, 0:NS].rearrange("p (b r) -> p b r", b=DB), ACT.Copy)
                            activate(U[:, j, 50:50 + TH - NS], ps[:, 0, NS:TH], ACT.Copy)
                            activate(U[:, j, 50 + TH - NS:UW], ps[:, 1, 0:TH], ACT.Copy, evacuated[c % 2])
                            act.wait_ge(prev_set, e + 1)
                            if e:
                                act.wait_ge(gated_ready, e)
                            w = rows_t[:, i, 32 * (2 * j + half):32 * (2 * j + half) + 32]
                            act.wait_ge(evacuated[c % 2], c // 2 + 1)
                            activate(conv[:, j, :], U[:, j, 0:CW], ACT.Identity, tap0, bias=w[:, 19:20], scale=w[:, 16:17])
                            if j == 0:
                                split_hi(u + 1)
                                if e == 0:
                                    act.wait_ge(vct_turned, 1)
                                    activate(vcs[:, :, :], misc[0:2 * NCS, 1:3, :].rearrange("p a (b e) -> p (a b) e", b=4), ACT.Copy, tail_ev)
                            elif i:
                                tail_out(e - 1, i - 1, half, layer)
                        act.wait_ge(conv_done, 2 * e + 1)
                        activate(conv[:, 0, :], conv[:, 0, :], ACT.Gelu_apprx_tanh, gelu_done)
                        act.wait_ge(gated_ready, e + 1)
                        if i == 0:
                            act.wait_ge(gemm_done, FIRST_CHUNK[first + half * (FH + DC)])
                        activate(aH[:, i, :], gated[:, :], ACT.Copy, act_hi)
                    for m in range(DC):
                        u = first + half * (FH + DC) + FH + m
                        split_hi(u + 1)
                        c = FIRST_CHUNK[u]
                        if half == 0:
                            activate(halves(y[:, m, :]), chunk_ready(c)[:, :, 0:TH], ACT.Copy, evacuated[c % 2])
                        else:
                            act.wait_ge(evacuated[c % 2], c // 2 + 1)
                            square(n, m, y[:, m, :], sqf)
                        if m == 0:
                            tail_out(e, FH - 1, half, layer)
                root(n)

            def tail_out(e, i, half, layer):
                act.wait_ge(tail_turned, e + 1)
                if i == 0 and (half or layer):
                    act.wait_ge(rows_stored, 64 * (2 * layer + half))
                activate(rows_out[:, i * P:(i + 1) * P], b7[0:64, 0:P], ACT.Copy, tail_ev)

            project_out(E_OUT, 1)
            next_squares(2, 0, sqm)
            take_blocks(0)
            norm_fill(1, 2)
            ffn(0, 3)
            next_squares(4, 1, sqf)
            norm_fill(2, 3)
            meet(act, order, 2)
            for n in range(11):
                u = O_IN + n
                split_hi(u + 1)
                what = UNITS[u][2]
                if what == 10:
                    c = FIRST_CHUNK[u]
                    activate(halves(gT[:, :]), chunk_ready(c)[0:48, :, 0:TH], ACT.Sigmoid, evacuated[c % 2])
                    act.wait_ge(g_turned, 1)
                    activate(gN[:, :, :], b5[:, 0:48 * NT].rearrange("p (t e) -> p t e", t=NT), ACT.Copy, g_ready)
                    continue
                for t in range(NT):
                    c = FIRST_CHUNK[u] + t
                    ps = chunk_ready(c)[:, 0, :]
                    if what < 4:
                        activate(heads_of(t, what), ps[:, 0:256].rearrange("p (r d) -> p r d", r=R), ACT.Copy, evacuated[c % 2])
                    elif what < 10:
                        activate(kvN[:, t, (what - 4) * 256:(what - 3) * 256], ps[:, 0:256], ACT.Copy, evacuated[c % 2])
                if n == 3:
                    for z in range(4):
                        act.wait_ge(cp_turned, z + 1)
                        activate(cPT[:, z, :], misc[:, z % 2, :], ACT.Copy, cp_ev)
                elif n in (5, 7):
                    z = (n - 5) // 2
                    act.wait_ge(cp_done, z + 1)
                    activate((kcP, vcPt)[z][:, :, :], b7[:, z * 2 * NCP:(z + 1) * 2 * NCP].rearrange("p (j m) -> p j m", j=2),
                             ACT.Identity, cp_set, bias=pe_bias[:, z:z + 1])
                elif n == 8:
                    act.wait_ge(vp_turned, 1)
                    activate(vcP[:, :, :], b4[0:NCP, 0:2 * P].rearrange("p (j e) -> p j e", j=2), ACT.Copy)
            meet(act, order, 3)

            def exps(n):
                _, qt, _, _, _ = attention_unit(n)
                keys = (qt + 1) * P
                act.wait_ge(masked, n + 1)
                if n >= 2:
                    act.wait_ge(p_turned, n - 1)
                activate(pr[:, n % 2, 0:keys], sm[:, n % 2, 0:keys], ACT.Exp, exped, bias=negmax[:, n % 2:n % 2 + 1], scale=-1.0,
                         accum_out=rsum[:, n % 2:n % 2 + 1])
                if n % 8 == 0:
                    act.wait_ge(c_sub, n // 8 + 1)
                    activate(cs[:, :, :], cs[:, :, :], ACT.Exp, c_exped, scale=SCALE)

            def take_probs(n):
                _, qt, _, _, _ = attention_unit(n)
                keys = (qt + 1) * P
                if not on_vector(n):
                    act.wait_ge(p_turned, n + 1)
                    if n >= 2:
                        act.wait_ge(v_done, n - 1)
                    activate(pT[:, n % 2, 0:keys], gemm[1][:, n % 2, 0:keys], ACT.Copy, p_ev[n % 2])
                if n % 8 == 0:
                    grp = n // 8
                    act.wait_ge(c_turned, grp + 1)
                    if grp:
                        act.wait_ge(v_done, 8 * grp)
                    activate(cpT[:, :, :], b7[0:NCP, :].rearrange("p (r q) -> p r q", r=R), ACT.Copy, c_ev)

            def heads_hi(grp):
                j, qt, g2, _, _ = attention_unit(8 * grp)
                act.wait_ge(v_done, 8 * (grp + 1))
                c0 = 2 * (2 * j + g2)
                activate(hH[:, c0:c0 + 2, NS + qt * P:NS + (qt + 1) * P], misc[:, grp % 2, 0:2 * P].rearrange("p (c q) -> p c q", c=2), ACT.Copy, o_hi)

            def take_in(n, j, z):
                act.wait_ge(qk_turned, n + 1)
                activate(qTj[:, z, :] if z < R else (ksT, kwT)[z - R][:, j, :], misc[:, 2 + n % 2, :], ACT.Copy, qk_ev)

            for n, (j, z) in enumerate(FIRST_TURNS):
                take_in(n, j, z)
            for n in range(128 + 3):
                if n >= 3:
                    take_probs(n - 3)
                if n == 64:
                    act.wait_ge(s_done, 64)
                    for z in range(R):
                        take_in(8 + z, 1, z)
                if n < 128:
                    exps(n)
                if (n - 3) % 8 == 1 and n - 3 > 8:
                    heads_hi((n - 3) // 8 - 1)
            heads_hi(15)
            meet(act, order, 4)

            def take_keys(b):
                for br in range(2):
                    n = 2 * b + br
                    act.wait_ge(ks_turned, n + 1)
                    if b >= 2:
                        act.wait_ge(ss_done, n - 3)
                    activate(kTs[:, b % 2, br, :, 0:PAST], misc[:, br, :].rearrange("p (j t) -> p j t", j=2), ACT.Copy, ks_ev)

            def sample_exps(b):
                for br in range(2):
                    n = 2 * b + br
                    act.wait_ge(s_masked, n + 1)
                    if b >= 2:
                        act.wait_ge(ps_turned, n - 3)
                    activate(prs[:, b % 2, br, :], sms[:, b % 2, br, :], ACT.Exp, s_exped, bias=nms[:, b, br:br + 1], scale=-1.0, accum_out=rss[:, b, br:br + 1])

            act.wait_ge(kn_turned, 1)
            for slot in range(2):
                activate(kTs[:, slot, :, :, PAST:KW], misc[:, 2, 0:4 * NS].rearrange("p (e j t) -> p e j t", e=2, j=2), ACT.Copy, kn_ev)
            take_keys(0)
            act.wait_ge(z_sub, 1)
            activate(css[:, :, :], css[:, :, :], ACT.Exp, z_exped, scale=SCALE)
            sample_exps(0)
            act.wait_ge(z_turned, 1)
            activate(cpTs[:, :, :], gemm[1][0:2 * NCS, :, :].rearrange("p a (b e) -> p (a b) e", b=4), ACT.Copy, z_ev)
            for b in range(DB):
                if b + 1 < DB:
                    take_keys(b + 1)
                act.wait_ge(ps_turned, 2 * (b + 1))
                if b:
                    act.wait_ge(os_done, b)
                activate(pTs[:, :, 0:2, :], misc[:, 2:4, 0:2 * P].rearrange("p e (k q) -> p e k q", k=2), ACT.Copy, ps_ev)
                activate(pTs[0:NS, :, 2, :], misc[0:NS, 2:4, 2 * P:3 * P], ACT.Copy, ps_ev)
                if b + 1 < DB:
                    sample_exps(b + 1)
            act.wait_ge(os_done, DB)
            for z in range(8):
                dst, src = sample_heads(z)
                activate(dst(hH), src, ACT.Copy, o_hi)
            meet(act, order, 5)
            project_out(O_OUT, 5)
            next_squares(6, 2, sqm)
            norm_fill(3, 4)
            ffn(1, 7)
            for n in range(2 * DC):
                m, half = n // 2, n % 2
                act.wait_ge(out_turned, n + 1)
                if half == 0:
                    activate(yout[0:NS, 0, m * P:(m + 1) * P], misc[0:NS, 0, 0:P], ACT.Copy)
                    activate(yout[:, 1, m * P:(m + 1) * P], misc[:, 0, P:2 * P], ACT.Copy, out_ev)
                else:
                    activate(yout[:, 2:5, m * P:(m + 1) * P], misc[:, 3, 0:3 * P].rearrange("p (t f) -> p t f", t=3), ACT.Copy, out_ev)

        @block.vector
        def _(dve):
            order = Order(dve, dve_c)

            def split_lo(u):
                if u >= LAST_UNIT:
                    return
                dve.wait_ge(hi_ready, u + 1)
                order(dve.tensor_tensor(unit_view(wL, u), unit_view(raw, u), unit_view(wH, u).bitcast(F32), ALU.subtract), lo_ready)

            def rec(n):
                dve.wait_ge(root_ready, n + 1)
                if n:
                    dve.wait_ge(rstd_ready, n)
                order(dve.reciprocal(rr[:, :], rq[:, :]), rec_ready)
                dve.wait_ge(rstd_ready, n + 1)

            def fill_lo(fill, k, src, first=0):
                dve.wait_ge(h_hi, DC * fill + (k - first) % DC + 1)
                order(dve.tensor_tensor(hL[:, k, :], src, hH[:, k, :].bitcast(F32), ALU.subtract), h_ready)

            def norm_fill(n, fill):
                rec(n)
                for k in range(DC + 1):
                    if k < DC:
                        order(dve.scalar_tensor_tensor(halves(y[:, k, :]), halves(xT[:, k, :]), gains[:, k, NORM_GAIN[n]:NORM_GAIN[n] + 1],
                                                       RS, ALU.mult, ALU.mult), ht_ready)
                    if k:
                        fill_lo(fill, k - 1, y[:, k - 1, :])

            def residual(n):
                rec(n)
                for k in range(DC + 1):
                    if k < DC:
                        order(dve.scalar_tensor_tensor(halves(y[:, k, :]), halves(y[:, k, :]), gains[:, k, NORM_GAIN[n]:NORM_GAIN[n] + 1],
                                                       RS, ALU.mult, ALU.mult), y_scaled)
                    if k:
                        dve.wait_ge(y_scaled, DC * (n // 2) + k)
                        order(dve.tensor_tensor(xT[:, k - 1, :], xT[:, k - 1, :], y[:, k - 1, :], ALU.add), x_ready)
                order.wait()

            dve.wait_ge(xt_turned, 1)
            order(dve.tensor_copy(xT[:, :, 0:NS], misc[:, 2, 0:DC * NS].rearrange("p (c t) -> p c t", c=DC)), gain_ready)
            dve.wait_ge(xt_turned, DC + 2)
            order(dve.tensor_copy(gains[:, :, :], gemm[1][:, 0, 0:DC * 8].rearrange("p (c t) -> p c t", c=DC)), gain_ready)
            split_lo(0)
            norm_fill(0, 0)
            meet(dve, order, 0)

            def gate_weights():
                dve.wait_ge(gate_turned, 1)
                order(dve.tensor_tensor(wmT[:, :, :], by4(b7), tril[:, :].unsqueeze(1).to_broadcast([P, 4, P]), ALU.mult), gate_ready)
                dve.wait_ge(gates_s, 1)
                order(dve.tensor_tensor(wmS[:, :, :], b5[0:NS, 0:4 * NS].rearrange("p (g i) -> p g i", g=4),
                                        same_s[:, :].unsqueeze(1).to_broadcast([NS, 4, NS]), ALU.mult), gates_sev)

            def layer_norm():
                dve.wait_ge(e_in, E_LOADS)
                allx = svn[:, :, :].rearrange("p t (g c) -> p (t g) c", g=4)

                def per_group(row):
                    return lns[:, row, :].unsqueeze(2).to_broadcast([P, 4 * NT, P])

                order.wait()
                order(dve.tensor_reduce(lns[:, 3, :], allx, AX_X, ALU.add))
                order.wait()
                order(dve.tensor_scalar(lns[:, 0, :], lns[:, 3, :], -1.0 / P, None, ALU.mult))
                order.wait()
                order(dve.tensor_tensor(allx, allx, per_group(0), ALU.add))
                for t in range(NT):
                    order.wait()
                    order(dve.tensor_tensor(lnt[:, :], svn[:, t, :], svn[:, t, :], ALU.mult))
                    order.wait()
                    order(dve.tensor_reduce(lns[:, 1, 4 * t:4 * t + 4], by4(lnt[:, :]), AX_X, ALU.add),
                          ln_var if t == NT - 1 else None)

            def layer_norm_scaled():
                allx = svn[:, :, :].rearrange("p t (g c) -> p (t g) c", g=4)

                def per_group(row):
                    return lns[:, row, :].unsqueeze(2).to_broadcast([P, 4 * NT, P])

                dve.wait_ge(ln_root, 1)
                order(dve.reciprocal(lns[:, 3, :], lns[:, 2, :]))
                order.wait()
                order(dve.tensor_tensor(allx, allx, per_group(3), ALU.mult))
                for op, vec in ((ALU.mult, lng), (ALU.add, lnb)):
                    order.wait()
                    order(dve.tensor_tensor(svn[:, :, :], svn[:, :, :], vec[:, :].unsqueeze(1).to_broadcast([P, NT, 512]), op),
                          svn_ready if vec is lnb else None)

            def rope(c, what, j):
                rc = 2 * what + j
                dst, h = (qT, rc) if what < 2 else (kT, rc - 4)
                scale = 1.0 if what < 2 else DK ** -0.5
                dve.wait_ge(swapped, rc + 1)
                order(dve.scalar_tensor_tensor(halves(dst[:, h, :]), gemm[c % 2][:, :, 0:TH], scale, halves(cosE[:, :]),
                                               ALU.mult, ALU.mult), evacuated[c % 2])
                order(dve.scalar_tensor_tensor(swp[:, :], swp[:, :], scale, sinE[:, :], ALU.mult, ALU.mult))
                order.wait()
                order(dve.tensor_tensor(dst[:, h, :], dst[:, h, :], swp[:, :], ALU.add), roped)

            def retention_scores(c):
                lo, hi = NS + P * c, NS + P * (c + 1)
                dve.wait_ge(k_turned, c + 1)
                if c:
                    dve.wait_ge(st_done, c)
                order(dve.tensor_tensor(kN[:, :, :], by4(b4), kdec[:, 0:4].unsqueeze(2).to_broadcast([P, 4, P]), ALU.mult), k_ready)
                order(dve.tensor_tensor(qd[:, :, :], qT[:, :, lo:hi], qdec[:, :, :], ALU.mult), qd_ready)
                dve.wait_ge(in_done, c + 1)
                order(dve.tensor_tensor(inner[:, :, :], by4(b5), decay[:, :, :], ALU.mult), in_ready)

            def retention_values(c):
                lo, hi = NS + P * c, NS + P * (c + 1)
                dve.wait_ge(o_done, c + 1)
                order(dve.tensor_copy(qT[:, :, lo:hi], by4(b6)), o_ev)
                dve.wait_ge(st_done, c + 1)
                if c == 0:
                    order(dve.tensor_copy(st[:, :, :], by4(b7)), st_ready)
                else:
                    for h in range(RH):
                        order(dve.scalar_tensor_tensor(st[:, h, :], st[:, h, :], float(GAMMA[h] ** P), b7[:, h * P:(h + 1) * P],
                                                       ALU.mult, ALU.add), st_ready if h == RH - 1 else None)

            def sample_scores():
                dve.wait_ge(kns_turned, 1)
                order(dve.tensor_tensor(kNs[:, :, :], by4(b6[0:NS, :]), kdec[0:NS, 4:8].unsqueeze(2).to_broadcast([NS, 4, P]), ALU.mult), ks_ready)
                order(dve.tensor_tensor(qds[:, :, :], qT[:, :, 0:NS], qdecs[:, :, :], ALU.mult), qds_ready)
                dve.wait_ge(ins_done, 1)
                order(dve.tensor_tensor(inner_s[:, :, :], b7[0:NS, 0:4 * NS].rearrange("p (h i) -> p h i", h=4), decs[:, :, :], ALU.mult), ins_ready)

            def sample_outputs(h):
                dve.wait_ge(so_done, h + 1)
                order(dve.tensor_copy(qT[:, h, 0:NS], b6[:, 0:NS]), so_ev)
                if h:
                    dve.wait_ge(s0_done, h)
                order(dve.tensor_tensor(vB[:, :, :], vN[0:NS, 0, h * P:(h + 1) * P].unsqueeze(1).to_broadcast([NS, DB, P]),
                                        batch_of[:, :].unsqueeze(2).to_broadcast([NS, DB, P]), ALU.mult), vb_ready)

            def sample_states(h):
                dve.wait_ge(s0_done, h + 1)
                for bb, bank in enumerate((b4, b5)):
                    part = s0[:, 4 * bb:4 * bb + 4, h % 2, :]
                    order(dve.scalar_tensor_tensor(part, part, float(GAMMA[h] ** DS), by4(bank), ALU.mult, ALU.add),
                          s0_ready if bb else None)

            def mix_tokens():
                for c in range(NT):
                    dve.wait_ge(mixed, c + 1)
                    w = NS if c == 0 else P
                    ps = misc[:, c % 2, 0:4 * w].rearrange("p (g i) -> p g i", g=4)
                    if c:
                        order(dve.tensor_tensor(uT[:, :, tile_start(c):tile_start(c) + P], ps, sgb[:, :, :], ALU.add), mix_ready)
                    else:
                        for g in range(4):
                            order(dve.tensor_tensor(uT[:, g, 0:NS].rearrange("p (b i) -> p b i", b=DB), ps[:, g, :].rearrange("p (b i) -> p b i", b=DB),
                                                    sgb[:, g, 0:DS].unsqueeze(1).to_broadcast([P, DB, DS]), ALU.add), mix_ready if g == 3 else None)

            for n in range(12):
                u = E_IN + n
                split_lo(u + 1)
                what = UNITS[u][2]
                for j in range(UNITS[u][3]):
                    c = FIRST_CHUNK[u] + j
                    if what < 4:
                        rope(c, what, j)
                    elif what >= 10:
                        dve.wait_ge(gemm_done, c + 1)
                        order(dve.tensor_copy(svn[:, j, 256 * (what % 2):256 * (what % 2) + 256], gemm[c % 2][:, 0, 0:256]), evacuated[c % 2])
                    elif what in (8, 9):
                        m = 2 * (what - 8) + j
                        dve.wait_ge(gemm_done, c + 1)
                        order(dve.tensor_tensor(halves(uT[:, m, :]), halves(uT[:, m, :]), gemm[c % 2][:, :, 0:TH], ALU.mult), evacuated[c % 2])
                    if n >= 8 and j == 0:
                        if n == 8:
                            sample_scores()
                        retention_scores(n - 8)
                        sample_outputs(n - 8)
                    elif n >= 8:
                        retention_values(n - 8)
                        sample_states(n - 8)
                if n == 1:
                    layer_norm()
                elif n == 2:
                    layer_norm_scaled()
                elif n == 3:
                    gate_weights()
                elif n == 4:
                    mix_tokens()
            last = FIRST_CHUNK[E_OUT] - 1
            dve.wait_ge(evacuated[last % 2], last // 2 + 1)
            for h in range(RH):
                dve.wait_ge(hsq, h + 1)
                order(dve.tensor_tensor(qT[:, h, :], qT[:, h, :], silu_g[:, h, :], ALU.mult))
            for k in range(4, DC):
                fill_lo(1, k, uT[:, k - 4, :], 4)
            dve.wait_ge(hroot, 1)
            order(dve.reciprocal(kT[:, 1, :], kT[:, 0, :]), hrec)
            for h in range(RH + 1):
                if h < RH:
                    dve.wait_ge(hspread, h + 1)
                    order(dve.tensor_tensor(halves(qT[:, h, :]), halves(qT[:, h, :]), misc[:, 2 * (h % 2):2 * (h % 2) + 2, 0:TH], ALU.mult), ret_ready)
                if h:
                    fill_lo(1, h - 1, qT[:, h - 1, :], 4)
            meet(dve, order, 1)

            def project_out(first):
                for i in range(4):
                    split_lo(first + i + 1)
                    if first == E_OUT and i == 0:
                        dve.wait_ge(phase, 2 * N_BAR)
                        for phi in (phiK, phiV):
                            order(dve.memset(phi[:, :, :], 0.0), phi_clear)
                        order(dve.memset(cT[:, :, 2 * DB, :], 0.0), pe_clear)

            def ffn(layer):
                first = F0 if layer == 0 else F1
                for half in range(2):
                    for i in range(FH):
                        u, e = first + half * (FH + DC) + i, (2 * layer + half) * FH + i
                        U = up[e % 2]
                        for j in range(2):
                            w = rows_t[:, i, 32 * (2 * j + half):32 * (2 * j + half) + 32]
                            dve.wait_ge(tap0, 2 * e + j + 1)
                            order(dve.scalar_tensor_tensor(conv[:, j, :], U[:, j, 1:1 + CW], w[:, 17:18], conv[:, j, :], ALU.mult, ALU.add))
                            order.wait()
                            order(dve.scalar_tensor_tensor(conv[:, j, :], U[:, j, 2:2 + CW], w[:, 18:19], conv[:, j, :], ALU.mult, ALU.add), conv_done)
                            if j == 0:
                                split_lo(u + 1)
                        dve.wait_ge(conv_done, 2 * e + 2)
                        dve.wait_ge(gelu_done, e + 1)
                        if e:
                            dve.wait_ge(act_ready, e)
                        order(dve.tensor_tensor(gated[:, 0:NS].rearrange("p (b r) -> p b r", b=DB),
                                                conv[:, 0, 0:6 * DB].rearrange("p (b r) -> p b r", b=DB)[:, :, 0:4],
                                                conv[:, 1, 0:6 * DB].rearrange("p (b r) -> p b r", b=DB)[:, :, 0:4], ALU.mult))
                        order(dve.tensor_tensor(gated[:, NS:T], conv[:, 0, 48:CW], conv[:, 1, 48:CW], ALU.mult), gated_ready)
                        dve.wait_ge(act_hi, e + 1)
                        order(dve.tensor_tensor(aL[:, i, :], gated[:, :], aH[:, i, :].bitcast(F32), ALU.subtract), act_ready)
                    for m in range(DC):
                        u = first + half * (FH + DC) + FH + m
                        split_lo(u + 1)
                        if half:
                            c = FIRST_CHUNK[u]
                            dve.wait_ge(gemm_done, c + 1)
                            order(dve.tensor_tensor(halves(y[:, m, :]), halves(y[:, m, :]), gemm[c % 2][:, :, 0:TH], ALU.add), evacuated[c % 2])

            project_out(E_OUT)
            residual(1)
            norm_fill(2, 2)
            ffn(0)
            residual(3)
            norm_fill(4, 3)
            order.wait()
            meet(dve, order, 2)
            for n in range(11):
                u = O_IN + n
                split_lo(u + 1)
                what = UNITS[u][2]
                if what in (4, 6, 8, 0, 1, 2, 3):
                    last = FIRST_CHUNK[u + 1] - 1
                    dve.wait_ge(evacuated[last % 2], last // 2 + 1)
                    dve.wait_ge(o_in, ODD_LOADS)
                    if what < 4:
                        x = qN[:, :, (what // 2) * 512:(what // 2) * 512 + 512].rearrange("p t (r g d) -> p t r g d", r=R, g=2)[:, :, :, what % 2, :]
                    else:
                        x = kvN[:, :, (what - 4) * 256:(what - 3) * 256].rearrange("p t (g d) -> p t g d", g=G)
                    x1, x2 = x[:, :, :, 0:8], x[:, :, :, 8:16]
                    ta, tb, tc, td = (rt[:, z, :].rearrange("p (t h d) -> p t h d", t=NT, h=4) for z in range(4))
                    cos = cosO[:, :, :].unsqueeze(2).to_broadcast([P, NT, 4, 8])
                    sin = sinO[:, :, :].unsqueeze(2).to_broadcast([P, NT, 4, 8])
                    for dst, p1, p2 in ((ta, x1, cos), (tb, x2, sin), (tc, x2, cos), (td, x1, sin)):
                        order(dve.tensor_tensor(dst, p1, p2, ALU.mult))
                    order.wait()
                    order(dve.tensor_tensor(x1, ta, tb, ALU.subtract))
                    order(dve.tensor_tensor(x2, tc, td, ALU.add), o_ropes)
                    order.wait()
            dve.wait_ge(cp_done, 2)
            order(dve.memset(qS[:, :, :, :, :], 0.0))
            dve.wait_ge(qs_turned, 1)
            order.wait()
            for j in range(2):
                for g2 in range(2):
                    half = slice(64 * g2, 64 * g2 + 64)
                    order(dve.tensor_copy(qS[half, :, j, g2, 0:16].rearrange("p b (r n) -> p r b n", r=R),
                                          b4[half, j * P:(j + 1) * P].rearrange("p (r b n) -> p r b n", r=R, b=DB)))
            meet(dve, order, 3)

            def mask(n):
                _, qt, _, _, _ = attention_unit(n)
                keys = (qt + 1) * P
                dve.wait_ge(s_done, n + 1)
                if n >= 2:
                    dve.wait_ge(exped, n - 1)
                order(dve.tensor_tensor_reduce(sm[:, n % 2, 0:keys], gemm[0][:, n % 2, 0:keys], causal[:, SEQ - keys:SEQ], -SCALE, BIG,
                                               ALU.add, ALU.min, negmax[:, n % 2:n % 2 + 1]), masked)
                if n % 8 == 0:
                    grp = n // 8
                    dve.wait_ge(c_scored, grp + 1)
                    if grp:
                        dve.wait_ge(c_turned, grp)
                    order(dve.tensor_tensor(cs[:, :, :], b6[:, 0:R * NCP].rearrange("p (r m) -> p r m", r=R),
                                            cmask[:, qt, :].unsqueeze(1).to_broadcast([P, R, NCP]), ALU.add))
                    order.wait()
                    order(dve.tensor_reduce(cmx[:, :], cs[:, :, :], AX_X, ALU.max))
                    order.wait()
                    order(dve.tensor_tensor(cs[:, :, :], cs[:, :, :], cmx[:, :].unsqueeze(2).to_broadcast([P, R, NCP]), ALU.subtract), c_sub)

            def scale(n):
                j, qt, g2, r, br = attention_unit(n)
                g = 2 * j + g2
                keys = (qt + 1) * P
                dve.wait_ge(exped, n + 1)
                order(dve.reciprocal(rscale[:, n % 2:n % 2 + 1], rsum[:, n % 2:n % 2 + 1]))
                order.wait()
                gate = gN[:, qt + 1, (br + 1) * 16 + g * R + r:(br + 1) * 16 + g * R + r + 1]
                order(dve.tensor_scalar(pr[:, n % 2, 0:keys], pr[:, n % 2, 0:keys], rscale[:, n % 2:n % 2 + 1], gate, ALU.mult, ALU.mult), scaled)
                if n % 8 == 0:
                    dve.wait_ge(c_exped, n // 8 + 1)
                    order(dve.tensor_reduce(crs[:, 0, :], cs[:, :, :], AX_X, ALU.add))
                    order.wait()
                    order(dve.tensor_tensor(cs[:, :, :], cs[:, :, :], cvalid[:, qt, :].unsqueeze(1).to_broadcast([P, R, NCP]), ALU.mult))
                    order(dve.reciprocal(crs[:, 1, :], crs[:, 0, :]))
                    order.wait()
                    order(dve.tensor_tensor(crs[:, 0, :], crs[:, 1, :], gN[:, qt + 1, g * R:(g + 1) * R], ALU.mult))
                    order.wait()
                    order(dve.tensor_tensor(cs[:, :, :], cs[:, :, :], crs[:, 0, :].unsqueeze(2).to_broadcast([P, R, NCP]), ALU.mult), c_ready)

            def heads_lo(grp):
                j, qt, g2, _, _ = attention_unit(8 * grp)
                dve.wait_ge(o_hi, grp + 1)
                c0 = 2 * (2 * j + g2)
                cols = slice(NS + qt * P, NS + (qt + 1) * P)
                order(dve.tensor_tensor(hL[:, c0:c0 + 2, cols], misc[:, grp % 2, 0:2 * P].rearrange("p (c q) -> p c q", c=2),
                                        hH[:, c0:c0 + 2, cols].bitcast(F32), ALU.subtract), o_lo)

            dve.wait_ge(b_in, BIN_LOADS)
            for n in range(128 + 3):
                if n >= 3 and on_vector(n - 3):
                    dve.wait_ge(p_turned, n - 2)
                    if n >= 5:
                        dve.wait_ge(v_done, n - 4)
                    keys = (attention_unit(n - 3)[1] + 1) * P
                    order(dve.tensor_copy(pT[:, (n - 3) % 2, 0:keys], gemm[1][:, (n - 3) % 2, 0:keys]), p_ev[(n - 3) % 2])
                if n < 128:
                    mask(n)
                if 1 <= n < 129:
                    scale(n - 1)
                if (n - 3) % 8 == 1 and n - 3 > 8:
                    heads_lo((n - 3) // 8 - 1)
            heads_lo(15)
            meet(dve, order, 4)

            dve.wait_ge(z_scored, 1)
            cpsum = gemm[0][:, 0, 0:DB * NCS].rearrange("p (b m) -> p b m", b=DB)
            order(dve.tensor_reduce(csm[:, :], cpsum, AX_X, ALU.max))
            order.wait()
            order(dve.tensor_tensor(css[:, :, :], cpsum, csm[:, :].unsqueeze(2).to_broadcast([P, DB, NCS]), ALU.subtract), z_sub)
            dve.wait_ge(z_exped, 1)
            order(dve.tensor_reduce(rss[:, :, 2], css[:, :, :], AX_X, ALU.add))
            order.wait()
            order(dve.reciprocal(rsc[:, :, 2], rss[:, :, 2]))
            order.wait()
            dve.wait_ge(gs_in, GS_LOADS)
            order(dve.tensor_tensor(rsc[:, :, 2], rsc[:, :, 2], gS[:, :, 0], ALU.mult))
            order.wait()
            order(dve.tensor_tensor(css[:, :, :], css[:, :, :], rsc[:, :, 2].unsqueeze(2).to_broadcast([P, DB, NCS]), ALU.mult))
            order.wait()
            for j in range(2):
                order(dve.tensor_tensor(cpb[:, :, j, :], css[:, :, :], pair_of[:, j, :].unsqueeze(1).to_broadcast([P, DB, NCS]), ALU.mult),
                      z_ready if j else None)
            for b in range(DB):
                for br in range(2):
                    n = 2 * b + br
                    dve.wait_ge(ss_done, n + 1)
                    dve.wait_ge(m_set, b + 1)
                    if b >= 2:
                        dve.wait_ge(s_exped, n - 3)
                    order(dve.tensor_tensor_reduce(sms[:, b % 2, br, :], gemm[0][:, br, 0:KW], mask_s[:, b % 2, :], -SCALE, BIG, ALU.add, ALU.min,
                                                   nms[:, b, br:br + 1]), s_masked)
                for br in range(2):
                    n = 2 * b + br
                    dve.wait_ge(s_exped, n + 1)
                    order(dve.reciprocal(rsc[:, b, br:br + 1], rss[:, b, br:br + 1]))
                    order.wait()
                    order(dve.tensor_scalar(prs[:, b % 2, br, :], prs[:, b % 2, br, :], rsc[:, b, br:br + 1], gS[:, b, br + 1:br + 2], ALU.mult, ALU.mult), s_scaled)
            for z in range(8):
                dve.wait_ge(o_hi, 16 + 8)
                dst, src = sample_heads(z)
                order(dve.tensor_tensor(dst(hL), src, dst(hH).bitcast(F32), ALU.subtract), o_lo)
            meet(dve, order, 5)
            project_out(O_OUT)
            residual(5)
            norm_fill(6, 4)
            ffn(1)
            residual(7)

        @block.gpsimd
        def _(pool):
            order = Order(pool, pool_c)
            order(pool.memset(mean_d[:, :], 1.0 / D), consts)
            order(pool.memset(mean_k[:, :], 1.0 / DK), consts)
            order(pool.memset(eps[:, :], EPS), consts)
            for dst, src in ((spread[:, :, :], a["spread"].rearrange("p (q m) -> p q m", q=4)),
                             (gin[0:2, :], a["norm_mix_pre"]), (gin[2:4, :], a["norm_mix_post"]),
                             (gin[4:6, :], a["norm_ffn_pre"]), (gin[6:8, :], a["norm_ffn_post"])):
                pool.dma_start(dst, src).then_inc(loads, 16)
            order(pool.memset(pool_mark[:, :], 0.0), phase)
            for dst, src in ((decay[:, :, :], by4(a["decay"])), (decs[:, :, :], by4(a["decay_s"])),
                             (qdec[:, :, :], by4(a["qdecay"].to_broadcast([P, 4 * P]))), (qdecs[:, :, :], by4(a["qdecay_s"].to_broadcast([P, 4 * NS]))),
                             (kdec[:, :], a["kdecay"]), (batch_of[:, :], a["batch_of"]), (same_s[:, :], a["same_s"]), (row_of_s[:, :], a["row_of_s"]),
                             (tril[:, :], a["tril_t"]), (cosE[:, :], a["cos_even"]), (sinE[:, :], a["sin_even"]),
                             (sgw[:, :, :], a["e_sg_w"][0].rearrange("g i j -> i g j")),
                             (sgb[:, :, :], by4(a["e_sg_b"].rearrange("n g i -> n (g i)").to_broadcast([P, 4 * P]))),
                             (lng[:, :], a["e_sg_ln_g"].to_broadcast([P, 512])), (lnb[:, :], a["e_sg_ln_b"].to_broadcast([P, 512]))):
                pool.dma_start(dst, src).then_inc(e_in, 16)

            def load_s0(h):
                pool.dma_start(s0[:, :, h % 2, :], a["state_ret"][0, :, h].rearrange("b d v -> d b v")).then_inc(s0_in[h % 2], 16)

            load_s0(0)
            load_s0(1)
            pool.wait_ge(svn_ready, 1)
            pool.dma_start(o["sg_v_sample"][0].rearrange("b s w -> (b s) w"), svn[0:NS, 0, :]).then_inc(e_out, 16)
            for h in range(RH):
                pool.wait_ge(s0_ready, h + 1)
                pool.dma_start(o["ret_state_sample"][0, :, h].rearrange("b d v -> d b v"), s0[:, :, h % 2, :]).then_inc(s0_out, 16)
                if h == RH - 1:
                    pool.wait_ge(st_ready, 4)
                    pool.dma_start(o["ret_state_prompt"][0, 0].rearrange("h d v -> d h v"), st[:, :, :]).then_inc(e_out, 16)
                pool.wait_ge(s0_out, 16 * (h + 1))
                if h + 2 < RH:
                    load_s0(h + 2)
            pool.wait_ge(e_out, 32)
            meet(pool, order, 1)

            def load_page(n):
                if n >= 4:
                    pool.wait_ge(page_turned, n - 3)
                page = pool.value_load(a["page_table"][n // NPG:n // NPG + 1, n % NPG:n % NPG + 1], min_val=0, max_val=N_POOL - 1)
                pool.dma_start(pages[:, n % 4, :], a["cache_cmp"][0, page].rearrange("t z g d -> t (z g d)")).then_inc(page_in[n % 4], 16)

            for n in range(6):
                load_page(n)
            for z in range(2):
                for g in range(2):
                    pool.dma_start(pe_in[:, z, 64 * g:64 * g + 64], a[("o_pe_k", "o_pe_v")[z]][0]).then_inc(pe_in_land, 16)
            for n in range(6, DB * NPG):
                load_page(n)
            pool.wait_ge(page_turned, DB * NPG)

            def load_ffn_rows(layer):
                for q in range(4):
                    cols = slice(q * FH * P, (q + 1) * FH * P)
                    pool.dma_start(rows_in[32 * q:32 * q + 16, :], a["state_ffn"][layer].rearrange("b r f -> (b r) f")[:, cols]).then_inc(rows_land, 16)
                    pool.dma_start(rows_in[32 * q + 16:32 * q + 19, :], a["f_conv_w"][layer][:, cols]).then_inc(rows_land, 16)
                    pool.dma_start(rows_in[32 * q + 19:32 * q + 20, :], a["f_conv_b"][layer:layer + 1, cols]).then_inc(rows_land, 16)

            def ffn(layer):
                order(pool.memset(rows_in[:, :], 0.0))
                if layer == 0:
                    order.wait()
                    load_ffn_rows(layer)
                    pool.wait_ge(cmp_ev, 2)
                for s in range(2):
                    order(pool.memset(up[s][:, :, 48:50], 0.0))
                order(pool.memset(tail[:, :, :], 0.0))
                order.wait()
                if layer:
                    load_ffn_rows(layer)
                pool.wait_ge(rows_ev, 3 * (layer + 1))
                first = F0 if layer == 0 else F1
                for half in range(2):
                    for i in range(FH):
                        e = (2 * layer + half) * FH + i
                        U = up[e % 2]
                        if e >= 2:
                            pool.wait_ge(conv_done, 2 * e - 2)
                        for j in range(2):
                            q = 2 * j + half
                            order(pool.tensor_copy(U[:, j, 0:6 * DB].rearrange("p (b r) -> p b r", b=DB)[:, :, 0:2],
                                                   rows_t[:, i, 32 * q:32 * q + 16].rearrange("p (b r) -> p b r", b=DB)), prev_set if j else None)
                        if e >= 2:
                            pool.wait_ge(tail_turned, e - 1)
                        for j in range(2):
                            c = FIRST_CHUNK[first + half * (FH + DC) + i] + j
                            pool.wait_ge(evacuated[c % 2], c // 2 + 1)
                            order(pool.tensor_copy(tail[:, e % 2, 32 * j:32 * j + 2], U[:, j, UW - 2:UW]))
                            order(pool.tensor_copy(tail[:, e % 2, 32 * j + 2:32 * j + 18].rearrange("p (b r) -> p b r", b=DB),
                                                   U[:, j, 0:6 * DB].rearrange("p (b r) -> p b r", b=DB)[:, :, 4:6]), tail_set if j else None)
                    pool.wait_ge(tail_ev, e + 2)
                    for j in range(2):
                        cols = slice(j * FF + half * FH * P, j * FF + (half + 1) * FH * P)
                        pool.dma_start(o["ffn_prompt"][layer, 0][:, cols], rows_out[32 * j:32 * j + 2, :]).then_inc(rows_stored, 16)
                        pool.dma_start(o["ffn_sample"][layer].rearrange("b r f -> (b r) f")[:, cols], rows_out[32 * j + 2:32 * j + 18, :]).then_inc(rows_stored, 16)

            ffn(0)
            pool.wait_ge(rows_stored, 128)
            meet(pool, order, 2)
            for dst, src in ((cosO[:, :, :], a["cos_odd"].rearrange("p (t d) -> p t d", t=NT)),
                             (sinO[:, :, :], a["sin_odd"].rearrange("p (t d) -> p t d", t=NT))):
                pool.dma_start(dst, src).then_inc(o_in, 16)
            for phi in (phiK2, phiV2):
                order(pool.memset(phi[:, :, :], 0.0))
            order.wait()
            for phi, name in ((phiK2, "o_phi_k"), (phiV2, "o_phi_v")):
                for g in range(2):
                    pool.dma_start(phi[64 * g:64 * g + 64, :, 64 * g:64 * g + 64], a[name][0].rearrange("l d e -> d l e")).then_inc(o_in, 16)
            win_out = o["win_sample"][0].rearrange("b s z g d -> b s (z g d)")
            pool.dma_start(win_out[:, 0:PAST, :], a["state_win"][0].rearrange("b s z g d -> b s (z g d)")).then_inc(rows_out_done, 16)
            pool.wait_ge(vp_turned, 1)
            for dst, src in ((causal[:, :], a["causal"]), (cmask[:, :, :], by4(a["cmp_mask"])), (cvalid[:, :, :], by4(a["cmp_valid"]))):
                pool.dma_start(dst, src).then_inc(b_in, 16)
            pool.wait_ge(o_ropes, 7)
            for br, name in enumerate(("cmp_rows", "sel_rows", "win")):
                dst = o[f"{name}_prompt"][0, 0].rearrange("(t p) z g d -> p t (z g d)", p=P)
                pool.dma_start(dst, kvN[:, 1:NT, 512 * br:512 * br + 512]).then_inc(rows_out_done, 16)
                if br < 2:
                    dst = o[f"{name}_sample"][0].rearrange("b s z g d -> (b s) (z g d)")
                    pool.dma_start(dst, kvN[0:NS, 0, 512 * br:512 * br + 512]).then_inc(rows_out_done, 16)
                else:
                    for b in range(DB):
                        pool.dma_start(win_out[b, PAST:KS, :], kvN[DS * b:DS * (b + 1), 0, 512 * br:512 * br + 512]).then_inc(rows_out_done, 16)
            meet(pool, order, 3)
            pool.wait_ge(g_ready, 1)
            for e in range(3):
                pool.dma_start(scratch[:, :, e], gN[0:NS, 0, 16 * e:16 * e + 16], allow_slow_non_contiguous=True).then_inc(gates_out, 16)
            pool.wait_ge(gates_out, 48)
            order(pool.memset(gS[:, :, :], 0.0))
            order(pool.memset(mask_s[:, :, :], 0.0))
            order.wait()
            for g in range(G):
                for r in range(R):
                    at = 32 * g + DS * r
                    pool.dma_start(gS[at:at + DS, :, :], scratch.rearrange("(b n) h e -> n h b e", b=DB)[:, g * R + r, :, :]).then_inc(gs_in, 16)
            for dst, src in ((mask_new[:, :, :], a["mask_new"].rearrange("p (b m) -> p b m", b=DB)),
                             (pair_of[:, :, :], a["pair_of"].rearrange("p (j m) -> p j m", j=2))):
                pool.dma_start(dst, src).then_inc(gs_in, 16)
            pool.wait_ge(gs_in, GS_LOADS)

            def load_rows(b):
                for pg in range(NPG):
                    page = pool.value_load(a["page_table"][b:b + 1, pg:pg + 1], min_val=0, max_val=N_POOL - 1)
                    pool.dma_start(row_slot[b % 4][:, 0, pg, :], a["cache_sel"][0, page].rearrange("t z g d -> t (z g d)")).then_inc(row_in[b % 4], 16)
                pool.dma_start(row_slot[b % 4][:, 1, :, :], a["state_win"][0, b].rearrange("(q t) z g d -> t q (z g d)", q=NPG)).then_inc(row_in[b % 4], 16)

            pool.wait_ge(qk_ev, 12)
            for b in range(2):
                load_rows(b)
            pool.wait_ge(rows_out_done, ROWS_OUT)
            pool.wait_ge(b_in, BIN_LOADS)
            meet(pool, order, 4)
            for b in range(DB):
                if b >= 2:
                    pool.wait_ge(s_masked, 2 * (b - 1))
                order(pool.tensor_copy(mask_s[:, b % 2, PAST:KW], mask_new[:, b, :]), m_set)
                if b + 2 < DB:
                    if b >= 2:
                        pool.wait_ge(os_done, b - 1)
                    load_rows(b + 2)
            meet(pool, order, 5)
            ffn(1)
            for m0, m1 in ((0, 4), (4, 7), (7, 8)):
                pool.wait_ge(out_ev, 2 * m1)
                cols = slice(m0 * P, m1 * P)
                pool.dma_start(o["y_prompt"][0].rearrange("(t p) d -> p t d", p=P)[:, :, cols], yout[:, 1:NT, cols]).then_inc(out_stored, 16)
                pool.dma_start(o["y_sample"].rearrange("b s d -> (b s) d")[:, cols], yout[0:NS, 0, cols]).then_inc(out_stored, 16)
            pool.wait_ge(out_stored, 96)
            pool.wait_ge(rows_stored, 64 * N_FFN_HALVES)


LOADS = 16 * 5
PHI_LOADS = 16 * 4
E_LOADS = 16 * 15
ROWS_LAND = 16 * 12
N_POOL = (DB * NPG * 5 + 3) // 4
ODD_LOADS = 16 * 6
BIN_LOADS = 16 * 3
ROWS_OUT = 16 * (1 + 3 + 2 + DB)
GS_LOADS = 16 * (G * R + 2)
LAST_UNIT = len(UNITS)
FINAL_POST = 3
N_FFN_HALVES = 4

OUTPUTS = (
    ("y_prompt", (1, SEQ, D)), ("y_sample", (DB, DS, D)),
    ("ret_state_prompt", (1, 1, RH, DK, DK)), ("ret_state_sample", (1, DB, RH, DK, DK)),
    ("sg_v_sample", (1, DB, DS, 512)),
    ("cmp_rows_prompt", (1, 1, SEQ, 2, G, HD)), ("cmp_rows_sample", (1, DB, DS, 2, G, HD)),
    ("sel_rows_prompt", (1, 1, SEQ, 2, G, HD)), ("sel_rows_sample", (1, DB, DS, 2, G, HD)),
    ("win_prompt", (1, 1, SEQ, 2, G, HD)), ("win_sample", (1, DB, KS, 2, G, HD)),
    ("ffn_prompt", (2, 1, 2, 2 * FF)), ("ffn_sample", (2, DB, 2, 2 * FF)),
)


def kernel(**inputs):
    import concourse.bacc as bacc
    from concourse.bass_utils import run_bass_kernel_spmd

    nc = bacc.Bacc("TRN2", target_bir_lowering=False, num_devices=1)
    arrays, a, o = {}, {}, {}
    for name, value in {**inputs, **CONSTANTS}.items():
        value = np.ascontiguousarray(value)
        arrays[f"in_{name}"] = value
        a[name] = nc.dram_tensor(f"in_{name}", value.shape, mybir.dt.from_np(value.dtype), kind="ExternalInput").ap()
    for name, shape in OUTPUTS:
        o[name] = nc.dram_tensor(f"out_{name}", shape, F32, kind="ExternalOutput").ap()
    build_program(nc, a, o)
    r = run_bass_kernel_spmd(nc, [arrays], core_ids=[0])
    return tuple(r.results[0][f"out_{name}"] for name, _ in OUTPUTS)
```
